# Optimizing a Trainium2 kernel written in Bass

```python
import math
import jax
import jax.numpy as jnp
from jax import lax
import numpy as np

D_MODEL = 1024
BATCH = 1
SEQ = 512
DEPTH = 2

N_A = DEPTH // 2
N_B = DEPTH - N_A
HA = 4
DK_A = D_MODEL // (2 * HA)
DV_A = D_MODEL // HA
CHUNK = 64
GATE_SOFTCAP = 15.0
A_PROJ = 2 * HA * DK_A + 2 * HA * DV_A + 2 * HA
HB = 8
HD_B = D_MODEL // (2 * HB)
QK_B = HB * 2 * HD_B
V_B = HB * 2 * HD_B
Q_BLOCK = 128
DFF = 256 * ((8 * D_MODEL // 3 + 255) // 256)
CONV_W = 3
RMS_EPS = 1e-6

kernel_name = 'yoco_mlstm_diffattn_convffn'

def rms_norm(x, g):
    xf = x.astype(jnp.float32)
    y = xf * lax.rsqrt(jnp.mean(xf * xf, axis=-1, keepdims=True) + RMS_EPS)
    return (y * g.astype(jnp.float32)).astype(x.dtype)

def mlstm_chunkwise(q, k, v, i_pre, logf):
    b_, h_, s_, dk = q.shape
    dv = v.shape[-1]
    nc = s_ // CHUNK

    def chunks(t):
        return jnp.moveaxis(t.reshape(b_, h_, nc, CHUNK, *t.shape[3:]), 2, 0)

    tri = jnp.tril(jnp.ones((CHUNK, CHUNK), dtype=bool))

    def step(carry, inp):
        c_st, n_st, m_st = carry
        qc, kc, vc, ic, fc = inp
        bcum = jnp.cumsum(fc, axis=-1)
        log_intra = jnp.where(tri, bcum[..., :, None] - bcum[..., None, :] + ic[..., None, :], -jnp.inf)
        log_inter = bcum + m_st[..., None]
        m_t = jnp.maximum(log_inter, jnp.max(log_intra, axis=-1))
        w_intra = jnp.exp(log_intra - m_t[..., None])
        w_inter = jnp.exp(log_inter - m_t)
        sc = jnp.einsum('bhtd,bhsd->bhts', qc, kc) * w_intra
        num = jnp.einsum('bhts,bhsv->bhtv', sc, vc) + w_inter[..., None] * jnp.einsum('bhvd,bhtd->bhtv', c_st, qc)
        den = jnp.sum(sc, axis=-1) + w_inter * jnp.einsum('bhd,bhtd->bht', n_st, qc)
        h_out = num / jnp.maximum(jnp.abs(den), jnp.exp(-m_t))[..., None]
        b_last = bcum[..., -1]
        log_src = b_last[..., None] - bcum + ic
        m_new = jnp.maximum(b_last + m_st, jnp.max(log_src, axis=-1))
        w_src = jnp.exp(log_src - m_new[..., None])
        decay = jnp.exp(b_last + m_st - m_new)
        c_new = decay[..., None, None] * c_st + jnp.einsum('bhs,bhsv,bhsd->bhvd', w_src, vc, kc)
        n_new = decay[..., None] * n_st + jnp.einsum('bhs,bhsd->bhd', w_src, kc)
        return (c_new, n_new, m_new), h_out

    init = (jnp.zeros((b_, h_, dv, dk), jnp.float32), jnp.zeros((b_, h_, dk), jnp.float32), jnp.zeros((b_, h_), jnp.float32))
    _, hs = lax.scan(step, init, (chunks(q), chunks(k), chunks(v), chunks(i_pre), chunks(logf)))
    return jnp.moveaxis(hs, 0, 2).reshape(b_, h_, s_, dv)

def mlstm_mixer(h, w_in, b_gate, head_g, w_out):
    b_, s_, _ = h.shape
    proj = h @ w_in
    cuts = [HA * DK_A, 2 * HA * DK_A, 2 * HA * DK_A + HA * DV_A, 2 * HA * DK_A + 2 * HA * DV_A]
    q, k, v, o, gates = jnp.split(proj, cuts, axis=-1)

    def heads(t, dh):
        return t.reshape(b_, s_, HA, dh).transpose(0, 2, 1, 3).astype(jnp.float32)

    q = heads(q, DK_A)
    k = heads(k, DK_A) * (DK_A ** -0.5)
    v = heads(v, DV_A)
    gates = gates.astype(jnp.float32) + b_gate.astype(jnp.float32)
    gates = GATE_SOFTCAP * jnp.tanh(gates / GATE_SOFTCAP)
    i_pre = gates[..., :HA].transpose(0, 2, 1)
    logf = jax.nn.log_sigmoid(gates[..., HA:]).transpose(0, 2, 1)
    hs = mlstm_chunkwise(q, k, v, i_pre, logf).transpose(0, 2, 1, 3)
    hs = rms_norm(hs, head_g)
    y = hs.reshape(b_, s_, HA * DV_A).astype(h.dtype) * jax.nn.sigmoid(o)
    return y @ w_out

def shared_kv(x, kv_norm_g, w_kv):
    b_, s_, _ = x.shape
    kv = rms_norm(x, kv_norm_g) @ w_kv
    k = kv[..., :QK_B].reshape(b_, s_, HB, 2, HD_B)
    v = kv[..., QK_B:].reshape(b_, s_, HB, 2 * HD_B)
    return k, v

def diff_attention(q, k, v, lam):
    b_, s_ = q.shape[:2]
    nq = s_ // Q_BLOCK
    qb = q.reshape(b_, nq, Q_BLOCK, HB, 2, HD_B).swapaxes(0, 1)
    starts = jnp.arange(nq) * Q_BLOCK
    kpos = jnp.arange(s_)
    vf = v.astype(jnp.float32)

    def one(args):
        qblk, st = args
        sc = jnp.einsum('bqhcd,bkhcd->bhcqk', qblk, k, preferred_element_type=jnp.float32)
        mask = (st + jnp.arange(Q_BLOCK))[:, None] >= kpos[None, :]
        p = jax.nn.softmax(jnp.where(mask, sc, -jnp.inf), axis=-1)
        a = p[:, :, 0] - lam * p[:, :, 1]
        return jnp.einsum('bhqk,bkhe->bqhe', a, vf)

    out = lax.map(one, (qb, starts))
    return out.swapaxes(0, 1).reshape(b_, s_, HB, 2 * HD_B)

def diff_mixer(h, k_sh, v_sh, w_q, lq1, lk1, lq2, lk2, subln_g, w_out, layer_idx):
    b_, s_, _ = h.shape
    lam_init = 0.8 - 0.6 * math.exp(-0.3 * layer_idx)
    lam = (jnp.exp(jnp.sum(lq1.astype(jnp.float32) * lk1.astype(jnp.float32)))
           - jnp.exp(jnp.sum(lq2.astype(jnp.float32) * lk2.astype(jnp.float32))) + lam_init)
    q = (h @ w_q).reshape(b_, s_, HB, 2, HD_B) * (HD_B ** -0.5)
    o = diff_attention(q, k_sh, v_sh, lam)
    o = rms_norm(o, subln_g) * (1.0 - lam_init)
    return o.reshape(b_, s_, V_B).astype(h.dtype) @ w_out

def conv_ffn(h, w_up, conv_w, conv_b, w_down):
    s_ = h.shape[1]
    up = h @ w_up
    g, u = up[..., :DFF], up[..., DFF:]
    gp = jnp.pad(g, ((0, 0), (CONV_W - 1, 0), (0, 0)))
    gc = conv_b + sum(conv_w[j] * gp[:, j:j + s_, :] for j in range(CONV_W))
    return (jax.nn.silu(gc) * u) @ w_down

def setup_inputs(seed: int = 0) -> dict:
    key = jax.random.key(seed)
    ks = jax.random.split(key, 24)

    def nrm(k, shape, scale):
        return jax.random.normal(k, shape, jnp.float32) * scale

    def gain(k, shape):
        return 1.0 + nrm(k, shape, 0.02)

    x = nrm(ks[0], (BATCH, SEQ, D_MODEL), 1.0)
    b_gate = jnp.concatenate([nrm(ks[5], (N_A, HA), 0.1), 3.0 + nrm(ks[6], (N_A, HA), 0.1)], axis=-1)
    return {
        'x': x,
        'attn_norm_g': gain(ks[1], (DEPTH, D_MODEL)),
        'ffn_norm_g': gain(ks[2], (DEPTH, D_MODEL)),
        'mlstm_w_in': nrm(ks[3], (N_A, D_MODEL, A_PROJ), D_MODEL ** -0.5),
        'mlstm_b_gate': b_gate,
        'mlstm_head_g': gain(ks[7], (N_A, HA, DV_A)),
        'mlstm_w_out': nrm(ks[8], (N_A, HA * DV_A, D_MODEL), (HA * DV_A) ** -0.5),
        'kv_norm_g': gain(ks[9], (D_MODEL,)),
        'w_kv': nrm(ks[10], (D_MODEL, QK_B + V_B), D_MODEL ** -0.5),
        'diff_w_q': nrm(ks[11], (N_B, D_MODEL, QK_B), D_MODEL ** -0.5),
        'diff_lambda_q1': nrm(ks[12], (N_B, HD_B), 0.1),
        'diff_lambda_k1': nrm(ks[13], (N_B, HD_B), 0.1),
        'diff_lambda_q2': nrm(ks[14], (N_B, HD_B), 0.1),
        'diff_lambda_k2': nrm(ks[15], (N_B, HD_B), 0.1),
        'diff_subln_g': gain(ks[16], (N_B, 2 * HD_B)),
        'diff_w_out': nrm(ks[17], (N_B, V_B, D_MODEL), V_B ** -0.5),
        'ffn_w_up': nrm(ks[18], (DEPTH, D_MODEL, 2 * DFF), D_MODEL ** -0.5),
        'ffn_conv_w': nrm(ks[19], (DEPTH, CONV_W, DFF), CONV_W ** -0.5),
        'ffn_conv_b': nrm(ks[20], (DEPTH, DFF), 0.02),
        'ffn_w_down': nrm(ks[21], (DEPTH, DFF, D_MODEL), DFF ** -0.5),
        'final_norm_g': gain(ks[22], (D_MODEL,)),
    }

def reference(x, attn_norm_g, ffn_norm_g, mlstm_w_in, mlstm_b_gate, mlstm_head_g, mlstm_w_out,
              kv_norm_g, w_kv, diff_w_q, diff_lambda_q1, diff_lambda_k1, diff_lambda_q2, diff_lambda_k2,
              diff_subln_g, diff_w_out, ffn_w_up, ffn_conv_w, ffn_conv_b, ffn_w_down, final_norm_g):
    k_sh, v_sh = None, None
    for l in range(DEPTH):
        if l == N_A:
            k_sh, v_sh = shared_kv(x, kv_norm_g, w_kv)
        h = rms_norm(x, attn_norm_g[l])
        if l < N_A:
            x = x + mlstm_mixer(h, mlstm_w_in[l], mlstm_b_gate[l], mlstm_head_g[l], mlstm_w_out[l])
        else:
            j = l - N_A
            x = x + diff_mixer(h, k_sh, v_sh, diff_w_q[j], diff_lambda_q1[j], diff_lambda_k1[j],
                               diff_lambda_q2[j], diff_lambda_k2[j], diff_subln_g[j], diff_w_out[j], l)
        x = x + conv_ffn(rms_norm(x, ffn_norm_g[l]), ffn_w_up[l], ffn_conv_w[l], ffn_conv_b[l], ffn_w_down[l])
    return rms_norm(x, final_norm_g)


_drawn_inputs = setup_inputs


def setup_inputs(seed=0):
    import zlib

    import numpy as np

    out = dict(_drawn_inputs(seed))
    spreads = {}
    factors = {'ffn_norm_g': 2.676,
     'mlstm_head_g': 4.215,
     'kv_norm_g': 3.848,
     'diff_lambda_q2': 200.0,
     'diff_subln_g': 66.612,
     'ffn_conv_b': 3.97,
     'final_norm_g': 22.595}
    for name, (base, spread) in spreads.items():
        noise = np.random.default_rng([zlib.crc32(name.encode()), seed]).standard_normal(out[name].shape)
        drawn = base * np.exp(spread * noise) if base else spread * noise
        out[name] = jnp.asarray(drawn.astype(out[name].dtype))
    for name, factor in factors.items():
        out[name] = (out[name] * factor).astype(out[name].dtype)
    return out
```

```python
import math
from contextlib import ExitStack, contextmanager

import concourse.bass as bass
from concourse import mybir

F32 = mybir.dt.float32
F32R = mybir.dt.float32r
BF16 = mybir.dt.bfloat16
ALU = mybir.AluOpType
ACT = mybir.ActivationFunctionType
AX = mybir.AxisListType

P = 128
SLOT = 2048
EPS = 1e-6
SOFTCAP = 15.0
MASKED = -1e30
LAM_INIT = 0.8 - 0.6 * math.exp(-0.3 * 1)


@contextmanager
def by_two(engine, start, stop):
    with engine.Fori(0, (stop - start) // 2) as pair:
        yield pair * 2 + start


def build_trunk(nc, x, attn_norm_g, ffn_norm_g, mlstm_w_in, mlstm_b_gate, mlstm_head_g, mlstm_w_out,
                kv_norm_g, w_kv, diff_w_q, diff_lambda_q1, diff_lambda_k1, diff_lambda_q2,
                diff_lambda_k2, diff_subln_g, diff_w_out, ffn_w_up, ffn_conv_w, ffn_conv_b,
                ffn_w_down, final_norm_g, out):
    S, D = x.shape[1], x.shape[2]
    KT = D // P
    TB = S // P
    HA = mlstm_head_g.shape[1]
    DVA = mlstm_head_g.shape[2]
    DKA = P
    HB = D // P
    HDB = P // 2
    DFF = ffn_conv_b.shape[1]
    FT = DFF // P
    assert (S, D, HA, DVA, FT) == (512, 1024, 4, 256, 22)
    HALVES = ((0, 12), (12, 10))
    HT = 12

    U_HEAD, E_HEAD = 0, 0
    U_OUTA, E_OUTA = 4 * HA, 8 * HA
    U_FFN0, E_FFN0 = U_OUTA + KT // 2, E_OUTA + KT
    n_ffn = FT + 2 * KT
    U_V, E_V = U_FFN0 + n_ffn, E_FFN0 + n_ffn
    U_QK, E_QK = U_V + 4, E_V + 4 * TB
    U_OUTB, E_OUTB = U_QK + HB, E_QK + 2 * HB
    U_FFN1, E_FFN1 = U_OUTB + KT // 2, E_OUTB + KT
    U_END = U_FFN1 + n_ffn
    U_FFN, E_FFN = (U_FFN0, U_FFN1), (E_FFN0, E_FFN1)
    S_FFN = (1, 3)
    G_STAGE = {0: 0, 1: 16, 3: 24, 4: 40}
    G_Q, G_KV, G_HEAD, G_SUB = 8, 32, 48, 56

    es = ExitStack()
    with es:
        def sb(name, shape, dt):
            return es.enter_context(nc.sbuf_tensor(name, shape, dt))

        def sem(name):
            return es.enter_context(nc.semaphore(name))

        ps = es.enter_context(nc.psum_tensor("ps", [P, 8, 512], F32))

        xT = sb("xT", [P, KT, S], F32)
        xs_hi = sb("xs_hi", [P, KT, S], F32R)
        xs_lo = sb("xs_lo", [P, KT, S], F32R)
        wraw = sb("wraw", [P, 2, SLOT], F32)
        w_hi = sb("w_hi", [P, 2, SLOT], F32R)
        w_lo = sb("w_lo", [P, 2, SLOT], F32R)
        h_hi = sb("h_hi", [P, HT, S], F32R)
        h_lo = sb("h_lo", [P, HT, S], F32R)
        mixR = sb("mixR", [P, 8 * S], F32R)
        mixF = sb("mixF", [P, 14 * S], F32)
        rowsM = sb("rowsM", [HA, 2 * S], F32)
        rstd = sb("rstd", [P, S], F32)
        sqacc = sb("sqacc", [P, S], F32)
        sq = sb("sq", [P, 2, S], F32)
        ytmp = sb("ytmp", [P, S], F32)
        ident = sb("ident", [P, P], F32)
        onesf = sb("onesf", [P, P], F32)
        ones_r = sb("ones_r", [P, P], F32R)
        tri = sb("tri", [P, P], F32)
        ident_b = sb("ident_b", [P, P], BF16)
        mask_b = sb("mask_b", [P, P], BF16)
        gainT = sb("gainT", [P, 57], F32)
        convT = sb("convT", [P, 2, 4 * FT], F32)
        acol = sb("acol", [P, 4 * HA], F32)
        rcol = sb("rcol", [P, TB], F32)
        eps = sb("eps", [P, 1], F32)
        bgate = sb("bgate", [P, 2], F32)
        lam_in = sb("lam_in", [1, 4, HDB], F32)
        lam_w = sb("lam_w", [1, 8], F32)
        coef = sb("coef", [P, 2], F32)
        nmax = sb("nmax", [P, 2, 2], F32)
        lsum = sb("lsum", [P, 2, 2], F32)
        rsum = sb("rsum", [P, 2, 2], F32)

        def f32(ap):
            return ap.bitcast(F32)

        x_in = mixF[:, 0:4096].rearrange("p (b c) -> p b c", b=TB)
        gain_rows = mixF[0:57, 4096:4224]
        conv_rows = mixF[0:4 * FT, 4224:4480].rearrange("p (l c) -> p l c", l=2)
        wg_raw = mixF[:, 4608:5632].rearrange("p (t c) -> p t c", t=KT)
        wg_hi = h_hi[:, 8:10, :].rearrange("p a b -> p (a b)").rearrange("p (t c) -> p t c", t=KT)
        wg_lo = h_lo[:, 8:10, :].rearrange("p a b -> p (a b)").rearrange("p (t c) -> p t c", t=KT)
        g_z, g_t, g_e, g_L, g_a, g_M = (mixF[0:36, k * S:(k + 1) * S] for k in range(6))

        OFF = [j * S - P * (j * (j - 1) // 2) for j in range(TB)]
        PTRI = OFF[-1] + P
        q_hi, q_lo, k_hi, k_lo = (mixR[:, n * S:(n + 1) * S] for n in range(4))
        v_hi = mixR[:, 4 * S:6 * S].rearrange("p (b c) -> p b c", b=TB)
        v_lo = mixR[:, 6 * S:8 * S].rearrange("p (b c) -> p b c", b=TB)
        p_hi = h_hi[:, 8:11, :].rearrange("p a b -> p (a b)")[:, 0:PTRI]
        p_lo = h_lo[:, 8:11, :].rearrange("p a b -> p (a b)")[:, 0:PTRI]
        decay = mixF[:, 0:PTRI]
        pw = mixF[:, PTRI:2 * PTRI]
        tq, tk, floor, den, num0, num1, var, gate0, gate1 = (
            mixF[:, 2 * PTRI + n * S:2 * PTRI + (n + 1) * S] for n in range(9))
        numsq, gates = (num0, num1), (gate0, gate1)

        v_all = mixF[:, 0:4096].rearrange("p (b c) -> p b c", b=TB)
        prob = mixF[:, 4096:6144].rearrange("p (a c s) -> p a c s", a=2, c=2)
        tqk = (mixF[:, 6144:6656], mixF[:, 6656:7168])
        qk_hi = (q_hi, k_hi)
        qk_lo = (q_lo, k_lo)
        vh_hi = mixR[:, 4 * S:5 * S].rearrange("p (b c) -> p b c", b=TB)
        vh_lo = mixR[:, 5 * S:6 * S].rearrange("p (b c) -> p b c", b=TB)
        pT_hi = h_hi[:, 8:12, :]
        pT_lo = h_lo[:, 8:12, :]

        gpad = mixF[:, 0:2 * (S + 2)].rearrange("p (a s) -> p a s", a=2)
        FB = 2 * (S + 2)
        cv, act_o, hid = (mixF[:, FB + n * 2 * S:FB + (n + 1) * 2 * S]
                          .rearrange("p (a s) -> p a s", a=2) for n in range(3))
        xg_fin = mixF[:, 0:KT * S].rearrange("p (t s) -> p t s", t=KT)
        o_sb = wraw[:, :, :].rearrange("p a (b c) -> p (a b) c", b=2)

        x_loaded = sem("x_loaded")
        rows_loaded = sem("rows_loaded")
        wg_loaded = sem("wg_loaded")
        const_made = sem("const_made")
        bg_zeroed = sem("bg_zeroed")
        wg_zeroed = sem("wg_zeroed")
        ones_r_made = sem("ones_r_made")
        rows_turned = sem("rows_turned")
        rows_kept = sem("rows_kept")
        x_turned = sem("x_turned")
        x_kept = sem("x_kept")
        wg_hi_made = sem("wg_hi_made")
        wg_split = sem("wg_split")
        bg_scaled = sem("bg_scaled")
        lam_dve = sem("lam_dve")
        lam_exp = sem("lam_exp")
        lam_spread = sem("lam_spread")
        lam_kept = sem("lam_kept")
        sub_scaled = sem("sub_scaled")
        gate_mm = sem("gate_mm")
        gate_z = sem("gate_z")
        gate_act = sem("gate_act")
        gate_scan = sem("gate_scan")
        rows_made = sem("rows_made")
        a_turned = sem("a_turned")
        acol_made = sem("acol_made")

        slot_loaded = [sem("slot0_loaded"), sem("slot1_loaded")]
        w_scaled = sem("w_scaled")
        w_hi_made = sem("w_hi_made")
        w_split = sem("w_split")
        unit_done = sem("unit_done")
        evacuated = sem("evacuated")

        xs_hi_made = sem("xs_hi_made")
        x_split = sem("x_split")
        sq_made = sem("sq_made")
        sq_added = sem("sq_added")
        norm_summed = sem("norm_summed")
        std_made = sem("std_made")
        rstd_made = sem("rstd_made")
        rcol_turned = sem("rcol_turned")
        rcol_made = sem("rcol_made")

        m_picked = sem("m_picked")
        m_spread = sem("m_spread")
        floor_kept = sem("floor_kept")
        qk_hi_made = sem("qk_hi_made")
        qk_split = sem("qk_split")
        arg_made = sem("arg_made")
        decay_made = sem("decay_made")
        decay_masked = sem("decay_masked")
        v_hi_made = sem("v_hi_made")
        scored = sem("scored")
        p_made = sem("p_made")
        p_hi_made = sem("p_hi_made")
        p_split = sem("p_split")
        pv_done = sem("pv_done")
        gate_open = sem("gate_open")
        den_made = sem("den_made")
        den_sq = sem("den_sq")
        num_sq = sem("num_sq")
        num_added = sem("num_added")
        head_summed = sem("head_summed")
        var_made = sem("var_made")
        head_std = sem("head_std")
        head_rstd = sem("head_rstd")
        gate_scaled = sem("gate_scaled")
        y_made = sem("y_made")
        y_hi_made = sem("y_hi_made")
        y_split = sem("y_split")

        pads_zeroed = sem("pads_zeroed")
        g_made = sem("g_made")
        tap2 = sem("tap2")
        tap1 = sem("tap1")
        tap0 = sem("tap0")
        silu_made = sem("silu_made")
        silu_scaled = sem("silu_scaled")
        hid_hi_made = sem("hid_hi_made")
        hid_split = sem("hid_split")

        dscored = sem("dscored")
        maxed = sem("maxed")
        exped = sem("exped")
        sum_inv = sem("sum_inv")
        sum_coef = sem("sum_coef")
        p0_scaled = sem("p0_scaled")
        a_made = sem("a_made")
        pT_turned = sem("pT_turned")
        pT_hi_made = sem("pT_hi_made")
        pT_split = sem("pT_split")
        vh_hi_made = sem("vh_hi_made")
        vh_split = sem("vh_split")
        dqk_hi_made = sem("dqk_hi_made")
        dqk_split = sem("dqk_split")
        dpv_done = sem("dpv_done")
        o_sq = sem("o_sq")
        o_summed = sem("o_summed")
        o_ln = sem("o_ln")
        o_rstd = sem("o_rstd")
        o_made = sem("o_made")
        o_hi_made = sem("o_hi_made")
        o_split = sem("o_split")

        fin_summed = sem("fin_summed")
        fin_std = sem("fin_std")
        fin_rstd = sem("fin_rstd")
        fin_turned = sem("fin_turned")
        fin_scaled_a = sem("fin_scaled_a")
        fin_scaled_v = sem("fin_scaled_v")
        out_stored = sem("out_stored")

        block = es.enter_context(nc.Block())

        w_in = mlstm_w_in[0].rearrange("(t p) n -> p t n", p=P)
        w_outA = mlstm_w_out[0].rearrange("(t p) n -> p t n", p=P)
        w_kvr = w_kv.rearrange("(t p) n -> p t n", p=P)
        w_q = diff_w_q[0].rearrange("(t p) n -> p t n", p=P)
        w_outB = diff_w_out[0].rearrange("(t p) n -> p t n", p=P)
        w_up = [ffn_w_up[l].rearrange("(t p) n -> p t n", p=P) for l in range(2)]
        w_down = [ffn_w_down[l].rearrange("(t p) n -> p t n", p=P) for l in range(2)]

        def cols(w, t, c):
            return w[:, 0:t * c].rearrange("p (t c) -> p t c", t=t)

        @block.sync
        def _(sp):
            def free_slot(u, peeled=False):
                if not peeled:
                    sp.wait_ge(w_split, u - 1)

            def load_pair(u, s, left, right, peeled=False):
                free_slot(u, peeled)
                d = cols(wraw[:, s, :], KT, 2 * P)
                sp.dma_start(d[:, :, 0:P], left).then_inc(slot_loaded[s], 16)
                sp.dma_start(d[:, :, P:2 * P], right).then_inc(slot_loaded[s], 16)

            def load_block(u, s, src, peeled=False):
                free_slot(u, peeled)
                t, c = src.shape[1], src.shape[2]
                d = cols(wraw[:, s, :], t, c)
                sp.dma_start(d[:, 0:t // 2, :], src[:, 0:t // 2, :]).then_inc(slot_loaded[s], 16)
                sp.dma_start(d[:, t // 2:t, :], src[:, t // 2:t, :]).then_inc(slot_loaded[s], 16)

            def load_head(h, first=False):
                u = 4 * h
                load_pair(u, 0, w_in[:, :, bass.ds(h * DKA, P)],
                          w_in[:, :, bass.ds(h * DKA + HA * DKA, P)], first)
                load_block(u + 1, 1, w_in[:, :, bass.ds(h * DVA + 2 * HA * DKA, DVA)], first)
                for v in range(2):
                    load_block(u + 2 + v, v, w_in[:, :, bass.ds(h * DVA + 2 * HA * DKA + HA * DVA + v * P, P)])

            def load_ffn(l):
                u0 = U_FFN[l]
                for k0, n in HALVES:
                    with by_two(sp, 0, n) as i:
                        for s in range(2):
                            load_pair(i + (u0 + s), s, w_up[l][:, :, bass.ds((i + (k0 + s)) * P, P)],
                                      w_up[l][:, :, bass.ds((i + (k0 + s)) * P + DFF, P)])
                    u0 += n
                    with by_two(sp, 0, KT) as j:
                        for s in range(2):
                            load_block(j + (u0 + s), s, w_down[l][:, k0:k0 + n, bass.ds((j + s) * P, P)])
                    u0 += KT

            xr = x[0].rearrange("(b p) d -> p b d", p=P)
            for b in range(TB):
                sp.dma_start(x_in[:, b, :], xr[:, b, :]).then_inc(x_loaded, 16)
            load_head(0, first=True)
            with sp.Fori(1, HA) as h:
                load_head(h)
            for m in range(KT // 2):
                load_block(U_OUTA + m, m % 2, w_outA[:, :, m * 2 * P:(m + 1) * 2 * P])
            load_ffn(0)
            for m in range(4):
                load_block(U_V + m, m % 2, w_kvr[:, :, D + m * 2 * P:D + (m + 1) * 2 * P])
            with by_two(sp, 0, HB) as h:
                for s in range(2):
                    load_pair(h + (U_QK + s), s, w_q[:, :, bass.ds((h + s) * P, P)],
                              w_kvr[:, :, bass.ds((h + s) * P, P)])
            for m in range(KT // 2):
                load_block(U_OUTB + m, m % 2, w_outB[:, :, m * 2 * P:(m + 1) * 2 * P])
            load_ffn(1)
            outr = out[0].rearrange("(b p) (a d) -> b a p d", p=P, a=2)
            for b in range(TB):
                for a in range(2):
                    sp.wait_ge(fin_scaled_v if a else fin_scaled_a, b + 1)
                    sp.dma_start(outr[b, a], o_sb[:, b, a * 512:(a + 1) * 512]).then_inc(out_stored, 16)
            sp.wait_ge(out_stored, 16 * 2 * TB)

        @block.gpsimd
        def _(pool):
            pool.memset(ident[:, :], 0.0).then_inc(const_made, 1)
            pool.memset(onesf[:, :], 1.0).then_inc(const_made, 1)
            pool.memset(ident_b[:, :], 0.0).then_inc(const_made, 1)
            pool.memset(mask_b[:, :], 0.0).then_inc(const_made, 1)
            pool.memset(eps[:, :], EPS).then_inc(const_made, 1)
            pool.memset(coef[:, :], 1.0).then_inc(const_made, 1)
            pool.memset(bgate[:, :], 0.0).then_inc(bg_zeroed, 1)
            pool.memset(mixF[:, 4608:5632], 0.0).then_inc(wg_zeroed, 1)
            pool.wait_ge(const_made, 6)
            pool.affine_select(out=ident[:, :], in_=ident[:, :], compare_op=ALU.not_equal, fill=1.0,
                               base=0, pattern=[[-1, P]], channel_multiplier=1).then_inc(const_made, 1)
            pool.affine_select(out=ident_b[:, :], in_=ident_b[:, :], compare_op=ALU.not_equal, fill=1.0,
                               base=0, pattern=[[-1, P]], channel_multiplier=1).then_inc(const_made, 1)
            pool.affine_select(out=mask_b[:, :], in_=mask_b[:, :], compare_op=ALU.is_ge, fill=MASKED,
                               base=0, pattern=[[-1, P]], channel_multiplier=1).then_inc(const_made, 1)
            pool.affine_select(out=tri[:, :], in_=onesf[:, :], compare_op=ALU.is_ge, fill=0.0,
                               base=0, pattern=[[1, P]], channel_multiplier=-1).then_inc(const_made, 1)

            def add_squares(s, j):
                n = 8 * s + j
                pool.wait_ge(sq_made, n + 1)
                if j == 0:
                    if s:
                        pool.wait_ge(norm_summed, s)
                    pool.tensor_copy(sqacc[:, :], sq[:, 0, :]).then_inc(sq_added, 1)
                else:
                    pool.wait_ge(sq_added, n)
                    pool.tensor_tensor(sqacc[:, :], sqacc[:, :], sq[:, j % 2, :], ALU.add)\
                        .then_inc(sq_added, 1)

            def head(h, first=False):
                pool.wait_ge(decay_made, h + 1)
                for j in range(TB):
                    d = decay[:, OFF[j]:OFF[j] + P]
                    pool.tensor_tensor(d, d, tri[:, :], ALU.mult).then_inc(decay_masked, 1)
                pool.wait_ge(num_sq, 2 * h + 2)
                pool.tensor_tensor(num0, num0, num1, ALU.add).then_inc(num_added, 1)
                pool.wait_ge(gate_open, 2 * h + 2)
                pool.wait_ge(head_rstd, h + 1)
                for v in range(2):
                    pool.tensor_tensor(gates[v], gates[v], den, ALU.mult).then_inc(gate_scaled, 1)
                for v in range(2):
                    pool.wait_ge(y_hi_made, 2 * h + v + 1)
                    t = h * 2 + v
                    pool.tensor_tensor(h_lo[:, t, :], numsq[v], f32(h_hi[:, t, :]), ALU.subtract)\
                        .then_inc(y_split, 1)

            def ffn_up(i, f0, s):
                f = i + (f0 + s)
                pool.wait_ge(silu_made, f + 1)
                pool.tensor_tensor(act_o[:, s, :], act_o[:, s, :], rstd[:, :], ALU.mult)\
                    .then_inc(silu_scaled, 1)
                pool.wait_ge(hid_hi_made, f + 1)
                pool.tensor_tensor(h_lo[:, i + s, :], hid[:, s, :], f32(h_hi[:, i + s, :]), ALU.subtract)\
                    .then_inc(hid_split, 1)

            def scale_unit(u, s, gl, gr):
                pool.wait_ge(slot_loaded[s], (u - s) * 16 + 32)
                d = cols(wraw[:, s, :], KT, 2 * P)
                for side, g in enumerate((gl, gr)):
                    half = d[:, :, side * P:(side + 1) * P]
                    pool.tensor_tensor(half, half, gainT[:, g:g + KT].unsqueeze(2).broadcast_to([P, KT, P]),
                                       ALU.mult).then_inc(w_scaled, 1)

            def ffn(l):
                for n_half, (k0, n) in enumerate(HALVES):
                    with by_two(pool, 0, n) as i:
                        for s in range(2):
                            ffn_up(i, l * FT + k0, s)
                for j in range(KT):
                    if l == 0 and j == KT - 1:
                        scale_unit(U_V, 0, G_KV, G_KV)
                    add_squares(S_FFN[l] + 1, j)

            for j in range(KT):
                add_squares(0, j)
            head(0, first=True)
            with pool.Fori(1, HA) as h:
                head(h)
            for j in range(KT):
                add_squares(1, j)
            ffn(0)
            for m in range(1, 4):
                scale_unit(U_V + m, m % 2, G_KV, G_KV)

            def attn_o_lo(h):
                pool.wait_ge(o_hi_made, h + 1)
                pool.tensor_tensor(h_lo[:, h, :], ytmp[:, :], f32(h_hi[:, h, :]), ALU.subtract)\
                    .then_inc(o_split, 1)

            def vh_lo_made(h):
                pool.wait_ge(vh_hi_made, h + 1)
                pool.tensor_tensor(vh_lo, v_all[:, :, bass.ds(h * P, P)], f32(vh_hi), ALU.subtract)\
                    .then_inc(vh_split, 1)

            scale_unit(U_QK, 0, G_Q, G_KV)
            vh_lo_made(0)
            scale_unit(U_QK + 1, 1, G_Q, G_KV)

            def attn(h, s, scale=True, nxt=True, prev=True):
                if scale:
                    scale_unit(h + (U_QK + 2), s, G_Q, G_KV)
                if prev:
                    attn_o_lo(h - 1)
                if nxt:
                    vh_lo_made(h + 1)

            attn(0, 0, prev=False)
            with by_two(pool, 1, HB - 3) as h:
                attn(h, 1)
                attn(h + 1, 0)
            attn(HB - 3, 1)
            attn(HB - 2, 0, scale=False)
            attn(HB - 1, 1, scale=False, nxt=False)
            attn_o_lo(HB - 1)
            for j in range(KT):
                add_squares(3, j)
            ffn(1)

        @block.scalar
        def _(act):
            n = 0
            for src in (attn_norm_g.rearrange("l (t p) -> (l t) p", p=P),
                        ffn_norm_g.rearrange("l (t p) -> (l t) p", p=P),
                        kv_norm_g.rearrange("(t p) -> t p", p=P),
                        final_norm_g.rearrange("(t p) -> t p", p=P),
                        mlstm_head_g[0].rearrange("h (t p) -> (h t) p", p=P),
                        diff_subln_g):
                act.dma_start(gain_rows[n:n + src.shape[0], :], src).then_inc(rows_loaded, 16)
                n += src.shape[0]
            for l in range(2):
                act.dma_start(conv_rows[0:3 * FT, l, :],
                              ffn_conv_w[l].rearrange("w (t p) -> (w t) p", p=P)).then_inc(rows_loaded, 16)
                act.dma_start(conv_rows[3 * FT:4 * FT, l, :],
                              ffn_conv_b[l].rearrange("(t p) -> t p", p=P)).then_inc(rows_loaded, 16)
            for n, src in enumerate((diff_lambda_q1, diff_lambda_k1, diff_lambda_q2, diff_lambda_k2)):
                act.dma_start(lam_in[0:1, n, :], src).then_inc(rows_loaded, 16)
            ROWS = 16 * 14
            act.wait_ge(bg_zeroed, 1)
            act.wait_ge(wg_zeroed, 1)
            wg = w_in[:, :, 2 * HA * (DKA + DVA):]
            bg = mlstm_b_gate.rearrange("a n -> n a")
            for r, c in ((0, 0), (32, HA)):
                act.dma_start(wg_raw[:, :, r:r + HA], wg[:, :, c:c + HA]).then_inc(wg_loaded, 16)
                act.dma_start(bgate[r:r + HA, 0:1], bg[c:c + HA, :]).then_inc(wg_loaded, 16)

            def weights_hi(u, s, scaled=None):
                if scaled is None:
                    act.wait_ge(slot_loaded[s], (u - s) * 16 + 32)
                else:
                    act.wait_ge(w_scaled, scaled)
                if not isinstance(u, int) or u >= 2:
                    act.wait_ge(unit_done, u - 1)
                act.activation(w_hi[:, s, :], wraw[:, s, :], ACT.Copy).then_inc(w_hi_made, 1)

            def split_x(s, j):
                n = 8 * s + j
                if s == 0:
                    act.wait_ge(x_kept, j + 1)
                g = G_STAGE.get(s)
                dst = xg_fin if s == 4 else xs_hi
                act.activation(dst[:, j, :], xT[:, j, :], ACT.Copy,
                               scale=1.0 if g is None else gainT[:, g + j:g + j + 1]).then_inc(xs_hi_made, 1)
                if n >= 2:
                    act.wait_ge(sq_added, n - 1)
                act.activation(sq[:, j % 2, :], xT[:, j, :], ACT.Square).then_inc(sq_made, 1)

            def norm_std(s):
                act.wait_ge(norm_summed, s + 1)
                act.activation(sq[:, 0, :], ps[:, 7, :], ACT.Sqrt, scale=1.0 / D, bias=eps[:, :])\
                    .then_inc(std_made, 1)

            act.wait_ge(rows_loaded, ROWS)
            act.wait_ge(lam_dve, 2)
            act.activation(lam_w[:, 4:6], lam_w[:, 2:4], ACT.Exp).then_inc(lam_exp, 1)
            act.wait_ge(const_made, 10)
            act.activation(ones_r[:, :], onesf[:, :], ACT.Copy).then_inc(ones_r_made, 1)
            act.wait_ge(wg_loaded, 64)
            act.activation(wg_hi, wg_raw, ACT.Copy).then_inc(wg_hi_made, 1)
            act.mul(bgate[:, 1:2], bgate[:, 0:1], 1.0 / SOFTCAP).then_inc(bg_scaled, 1)
            act.wait_ge(rows_kept, 3)
            split_x(0, 0)
            split_x(0, 1)
            weights_hi(0, 0)
            for j in range(2, KT):
                split_x(0, j)
            norm_std(0)
            act.wait_ge(gate_z, 1)
            act.wait_ge(bg_scaled, 1)
            act.activation(g_t, g_z, ACT.Tanh, scale=1.0 / SOFTCAP, bias=bgate[0:36, 1:2])\
                .then_inc(gate_act, 1)
            act.wait_ge(gate_act, 1)
            act.activation(g_e[32:36, :], g_t[32:36, :], ACT.Exp, scale=-SOFTCAP).then_inc(gate_act, 1)
            act.wait_ge(gate_act, 2)
            act.activation(g_e[32:36, :], g_e[32:36, :], ACT.Ln, bias=1.0).then_inc(gate_act, 1)
            act.wait_ge(gate_scan, 4)
            act.activation(rowsM[:, S:2 * S], g_z[0:HA, :], ACT.Exp).then_inc(rows_made, 1)

            def head(h, first=False, nxt_slot_wait=True):
                u = 4 * h
                weights_hi(u + 1, 1)
                for n, t in enumerate((tq, tk)):
                    act.wait_ge(evacuated, 8 * h + 1 + n)
                    act.activation(qk_hi[n], t, ACT.Copy).then_inc(qk_hi_made, 1)
                act.wait_ge(m_spread, 2 * h + 2)
                act.activation(floor, ps[:, 6, :], ACT.Square, scale=math.sqrt(EPS)).then_inc(floor_kept, 1)
                weights_hi(u + 2, 0)
                act.wait_ge(arg_made, 4 * h + 4)
                act.activation(decay, decay, ACT.Exp).then_inc(decay_made, 1)
                act.wait_ge(unit_done, u + 2)
                act.wait_ge(rcol_made, 1)
                for b in range(TB):
                    act.activation(v_hi[:, b, :], ps[:, 2 + b // 2, (b % 2) * DVA:(b % 2 + 1) * DVA], ACT.Copy,
                                   scale=rcol[:, b:b + 1]).then_inc(v_hi_made, 1)
                act.wait_ge(p_made, 4 * h + 4)
                act.activation(p_hi, pw, ACT.Copy).then_inc(p_hi_made, 1)
                weights_hi(u + 3, 1)
                act.wait_ge(evacuated, 8 * h + 7)
                act.activation(gate0, gate0, ACT.Sigmoid).then_inc(gate_open, 1)
                weights_hi(u + 4, 0)
                if not first:
                    act.wait_ge(y_split, 2 * h)
                for v in range(2):
                    act.wait_ge(pv_done, 3 * h + v + 1)
                    act.activation(numsq[v], ps[:, 4 + v, :], ACT.Square).then_inc(num_sq, 1)
                act.wait_ge(pv_done, 3 * h + 3)
                act.activation(den, ps[:, 6, :], ACT.Square, scale=math.sqrt(EPS)).then_inc(den_sq, 1)
                act.wait_ge(evacuated, 8 * h + 8)
                act.activation(gate1, gate1, ACT.Sigmoid).then_inc(gate_open, 1)
                act.wait_ge(var_made, h + 1)
                act.activation(var, var, ACT.Sqrt).then_inc(head_std, 1)
                for v in range(2):
                    act.wait_ge(y_made, 2 * h + v + 1)
                    act.activation(h_hi[:, h * 2 + v, :], numsq[v], ACT.Copy).then_inc(y_hi_made, 1)

            def out_proj(u0, e0, s):
                for m in range(KT // 2):
                    weights_hi(u0 + m + 1, (m + 1) % 2)
                    for t in range(2):
                        act.wait_ge(evacuated, e0 + 2 * m + t + 1)
                        split_x(s, 2 * m + t)

            def ffn(l, next_scaled=None):
                u0, e0, f0 = U_FFN[l], E_FFN[l], l * FT
                for n_half, (k0, n) in enumerate(HALVES):
                    def up(i, s, norm=False):
                        u, f = i + (u0 + s), i + (f0 + s)
                        weights_hi(u + 1, 1 - s)
                        if norm:
                            norm_std(S_FFN[l])
                        c = i + (k0 + s)
                        act.wait_ge(g_made, f + 1)
                        act.activation(cv[:, s, :], gpad[:, s, 2:S + 2], ACT.Identity,
                                       scale=convT[:, l, bass.ds(c + 2 * FT, 1)],
                                       bias=convT[:, l, bass.ds(c + 3 * FT, 1)]).then_inc(tap2, 1)
                        act.wait_ge(tap0, f + 1)
                        act.activation(act_o[:, s, :], cv[:, s, :], ACT.Silu).then_inc(silu_made, 1)
                        act.wait_ge(evacuated, i + (e0 + s) + 1)
                        act.activation(h_hi[:, i + s, :], hid[:, s, :], ACT.Copy).then_inc(hid_hi_made, 1)

                    first = 0
                    if n_half == 0:
                        up(0, 0, norm=True)
                        up(0, 1)
                        first = 2
                    with by_two(act, first, n) as i:
                        up(i, 0)
                        up(i, 1)
                    u0, e0, f0 = u0 + n, e0 + n, f0 + n

                    def down(j, s, scaled=None):
                        u = j + (u0 + s)
                        if not (isinstance(u, int) and u + 1 >= U_END):
                            weights_hi(u + 1, 1 - s, scaled)
                        if n_half == 1:
                            act.wait_ge(evacuated, j + (e0 + s) + 1)
                            split_x(S_FFN[l] + 1, j + s)

                    if n_half == 0:
                        with by_two(act, 0, KT) as j:
                            down(j, 0)
                            down(j, 1)
                    else:
                        for j in range(0, KT, 2):
                            down(j, 0)
                            down(j, 1, next_scaled if j == KT - 2 else None)
                    u0, e0 = u0 + KT, e0 + KT

            head(0, first=True)
            with act.Fori(1, HA) as h:
                head(h)
            out_proj(U_OUTA, E_OUTA, 1)
            ffn(0, next_scaled=2)

            for m in range(4):
                weights_hi(U_V + m + 1, (m + 1) % 2, 2 * (m + 2))
                if m == 0:
                    norm_std(2)

            def attn_qk_hi(h):
                for n in range(2):
                    act.wait_ge(evacuated, 2 * h + (E_QK + n + 1))
                    act.activation(qk_hi[n], tqk[n], ACT.Copy).then_inc(dqk_hi_made, 1)

            def attn_v_hi(h):
                act.activation(vh_hi, v_all[:, :, bass.ds(h * P, P)], ACT.Copy).then_inc(vh_hi_made, 1)

            def attn_exp(h, i, first):
                for c in range(2):
                    act.wait_ge(maxed, 8 * h + (2 * i + c + 1))
                    if not (first and i < 2):
                        act.wait_ge(pT_turned, 4 * h + (i - 1))
                    act.activation(prob[:, i % 2, c, 0:(i + 1) * P], ps[:, 2 + (i % 2) * 2 + c, 0:(i + 1) * P],
                                   ACT.Exp, bias=nmax[:, i % 2, c:c + 1],
                                   accum_out=lsum[:, i % 2, c:c + 1]).then_inc(exped, 1)

            def attn_pT_hi(h, i):
                act.wait_ge(pT_turned, 4 * h + (i + 1))
                act.activation(pT_hi[:, 0:i + 1, i * P:(i + 1) * P],
                               ps[:, 6, 0:(i + 1) * P].rearrange("p (j c) -> p j c", c=P), ACT.Copy)\
                    .then_inc(pT_hi_made, 1)

            def attn_finish(h):
                act.wait_ge(o_summed, h + 1)
                act.activation(sq[:, 1, :], ps[:, 6, :], ACT.Ln, scale=1.0 / P, bias=eps[:, :])\
                    .then_inc(o_ln, 1)
                act.wait_ge(o_ln, h + 1)
                act.activation(sqacc[:, :], sq[:, 1, :], ACT.Exp, scale=-0.5).then_inc(o_rstd, 1)
                act.wait_ge(o_made, h + 1)
                act.activation(h_hi[:, h, :], ytmp[:, :], ACT.Copy).then_inc(o_hi_made, 1)

            def attn(h, s, scaled, prev=True, nxt=True, more=True):
                if more:
                    weights_hi(h + (U_QK + 2), s, scaled)
                attn_exp(h, 0, not prev)
                attn_exp(h, 1, not prev)
                if prev:
                    attn_finish(h - 1)
                attn_exp(h, 2, not prev)
                attn_pT_hi(h, 0)
                attn_exp(h, 3, not prev)
                for i in range(1, TB):
                    attn_pT_hi(h, i)
                if nxt:
                    attn_qk_hi(h + 1)
                act.wait_ge(dpv_done, h + 1)
                act.activation(sq[:, 0, :], ps[:, 7, :], ACT.Square).then_inc(o_sq, 1)
                if nxt:
                    attn_v_hi(h + 1)

            SC = 2 * 4
            act.wait_ge(evacuated, E_QK)
            attn_v_hi(0)
            attn_qk_hi(0)
            weights_hi(U_QK + 1, 1, SC + 4)
            attn(0, 0, SC + 2 * 3, prev=False)
            with by_two(act, 1, HB - 3) as h:
                attn(h, 1, 2 * h + (SC + 6))
                attn(h + 1, 0, 2 * h + (SC + 8))
            attn(HB - 3, 1, SC + 2 * HB)
            attn(HB - 2, 0, None)
            attn(HB - 1, 1, None, nxt=False, more=False)
            attn_finish(HB - 1)
            out_proj(U_OUTB, E_OUTB, 3)
            ffn(1)

            act.wait_ge(fin_summed, 1)
            act.activation(rcol[:, :], ps[:, 7, 0:TB], ACT.Sqrt, scale=1.0 / D, bias=eps[:, :])\
                .then_inc(fin_std, 1)
            act.wait_ge(fin_rstd, 1)
            for b in range(TB):
                act.wait_ge(fin_turned, 2 * b + 1)
                act.activation(o_sb[:, b, 0:512], ps[:, 2 * b, :], ACT.Copy, scale=rcol[:, b:b + 1])\
                    .then_inc(fin_scaled_a, 1)

        @block.vector
        def _(dve):
            dve.wait_ge(rows_loaded, 16 * 14)
            dve.tensor_tensor(ytmp[0:1, 0:2 * HDB].rearrange("p (a c) -> p a c", a=2),
                              lam_in[:, 0:4:2, :], lam_in[:, 1:4:2, :], ALU.mult).then_inc(lam_dve, 1)
            dve.wait_ge(lam_dve, 1)
            dve.tensor_reduce(lam_w[:, 2:4], ytmp[0:1, 0:2 * HDB].rearrange("p (a c) -> p a c", a=2),
                              AX.X, ALU.add).then_inc(lam_dve, 1)
            dve.wait_ge(rows_turned, 3)
            dve.tensor_copy(gainT[:, :], ps[:, 4, 0:57]).then_inc(rows_kept, 1)
            for l in range(2):
                dve.tensor_copy(convT[:, l, :], ps[:, 4, 64 + 96 * l:64 + 96 * l + 4 * FT])\
                    .then_inc(rows_kept, 1)
            dve.wait_ge(wg_hi_made, 1)
            dve.tensor_tensor(wg_lo, wg_raw, f32(wg_hi), ALU.subtract).then_inc(wg_split, 1)
            dve.wait_ge(lam_exp, 1)
            dve.tensor_tensor(lam_w[:, 6:7], lam_w[:, 5:6], lam_w[:, 4:5], ALU.subtract).then_inc(lam_dve, 1)
            dve.wait_ge(lam_dve, 3)
            dve.tensor_scalar(lam_w[:, 7:8], lam_w[:, 6:7], -LAM_INIT, None, ALU.add).then_inc(lam_dve, 1)
            dve.wait_ge(rows_kept, 3)
            dve.tensor_scalar(gainT[:, G_SUB:G_SUB + 1], gainT[:, G_SUB:G_SUB + 1], 1.0 - LAM_INIT, None,
                              ALU.mult).then_inc(sub_scaled, 1)

            def weights_lo(u, s):
                dve.wait_ge(w_hi_made, u + 1)
                dve.tensor_tensor(w_lo[:, s, :], wraw[:, s, :], f32(w_hi[:, s, :]), ALU.subtract)\
                    .then_inc(w_split, 1)

            def split_x(s, j):
                n = 8 * s + j
                g = G_STAGE.get(s)
                dve.wait_ge(xs_hi_made, n + 1)
                if g is None:
                    dve.tensor_tensor(xs_lo[:, j, :], xT[:, j, :], f32(xs_hi[:, j, :]), ALU.subtract)\
                        .then_inc(x_split, 1)
                else:
                    dve.scalar_tensor_tensor(out=xs_lo[:, j, :], in0=xT[:, j, :], scalar=gainT[:, g + j:g + j + 1],
                                             in1=f32(xs_hi[:, j, :]), op0=ALU.mult, op1=ALU.subtract)\
                        .then_inc(x_split, 1)

            def norm_rstd(s):
                dve.wait_ge(std_made, s + 1)
                dve.reciprocal(rstd[:, :], sq[:, 0, :]).then_inc(rstd_made, 1)

            for j in range(KT):
                dve.wait_ge(x_turned, j + 1)
                dve.tensor_copy(xT[:, j, :], ps[:, j, :]).then_inc(x_kept, 1)
                if j:
                    split_x(0, j - 1)
            split_x(0, KT - 1)
            weights_lo(0, 0)
            dve.wait_ge(lam_spread, 1)
            dve.tensor_copy(coef[:, 1:2], ps[:, 4, 32:33]).then_inc(lam_kept, 1)
            norm_rstd(0)
            dve.wait_ge(gate_mm, 1)
            dve.wait_ge(rstd_made, 1)
            dve.tensor_tensor(g_z, ps[0:36, 5, :], rstd[0:36, :], ALU.mult).then_inc(gate_z, 1)
            dve.wait_ge(gate_act, 3)
            dve.tensor_tensor_scan(g_L[0:HA, :], g_e[32:36, :], g_e[32:36, :], 0.0, ALU.add, ALU.max)\
                .then_inc(gate_scan, 1)
            dve.wait_ge(gate_scan, 1)
            dve.scalar_tensor_tensor(out=g_a[0:HA, :], in0=g_t[0:HA, :], scalar=SOFTCAP, in1=g_L[0:HA, :],
                                     op0=ALU.mult, op1=ALU.add).then_inc(gate_scan, 1)
            dve.wait_ge(gate_scan, 2)
            dve.tensor_tensor_scan(g_M[0:HA, :], g_a[0:HA, :], g_a[0:HA, :], 0.0, ALU.max, ALU.max)\
                .then_inc(gate_scan, 1)
            dve.wait_ge(gate_scan, 3)
            dve.tensor_tensor(g_z[0:HA, :], g_L[0:HA, :], g_M[0:HA, :], ALU.subtract).then_inc(gate_scan, 1)
            dve.tensor_scalar(rowsM[:, 0:S], g_M[0:HA, :], -1.0, None, ALU.mult).then_inc(gate_scan, 1)
            dve.wait_ge(a_turned, 1)
            dve.tensor_copy(acol[:, :], ps[:, 5, 0:4 * HA]).then_inc(acol_made, 1)
            dve.wait_ge(rcol_turned, 1)
            dve.tensor_copy(rcol[:, :], ps[:, 4, 0:TB]).then_inc(rcol_made, 1)
            dve.wait_ge(rows_made, 1)
            dve.wait_ge(gate_scan, 5)
            dve.wait_ge(acol_made, 1)
            dve.wait_ge(rcol_made, 1)

            def head(h, first=False):
                u = 4 * h
                if not first:
                    dve.wait_ge(p_split, h)
                dve.tensor_scalar(pw[0:HA, 0:2 * S], rowsM[:, :], ident[0:HA, bass.ds(h, 1)], None, ALU.mult)\
                    .then_inc(m_picked, 1)
                weights_lo(u + 1, 1)
                dve.wait_ge(unit_done, u + 1)
                dve.scalar_tensor_tensor(out=tq, in0=ps[:, 0, :], scalar=DKA ** -0.5, in1=rstd[:, :],
                                         op0=ALU.mult, op1=ALU.mult).then_inc(evacuated, 1)
                dve.tensor_tensor(tk, ps[:, 1, :], rstd[:, :], ALU.mult).then_inc(evacuated, 1)
                dve.wait_ge(m_spread, 2 * h + 1)
                if not first:
                    dve.wait_ge(p_made, 4 * h)
                for j in range(TB):
                    dve.tensor_scalar(decay[:, OFF[j]:OFF[j] + S - j * P], ps[:, 7, j * P:S],
                                      acol[:, bass.ds(h + HA * j, 1)], 0.0, ALU.add, ALU.min)\
                        .then_inc(arg_made, 1)
                for n, t in enumerate((tq, tk)):
                    dve.wait_ge(qk_hi_made, 2 * h + n + 1)
                    dve.tensor_tensor(qk_lo[n], t, f32(qk_hi[n]), ALU.subtract).then_inc(qk_split, 1)
                weights_lo(u + 2, 0)
                for b in range(TB):
                    dve.wait_ge(v_hi_made, 4 * h + (b // 2 * 2 + 2))
                    dve.scalar_tensor_tensor(out=v_lo[:, b, :],
                                             in0=ps[:, 2 + b // 2, (b % 2) * DVA:(b % 2 + 1) * DVA],
                                             scalar=rcol[:, b:b + 1], in1=f32(v_hi[:, b, :]),
                                             op0=ALU.mult, op1=ALU.subtract).then_inc(evacuated, 1)
                dve.wait_ge(decay_masked, 4 * h + 4)
                dve.wait_ge(m_spread, 2 * h + 2)
                for j in range(TB):
                    dve.wait_ge(scored, 4 * h + (j + 1 if j < 2 else 4))
                    src = ps[:, 4 + j, 0:S - j * P] if j < 3 else ps[:, 6, 2 * P:3 * P]
                    dve.tensor_tensor(pw[:, OFF[j]:OFF[j] + S - j * P], src,
                                      decay[:, OFF[j]:OFF[j] + S - j * P], ALU.mult).then_inc(p_made, 1)
                dve.wait_ge(p_hi_made, h + 1)
                dve.tensor_tensor(p_lo, pw, f32(p_hi), ALU.subtract).then_inc(p_split, 1)
                weights_lo(u + 3, 1)
                dve.wait_ge(unit_done, u + 3)
                dve.tensor_tensor(gate0, ps[:, 0, :], rstd[:, :], ALU.mult).then_inc(evacuated, 1)
                weights_lo(u + 4, 0)
                dve.wait_ge(unit_done, u + 4)
                dve.tensor_tensor(gate1, ps[:, 2, :], rstd[:, :], ALU.mult).then_inc(evacuated, 1)
                dve.wait_ge(den_sq, h + 1)
                dve.tensor_tensor(den, den, floor, ALU.max).then_inc(den_made, 1)
                dve.wait_ge(head_summed, h + 1)
                dve.wait_ge(den_made, h + 1)
                dve.scalar_tensor_tensor(out=var, in0=ps[:, 7, :], scalar=1.0 / DVA, in1=den,
                                         op0=ALU.mult, op1=ALU.add).then_inc(var_made, 1)
                dve.wait_ge(head_std, h + 1)
                dve.reciprocal(den, var).then_inc(head_rstd, 1)
                for v in range(2):
                    dve.wait_ge(gate_scaled, 2 * h + v + 1)
                    dve.scalar_tensor_tensor(out=numsq[v], in0=ps[:, 4 + v, :],
                                             scalar=gainT[:, bass.ds(h * 2 + (G_HEAD + v), 1)], in1=gates[v],
                                             op0=ALU.mult, op1=ALU.mult).then_inc(y_made, 1)

            def add_x(tile, bank, wait_u):
                dve.wait_ge(unit_done, wait_u)
                dve.tensor_tensor(xT[:, tile, :], xT[:, tile, :], ps[:, bank, :], ALU.add)\
                    .then_inc(evacuated, 1)

            def out_proj(u0, s):
                for m in range(KT // 2):
                    weights_lo(u0 + m + 1, (m + 1) % 2)
                    for t in range(2):
                        add_x(2 * m + t, 2 * (m % 2) + t, u0 + m + 1)
                    for t in range(2):
                        split_x(s, 2 * m + t)

            def ffn(l):
                u0, f0 = U_FFN[l], l * FT
                dve.memset(gpad[:, :, 0:2], 0.0).then_inc(pads_zeroed, 1)
                for n_half, (k0, n) in enumerate(HALVES):
                    def up(i, s, norm=False):
                        u, f = i + (u0 + s), i + (f0 + s)
                        weights_lo(u + 1, 1 - s)
                        if norm:
                            norm_rstd(S_FFN[l])
                            dve.wait_ge(rstd_made, S_FFN[l] + 1)
                            dve.wait_ge(pads_zeroed, l + 1)
                        c = i + (k0 + s)
                        dve.wait_ge(unit_done, u + 1)
                        dve.tensor_tensor(gpad[:, s, 2:S + 2], ps[:, 2 * s, :], rstd[:, :], ALU.mult)\
                            .then_inc(g_made, 1)
                        dve.wait_ge(tap2, f + 1)
                        dve.scalar_tensor_tensor(out=cv[:, s, :], in0=gpad[:, s, 1:S + 1],
                                                 scalar=convT[:, l, bass.ds(c + FT, 1)], in1=cv[:, s, :],
                                                 op0=ALU.mult, op1=ALU.add).then_inc(tap1, 1)
                        dve.wait_ge(tap1, f + 1)
                        dve.scalar_tensor_tensor(out=cv[:, s, :], in0=gpad[:, s, 0:S],
                                                 scalar=convT[:, l, bass.ds(c, 1)], in1=cv[:, s, :],
                                                 op0=ALU.mult, op1=ALU.add).then_inc(tap0, 1)
                        dve.wait_ge(silu_scaled, f + 1)
                        dve.tensor_tensor(hid[:, s, :], ps[:, 2 * s + 1, :], act_o[:, s, :], ALU.mult)\
                            .then_inc(evacuated, 1)

                    first = 0
                    if n_half == 0:
                        up(0, 0, norm=True)
                        up(0, 1)
                        first = 2
                    with by_two(dve, first, n) as i:
                        up(i, 0)
                        up(i, 1)
                    u0, f0 = u0 + n, f0 + n

                    def down(j, s):
                        u = j + (u0 + s)
                        if not (isinstance(u, int) and u + 1 >= U_END):
                            weights_lo(u + 1, 1 - s)
                        add_x(j + s, 2 * s, u + 1)
                        if n_half == 1 and l == 0:
                            split_x(S_FFN[l] + 1, j + s)

                    if n_half == 0:
                        with by_two(dve, 0, KT) as j:
                            down(j, 0)
                            down(j, 1)
                    else:
                        for j in range(0, KT, 2):
                            down(j, 0)
                            down(j, 1)
                    u0 += KT

            head(0, first=True)
            with dve.Fori(1, HA) as h:
                head(h)
            out_proj(U_OUTA, 1)
            ffn(0)

            for m in range(4):
                weights_lo(U_V + m + 1, (m + 1) % 2)
                if m == 0:
                    norm_rstd(2)
                    dve.wait_ge(rcol_turned, 2)
                    dve.tensor_copy(rcol[:, :], ps[:, 4, 0:TB]).then_inc(rcol_made, 1)
                    dve.wait_ge(rcol_made, 2)
                dve.wait_ge(unit_done, U_V + m + 1)
                for b in range(TB):
                    dve.tensor_scalar(v_all[:, b, m * 2 * P:(m + 1) * 2 * P],
                                      ps[:, 2 * (m % 2) + b // 2, (b % 2) * 2 * P:(b % 2 + 1) * 2 * P],
                                      rcol[:, b:b + 1], None, ALU.mult).then_inc(evacuated, 1)

            def attn_qk(h):
                dve.wait_ge(unit_done, h + (U_QK + 1))
                dve.scalar_tensor_tensor(out=tqk[0], in0=ps[:, 0, :], scalar=HDB ** -0.5, in1=rstd[:, :],
                                         op0=ALU.mult, op1=ALU.mult).then_inc(evacuated, 1)
                dve.tensor_tensor(tqk[1], ps[:, 1, :], rstd[:, :], ALU.mult).then_inc(evacuated, 1)

            def attn_qk_lo(h):
                for n in range(2):
                    dve.wait_ge(dqk_hi_made, 2 * h + n + 1)
                    dve.tensor_tensor(qk_lo[n], tqk[n], f32(qk_hi[n]), ALU.subtract).then_inc(dqk_split, 1)

            def attn_max(h, i, first):
                for c in range(2):
                    dve.wait_ge(dscored, 8 * h + (2 * i + c + 1))
                    dve.tensor_reduce(nmax[:, i % 2, c:c + 1], ps[:, 2 + (i % 2) * 2 + c, 0:(i + 1) * P],
                                      AX.X, ALU.max, negate=True).then_inc(maxed, 1)

            def attn_mix(h, i):
                n = 4 * h + (i + 1)
                r = i % 2
                dve.wait_ge(exped, 8 * h + (2 * i + 2))
                dve.reciprocal(rsum[:, r, :], lsum[:, r, :]).then_inc(sum_inv, 1)
                dve.wait_ge(sum_inv, n)
                dve.tensor_tensor(rsum[:, r, :], rsum[:, r, :], coef[:, :], ALU.mult).then_inc(sum_coef, 1)
                dve.wait_ge(sum_coef, n)
                p0, p1 = (prob[:, r, c, 0:(i + 1) * P] for c in range(2))
                dve.tensor_scalar(p0, p0, rsum[:, r, 0:1], None, ALU.mult).then_inc(p0_scaled, 1)
                dve.wait_ge(p0_scaled, n)
                dve.scalar_tensor_tensor(out=p0, in0=p1, scalar=rsum[:, r, 1:2], in1=p0,
                                         op0=ALU.mult, op1=ALU.add).then_inc(a_made, 1)

            def attn_pT_lo(h, i):
                dve.wait_ge(pT_hi_made, 4 * h + (i + 1))
                dve.tensor_tensor(pT_lo[:, 0:i + 1, i * P:(i + 1) * P],
                                  ps[:, 6, 0:(i + 1) * P].rearrange("p (j c) -> p j c", c=P),
                                  f32(pT_hi[:, 0:i + 1, i * P:(i + 1) * P]), ALU.subtract).then_inc(pT_split, 1)

            def attn_finish(h, last=False):
                dve.wait_ge(o_rstd, h + 1)
                if last:
                    dve.wait_ge(o_split, h)
                else:
                    dve.wait_ge(vh_split, h + 2)
                dve.scalar_tensor_tensor(out=ytmp[:, :], in0=ps[:, 7, :], scalar=gainT[:, G_SUB:G_SUB + 1],
                                         in1=sqacc[:, :], op0=ALU.mult, op1=ALU.mult).then_inc(o_made, 1)

            def attn(h, s, prev=True, nxt=True, more=True):
                if more:
                    weights_lo(h + (U_QK + 2), s)
                attn_max(h, 0, not prev)
                attn_max(h, 1, not prev)
                attn_mix(h, 0)
                if prev:
                    attn_finish(h - 1)
                attn_max(h, 2, not prev)
                attn_mix(h, 1)
                attn_pT_lo(h, 0)
                attn_max(h, 3, not prev)
                attn_mix(h, 2)
                attn_pT_lo(h, 1)
                attn_mix(h, 3)
                attn_pT_lo(h, 2)
                if nxt:
                    attn_qk(h + 1)
                attn_pT_lo(h, 3)
                if nxt:
                    attn_qk_lo(h + 1)

            attn_qk(0)
            attn_qk_lo(0)
            weights_lo(U_QK + 1, 1)
            attn(0, 0, prev=False)
            with by_two(dve, 1, HB - 3) as h:
                attn(h, 1)
                attn(h + 1, 0)
            attn(HB - 3, 1)
            attn(HB - 2, 0)
            attn(HB - 1, 1, nxt=False, more=False)
            attn_finish(HB - 1, last=True)
            out_proj(U_OUTB, 3)
            ffn(1)

            dve.wait_ge(fin_std, 1)
            dve.reciprocal(rcol[:, :], rcol[:, :]).then_inc(fin_rstd, 1)
            dve.wait_ge(fin_rstd, 1)
            for b in range(TB):
                dve.wait_ge(fin_turned, 2 * b + 2)
                dve.tensor_scalar(o_sb[:, b, 512:1024], ps[:, 2 * b + 1, :], rcol[:, b:b + 1], None, ALU.mult)\
                    .then_inc(fin_scaled_v, 1)

        @block.tensor
        def _(pe):
            def mm3(o, w, m, start, stop):
                pe.matmul(o, w[0], m[0], start=start, stop=False)
                pe.matmul(o, w[0], m[1], start=False, stop=False)
                return pe.matmul(o, w[1], m[0], start=False, stop=stop)

            def xs(kt):
                return xs_hi[:, kt, :], xs_lo[:, kt, :]

            def hid_of(kt):
                return h_hi[:, kt, :], h_lo[:, kt, :]

            def wcol(s, t, c, kt, a, b):
                return cols(w_hi[:, s, :], t, c)[:, kt, a:b], cols(w_lo[:, s, :], t, c)[:, kt, a:b]

            def two_tiles(u, s, banks, moving, evac, ready=None, kts=range(KT)):
                if kts[0] == 0:
                    pe.wait_ge(w_split, u + 1)
                    if evac is not None:
                        pe.wait_ge(evacuated, evac)
                for kt in kts:
                    if ready is not None:
                        pe.wait_ge(ready[0], ready[1] + kt + 1)
                    for t, b in enumerate(banks):
                        last = mm3(ps[:, b, :], wcol(s, KT, 2 * P, kt, t * P, (t + 1) * P), moving(kt),
                                   kt == 0, kt == KT - 1)
                if kts[-1] == KT - 1:
                    last.then_inc(unit_done, 1)

            def one_tile(u, s, bank, moving, evac, n, ready=None):
                pe.wait_ge(w_split, u + 1)
                pe.wait_ge(evacuated, evac)
                for kt in range(n):
                    if ready is not None:
                        pe.wait_ge(ready[0], ready[1] + kt + 1)
                    last = mm3(ps[:, bank, :], wcol(s, n, P, kt, 0, P), moving(kt), kt == 0, kt == n - 1)
                last.then_inc(unit_done, 1)

            def token_major(u, s, evac, ready=None):
                pe.wait_ge(w_split, u + 1)
                if evac is not None:
                    pe.wait_ge(evacuated, evac)
                for b in range(TB):
                    for kt in range(KT):
                        if ready is not None and b == 0:
                            pe.wait_ge(ready[0], ready[1] + kt + 1)
                        st = tuple(a[:, b * P:(b + 1) * P] for a in xs(kt))
                        last = mm3(ps[:, 2 * s + b // 2, (b % 2) * 256:(b % 2 + 1) * 256], st,
                                   wcol(s, KT, 2 * P, kt, 0, 2 * P), kt == 0, kt == KT - 1)
                last.then_inc(unit_done, 1)

            def norm_sum(s):
                pe.wait_ge(sq_added, 8 * (s + 1))
                pe.matmul(ps[:, 7, :], onesf[:, :], sqacc[:, :], start=True, stop=True).then_inc(norm_summed, 1)

            def turn_rstd(s):
                pe.wait_ge(rstd_made, s + 1)
                for b in range(TB):
                    last = pe.matmul(ps[:, 4, b:b + 1], rstd[0:1, b * P:(b + 1) * P], onesf[0:1, 0:1],
                                     start=True, stop=True)
                last.then_inc(rcol_turned, 1)

            pe.wait_ge(const_made, 10)
            pe.wait_ge(rows_loaded, 16 * 14)
            pe.transpose(ps[:, 4, 0:57], gain_rows, ident[0:57, 0:57]).then_inc(rows_turned, 1)
            for l in range(2):
                pe.transpose(ps[:, 4, 64 + 96 * l:64 + 96 * l + 4 * FT], conv_rows[:, l, :],
                             ident[0:4 * FT, 0:4 * FT]).then_inc(rows_turned, 1)
            pe.wait_ge(x_loaded, 16 * TB)
            for j in range(KT):
                if j == 4:
                    pe.wait_ge(rows_kept, 3)
                for b in range(TB):
                    last = pe.transpose(ps[:, j, b * P:(b + 1) * P], x_in[:, b, j * P:(j + 1) * P], ident[:, :])
                last.then_inc(x_turned, 1)
            pe.wait_ge(lam_dve, 4)
            pe.wait_ge(x_kept, 8)
            pe.matmul(ps[:, 4, 32:33], onesf[0:1, :], lam_w[0:1, 7:8], start=True, stop=True)\
                .then_inc(lam_spread, 1)
            pe.wait_ge(wg_split, 1)
            for kt in range(KT):
                pe.wait_ge(x_split, kt + 1)
                last = mm3(ps[:, 5, :], (wg_hi[:, kt, :], wg_lo[:, kt, :]), xs(kt), kt == 0, kt == KT - 1)
            last.then_inc(gate_mm, 1)
            norm_sum(0)

            def head(h, first=False):
                u = 4 * h
                two_tiles(u, 0, (0, 1), xs, None if first else 8 * h - 1)
                if first:
                    turn_rstd(0)
                    pe.wait_ge(gate_scan, 2)
                    for b in range(TB):
                        last = pe.transpose(ps[:, 5, HA * b:HA * (b + 1)], g_a[0:HA, b * P:(b + 1) * P],
                                            ident[0:HA, 0:HA])
                    last.then_inc(a_turned, 1)
                pe.wait_ge(m_picked, h + 1)
                pe.matmul(ps[:, 7, :], onesf[0:HA, :], pw[0:HA, 0:S], start=True, stop=True)\
                    .then_inc(m_spread, 1)
                pe.matmul(ps[:, 6, :], onesf[0:HA, :], pw[0:HA, S:2 * S], start=True, stop=True)\
                    .then_inc(m_spread, 1)
                token_major(u + 1, 1, None if first else 8 * h)
                pe.wait_ge(qk_split, 2 * h + 2)
                pe.wait_ge(floor_kept, h + 1)
                if first:
                    pe.wait_ge(rcol_made, 1)
                    pe.wait_ge(acol_made, 1)
                else:
                    pe.wait_ge(y_made, 2 * h)
                for j in range(TB):
                    o = ps[:, 4 + j, 0:S - j * P] if j < 3 else ps[:, 6, 2 * P:3 * P]
                    mm3(o, (k_hi[:, j * P:(j + 1) * P], k_lo[:, j * P:(j + 1) * P]),
                        (q_hi[:, j * P:S], q_lo[:, j * P:S]), True, True).then_inc(scored, 1)
                one_tile(u + 2, 0, 0, xs, 8 * h + 2, KT)
                pe.wait_ge(evacuated, 8 * h + 6)
                pe.wait_ge(p_split, h + 1)
                for v in range(2):
                    for j in range(TB):
                        pj = tuple(a[:, OFF[j]:OFF[j] + S - j * P] for a in (p_hi, p_lo))
                        last = mm3(ps[:, 4 + v, j * P:S],
                                   (v_hi[:, j, v * P:(v + 1) * P], v_lo[:, j, v * P:(v + 1) * P]), pj,
                                   j == 0, j == TB - 1)
                    last.then_inc(pv_done, 1)
                for j in range(TB):
                    for n, a in enumerate((p_hi, p_lo)):
                        last = pe.matmul(ps[:, 6, j * P:S], ones_r[:, :], a[:, OFF[j]:OFF[j] + S - j * P],
                                         start=(j == 0 and n == 0), stop=(j == TB - 1 and n == 1))
                last.then_inc(pv_done, 1)
                one_tile(u + 3, 1, 2, xs, 8 * h + 6, KT)
                pe.wait_ge(num_added, h + 1)
                pe.wait_ge(arg_made, 4 * h + 4)
                pe.matmul(ps[:, 7, :], onesf[:, :], num0, start=True, stop=True).then_inc(head_summed, 1)

            def out_proj(u0, e0, ready):
                for m in range(KT // 2):
                    s = m % 2
                    evac = e0 if m < 2 else e0 + 2 * (m - 1)
                    two_tiles(u0 + m, s, (2 * s, 2 * s + 1), hid_of, evac, (ready, 0) if m == 0 else None)

            def ffn(l, e_in):
                u0, e0, f0 = U_FFN[l], E_FFN[l], l * FT
                for n_half, (k0, n) in enumerate(HALVES):
                    for s in range(2):
                        two_tiles(u0 + s, s, (2 * s, 2 * s + 1), xs, e_in[s],
                                  (x_split, 8 * S_FFN[l]) if n_half == 0 and s == 0 else None)
                        if n_half == 0 and s == 0:
                            norm_sum(S_FFN[l])
                    with by_two(pe, 2, n) as i:
                        for s in range(2):
                            two_tiles(i + (u0 + s), s, (2 * s, 2 * s + 1), xs, i + (e0 + s - 1))
                    e_in = (e0 + n - 1, e0 + n)
                    u0, e0 = u0 + n, e0 + n
                    for s in range(2):
                        one_tile(u0 + s, s, 2 * s, hid_of, e_in[s], n, (hid_split, f0 + k0) if s == 0 else None)
                    with by_two(pe, 2, KT) as j:
                        for s in range(2):
                            one_tile(j + (u0 + s), s, 2 * s, hid_of, j + (e0 + s - 1), n)
                    e_in = (e0 + KT - 1, e0 + KT)
                    u0, e0 = u0 + KT, e0 + KT

            head(0, first=True)
            with pe.Fori(1, HA) as h:
                head(h)
            out_proj(U_OUTA, E_OUTA, y_split)
            ffn(0, (E_OUTA + 6, E_OUTA + 8))

            for m in range(4):
                token_major(U_V + m, m % 2, E_V - 1 if m == 0 else E_V if m == 1 else E_V + 4 * (m - 1),
                            (x_split, 16) if m == 0 else None)
                if m == 0:
                    norm_sum(2)
                    turn_rstd(2)

            def attn_scores(h, i, first):
                for c in range(2):
                    if not (first and i < 2):
                        pe.wait_ge(exped, 8 * h + (2 * i + c - 3))
                    o = ps[:, 2 + (i % 2) * 2 + c, 0:(i + 1) * P]
                    r = slice(c * HDB, (c + 1) * HDB)
                    q = tuple(a[r, i * P:(i + 1) * P] for a in (q_hi, q_lo))
                    k = tuple(a[r, 0:(i + 1) * P] for a in (k_hi, k_lo))
                    pe.matmul(o, q[0], k[0], start=True, stop=False)
                    pe.matmul(ps[:, 2 + (i % 2) * 2 + c, i * P:(i + 1) * P], ident_b[:, :], mask_b[:, :],
                              start=False, stop=False)
                    pe.matmul(o, q[0], k[1], start=False, stop=False)
                    pe.matmul(o, q[1], k[0], start=False, stop=True).then_inc(dscored, 1)

            def attn_turn(h, i, first):
                pe.wait_ge(a_made, 4 * h + (i + 1))
                if not (first and i == 0):
                    pe.wait_ge(pT_split, 4 * h + i)
                for j in range(i + 1):
                    last = pe.transpose(ps[:, 6, j * P:(j + 1) * P], prob[:, i % 2, 0, j * P:(j + 1) * P],
                                        ident[:, :])
                last.then_inc(pT_turned, 1)

            def attn_sum(h):
                pe.wait_ge(o_sq, h + 1)
                pe.wait_ge(pT_split, 4 * h + 4)
                pe.matmul(ps[:, 6, :], onesf[:, :], sq[:, 0, :], start=True, stop=True).then_inc(o_summed, 1)

            def attn(h, s, prev=True, nxt=True):
                def project(part):
                    if nxt:
                        two_tiles(h + (U_QK + 1), s, (0, 1), xs, 2 * h + (E_QK + 2),
                                  kts=range(2 * part, 2 * part + 2))

                pe.wait_ge(dqk_split, 2 * h + 2)
                attn_scores(h, 0, not prev)
                attn_scores(h, 1, not prev)
                if prev:
                    attn_sum(h - 1)
                project(0)
                attn_scores(h, 2, not prev)
                if prev:
                    pe.wait_ge(o_ln, h)
                attn_turn(h, 0, not prev)
                project(1)
                attn_scores(h, 3, not prev)
                attn_turn(h, 1, not prev)
                project(2)
                attn_turn(h, 2, not prev)
                project(3)
                attn_turn(h, 3, not prev)
                pe.wait_ge(pT_split, 4 * h + 4)
                pe.wait_ge(vh_split, h + 1)
                if prev:
                    pe.wait_ge(o_made, h)
                for j in range(TB):
                    last = mm3(ps[:, 7, j * P:S], (vh_hi[:, j, :], vh_lo[:, j, :]),
                               (pT_hi[:, j, j * P:S], pT_lo[:, j, j * P:S]), j == 0, j == TB - 1)
                last.then_inc(dpv_done, 1)

            two_tiles(U_QK, 0, (0, 1), xs, E_QK)
            attn(0, 1, prev=False)
            with by_two(pe, 1, HB - 1) as h:
                attn(h, 0)
                attn(h + 1, 1)
            attn(HB - 1, 0, nxt=False)
            attn_sum(HB - 1)
            out_proj(U_OUTB, E_OUTB, o_split)
            ffn(1, (E_OUTB + 6, E_OUTB + 8))

            pe.wait_ge(sq_added, 8 * 5)
            for b in range(TB):
                last = pe.matmul(ps[:, 7, b:b + 1], sqacc[:, b * P:(b + 1) * P], onesf[:, 0:1],
                                 start=True, stop=True)
            last.then_inc(fin_summed, 1)
            pe.wait_ge(xs_hi_made, 8 * 5)
            pe.wait_ge(evacuated, E_FFN1 + n_ffn)
            for b in range(TB):
                for a in range(2):
                    if 2 * b + a == 7:
                        pe.wait_ge(fin_std, 1)
                    for t in range(4):
                        last = pe.transpose(ps[:, 2 * b + a, t * P:(t + 1) * P],
                                            xg_fin[:, 4 * a + t, b * P:(b + 1) * P], ident[:, :])
                    last.then_inc(fin_turned, 1)


_INS = ['x', 'attn_norm_g', 'ffn_norm_g', 'mlstm_w_in', 'mlstm_b_gate', 'mlstm_head_g', 'mlstm_w_out',
        'kv_norm_g', 'w_kv', 'diff_w_q', 'diff_lambda_q1', 'diff_lambda_k1', 'diff_lambda_q2',
        'diff_lambda_k2', 'diff_subln_g', 'diff_w_out', 'ffn_w_up', 'ffn_conv_w', 'ffn_conv_b',
        'ffn_w_down', 'final_norm_g']
_OUTS = [((1, 512, 1024), 'float32')]


def kernel(**inputs):
    import numpy as _np
    import concourse.bacc as _bacc
    from concourse import mybir as _mybir
    from concourse.bass_utils import run_bass_kernel_spmd as _run

    nc = _bacc.Bacc("TRN2", target_bir_lowering=False, num_devices=1)
    arrays, args = {}, []
    for name in _INS:
        a = _np.ascontiguousarray(inputs[name])
        arrays[f"in_{name}_dram"] = a
        args.append(nc.dram_tensor(f"in_{name}_dram", a.shape, _mybir.dt.from_np(a.dtype), kind="ExternalInput").ap())
    for i, (shape, dtype) in enumerate(_OUTS):
        dt = _mybir.dt.from_np(_np.dtype(dtype))
        args.append(nc.dram_tensor(f"out_{i}_dram", shape, dt, kind="ExternalOutput").ap())
    build_trunk(nc, *args)
    r = _run(nc, [arrays], core_ids=[0])
    got = tuple(r.results[0][f"out_{i}_dram"] for i in range(len(_OUTS)))
    return got[0]
```

```python
import math
from contextlib import ExitStack, contextmanager

import concourse.bass as bass
from concourse import mybir

F32 = mybir.dt.float32
F32R = mybir.dt.float32r
BF16 = mybir.dt.bfloat16
ALU = mybir.AluOpType
ACT = mybir.ActivationFunctionType
AX = mybir.AxisListType

P = 128
SLOT = 2048
EPS = 1e-6
SOFTCAP = 15.0
MASKED = -1e30
LAM_INIT = 0.8 - 0.6 * math.exp(-0.3 * 1)


@contextmanager
def by_two(engine, start, stop):
    with engine.Fori(0, (stop - start) // 2) as pair:
        yield pair * 2 + start


def build_trunk(nc, x, attn_norm_g, ffn_norm_g, mlstm_w_in, mlstm_b_gate, mlstm_head_g, mlstm_w_out,
                kv_norm_g, w_kv, diff_w_q, diff_lambda_q1, diff_lambda_k1, diff_lambda_q2,
                diff_lambda_k2, diff_subln_g, diff_w_out, ffn_w_up, ffn_conv_w, ffn_conv_b,
                ffn_w_down, final_norm_g, out):
    S, D = x.shape[1], x.shape[2]
    KT = D // P
    TB = S // P
    HA = mlstm_head_g.shape[1]
    DVA = mlstm_head_g.shape[2]
    DKA = P
    HB = D // P
    HDB = P // 2
    DFF = ffn_conv_b.shape[1]
    FT = DFF // P
    assert (S, D, HA, DVA, FT) == (512, 1024, 4, 256, 22)
    HALVES = ((0, 12), (12, 10))
    HT = 12

    U_HEAD, E_HEAD = 0, 0
    U_OUTA, E_OUTA = 4 * HA, 8 * HA
    U_FFN0, E_FFN0 = U_OUTA + KT // 2, E_OUTA + KT
    n_ffn = FT + 2 * KT
    U_V, E_V = U_FFN0 + n_ffn, E_FFN0 + n_ffn
    U_QK, E_QK = U_V + 4, E_V + 4 * TB
    U_OUTB, E_OUTB = U_QK + HB, E_QK + 2 * HB
    U_FFN1, E_FFN1 = U_OUTB + KT // 2, E_OUTB + KT
    U_END = U_FFN1 + n_ffn
    U_FFN, E_FFN = (U_FFN0, U_FFN1), (E_FFN0, E_FFN1)
    S_FFN = (1, 3)
    G_STAGE = {0: 0, 1: 16, 3: 24, 4: 40}
    G_Q, G_KV, G_HEAD, G_SUB = 8, 32, 48, 56

    es = ExitStack()
    with es:
        def sb(name, shape, dt):
            return es.enter_context(nc.sbuf_tensor(name, shape, dt))

        def sem(name):
            return es.enter_context(nc.semaphore(name))

        ps = es.enter_context(nc.psum_tensor("ps", [P, 8, 512], F32))

        xT = sb("xT", [P, KT, S], F32)
        xs_hi = sb("xs_hi", [P, KT, S], F32R)
        xs_lo = sb("xs_lo", [P, KT, S], F32R)
        wraw = sb("wraw", [P, 2, SLOT], F32)
        w_hi = sb("w_hi", [P, 2, SLOT], F32R)
        w_lo = sb("w_lo", [P, 2, SLOT], F32R)
        h_hi = sb("h_hi", [P, HT, S], F32R)
        h_lo = sb("h_lo", [P, HT, S], F32R)
        mixR = sb("mixR", [P, 8 * S], F32R)
        mixF = sb("mixF", [P, 14 * S], F32)
        rowsM = sb("rowsM", [HA, 2 * S], F32)
        rstd = sb("rstd", [P, S], F32)
        sqacc = sb("sqacc", [P, S], F32)
        sq = sb("sq", [P, 2, S], F32)
        ytmp = sb("ytmp", [P, S], F32)
        ident = sb("ident", [P, P], F32)
        onesf = sb("onesf", [P, P], F32)
        ones_r = sb("ones_r", [P, P], F32R)
        tri = sb("tri", [P, P], F32)
        ident_b = sb("ident_b", [P, P], BF16)
        mask_b = sb("mask_b", [P, P], BF16)
        gainT = sb("gainT", [P, 57], F32)
        convT = sb("convT", [P, 2, 4 * FT], F32)
        acol = sb("acol", [P, 4 * HA], F32)
        rcol = sb("rcol", [P, TB], F32)
        eps = sb("eps", [P, 1], F32)
        bgate = sb("bgate", [P, 2], F32)
        lam_in = sb("lam_in", [1, 4, HDB], F32)
        lam_w = sb("lam_w", [1, 8], F32)
        coef = sb("coef", [P, 2], F32)
        nmax = sb("nmax", [P, 2, 2], F32)
        lsum = sb("lsum", [P, 2, 2], F32)
        rsum = sb("rsum", [P, 2, 2], F32)

        def f32(ap):
            return ap.bitcast(F32)

        x_in = mixF[:, 0:4096].rearrange("p (b c) -> p b c", b=TB)
        gain_rows = mixF[0:57, 4096:4224]
        conv_rows = mixF[0:4 * FT, 4224:4480].rearrange("p (l c) -> p l c", l=2)
        wg_raw = mixF[:, 4608:5632].rearrange("p (t c) -> p t c", t=KT)
        wg_hi = h_hi[:, 8:10, :].rearrange("p a b -> p (a b)").rearrange("p (t c) -> p t c", t=KT)
        wg_lo = h_lo[:, 8:10, :].rearrange("p a b -> p (a b)").rearrange("p (t c) -> p t c", t=KT)
        g_z, g_t, g_e, g_L, g_a, g_M = (mixF[0:36, k * S:(k + 1) * S] for k in range(6))

        OFF = [j * S - P * (j * (j - 1) // 2) for j in range(TB)]
        PTRI = OFF[-1] + P
        q_hi, q_lo, k_hi, k_lo = (mixR[:, n * S:(n + 1) * S] for n in range(4))
        v_hi = mixR[:, 4 * S:6 * S].rearrange("p (b c) -> p b c", b=TB)
        v_lo = mixR[:, 6 * S:8 * S].rearrange("p (b c) -> p b c", b=TB)
        p_hi = h_hi[:, 8:11, :].rearrange("p a b -> p (a b)")[:, 0:PTRI]
        p_lo = h_lo[:, 8:11, :].rearrange("p a b -> p (a b)")[:, 0:PTRI]
        decay = mixF[:, 0:PTRI]
        pw = mixF[:, PTRI:2 * PTRI]
        tq, tk, floor, den, num0, num1, var, gate0, gate1 = (
            mixF[:, 2 * PTRI + n * S:2 * PTRI + (n + 1) * S] for n in range(9))
        numsq, gates = (num0, num1), (gate0, gate1)

        v_all = mixF[:, 0:4096].rearrange("p (b c) -> p b c", b=TB)
        prob = mixF[:, 4096:6144].rearrange("p (a c s) -> p a c s", a=2, c=2)
        tqk = (mixF[:, 6144:6656], mixF[:, 6656:7168])
        qk_hi = (q_hi, k_hi)
        qk_lo = (q_lo, k_lo)
        vh_hi = mixR[:, 4 * S:5 * S].rearrange("p (b c) -> p b c", b=TB)
        vh_lo = mixR[:, 5 * S:6 * S].rearrange("p (b c) -> p b c", b=TB)
        pT_hi = h_hi[:, 8:12, :]
        pT_lo = h_lo[:, 8:12, :]

        gpad = mixF[:, 0:2 * (S + 2)].rearrange("p (a s) -> p a s", a=2)
        FB = 2 * (S + 2)
        cv, act_o, hid = (mixF[:, FB + n * 2 * S:FB + (n + 1) * 2 * S]
                          .rearrange("p (a s) -> p a s", a=2) for n in range(3))
        xg_fin = mixF[:, 0:KT * S].rearrange("p (t s) -> p t s", t=KT)
        o_sb = wraw[:, :, :].rearrange("p a (b c) -> p (a b) c", b=2)

        x_loaded = sem("x_loaded")
        rows_loaded = sem("rows_loaded")
        wg_loaded = sem("wg_loaded")
        const_made = sem("const_made")
        bg_zeroed = sem("bg_zeroed")
        wg_zeroed = sem("wg_zeroed")
        ones_r_made = sem("ones_r_made")
        rows_turned = sem("rows_turned")
        rows_kept = sem("rows_kept")
        x_turned = sem("x_turned")
        x_kept = sem("x_kept")
        wg_hi_made = sem("wg_hi_made")
        wg_split = sem("wg_split")
        bg_scaled = sem("bg_scaled")
        lam_dve = sem("lam_dve")
        lam_exp = sem("lam_exp")
        lam_spread = sem("lam_spread")
        lam_kept = sem("lam_kept")
        sub_scaled = sem("sub_scaled")
        gate_mm = sem("gate_mm")
        gate_z = sem("gate_z")
        gate_act = sem("gate_act")
        gate_scan = sem("gate_scan")
        rows_made = sem("rows_made")
        a_turned = sem("a_turned")
        acol_made = sem("acol_made")

        slot_loaded = [sem("slot0_loaded"), sem("slot1_loaded")]
        w_scaled = sem("w_scaled")
        w_hi_made = sem("w_hi_made")
        w_split = sem("w_split")
        unit_done = sem("unit_done")
        evacuated = sem("evacuated")

        xs_hi_made = sem("xs_hi_made")
        x_split = sem("x_split")
        sq_made = sem("sq_made")
        sq_added = sem("sq_added")
        norm_summed = sem("norm_summed")
        std_made = sem("std_made")
        rstd_made = sem("rstd_made")
        rcol_turned = sem("rcol_turned")
        rcol_made = sem("rcol_made")

        m_picked = sem("m_picked")
        m_spread = sem("m_spread")
        floor_kept = sem("floor_kept")
        qk_hi_made = sem("qk_hi_made")
        qk_split = sem("qk_split")
        arg_made = sem("arg_made")
        decay_made = sem("decay_made")
        decay_masked = sem("decay_masked")
        v_hi_made = sem("v_hi_made")
        scored = sem("scored")
        p_made = sem("p_made")
        p_hi_made = sem("p_hi_made")
        p_split = sem("p_split")
        pv_done = sem("pv_done")
        gate_open = sem("gate_open")
        den_made = sem("den_made")
        den_sq = sem("den_sq")
        num_sq = sem("num_sq")
        num_added = sem("num_added")
        head_summed = sem("head_summed")
        var_made = sem("var_made")
        head_std = sem("head_std")
        head_rstd = sem("head_rstd")
        gate_scaled = sem("gate_scaled")
        y_made = sem("y_made")
        y_hi_made = sem("y_hi_made")
        y_split = sem("y_split")

        pads_zeroed = sem("pads_zeroed")
        g_made = sem("g_made")
        tap2 = sem("tap2")
        tap1 = sem("tap1")
        tap0 = sem("tap0")
        silu_made = sem("silu_made")
        silu_scaled = sem("silu_scaled")
        hid_hi_made = sem("hid_hi_made")
        hid_split = sem("hid_split")

        q_done = sem("q_done")
        dscored = sem("dscored")
        maxed = sem("maxed")
        exped = sem("exped")
        sum_inv = sem("sum_inv")
        sum_coef = sem("sum_coef")
        p0_scaled = sem("p0_scaled")
        a_made = sem("a_made")
        pT_turned = sem("pT_turned")
        pT_hi_made = sem("pT_hi_made")
        pT_split = sem("pT_split")
        vh_hi_made = sem("vh_hi_made")
        vh_split = sem("vh_split")
        dqk_hi_made = sem("dqk_hi_made")
        dqk_split = sem("dqk_split")
        dpv_done = sem("dpv_done")
        o_sq = sem("o_sq")
        o_summed = sem("o_summed")
        o_ln = sem("o_ln")
        o_rstd = sem("o_rstd")
        o_made = sem("o_made")
        o_hi_made = sem("o_hi_made")
        o_split = sem("o_split")

        fin_summed = sem("fin_summed")
        fin_std = sem("fin_std")
        fin_rstd = sem("fin_rstd")
        fin_turned = sem("fin_turned")
        fin_scaled_a = sem("fin_scaled_a")
        fin_scaled_v = sem("fin_scaled_v")
        out_stored = sem("out_stored")

        block = es.enter_context(nc.Block())

        w_in = mlstm_w_in[0].rearrange("(t p) n -> p t n", p=P)
        w_outA = mlstm_w_out[0].rearrange("(t p) n -> p t n", p=P)
        w_kvr = w_kv.rearrange("(t p) n -> p t n", p=P)
        w_q = diff_w_q[0].rearrange("(t p) n -> p t n", p=P)
        w_outB = diff_w_out[0].rearrange("(t p) n -> p t n", p=P)
        w_up = [ffn_w_up[l].rearrange("(t p) n -> p t n", p=P) for l in range(2)]
        w_down = [ffn_w_down[l].rearrange("(t p) n -> p t n", p=P) for l in range(2)]

        def cols(w, t, c):
            return w[:, 0:t * c].rearrange("p (t c) -> p t c", t=t)

        @block.sync
        def _(sp):
            def free_slot(u, peeled=False):
                if not peeled:
                    sp.wait_ge(w_split, u - 1)

            def load_pair(u, s, left, right, peeled=False):
                free_slot(u, peeled)
                d = cols(wraw[:, s, :], KT, 2 * P)
                sp.dma_start(d[:, :, 0:P], left).then_inc(slot_loaded[s], 16)
                sp.dma_start(d[:, :, P:2 * P], right).then_inc(slot_loaded[s], 16)

            def load_block(u, s, src, peeled=False):
                free_slot(u, peeled)
                t, c = src.shape[1], src.shape[2]
                d = cols(wraw[:, s, :], t, c)
                sp.dma_start(d[:, 0:t // 2, :], src[:, 0:t // 2, :]).then_inc(slot_loaded[s], 16)
                sp.dma_start(d[:, t // 2:t, :], src[:, t // 2:t, :]).then_inc(slot_loaded[s], 16)

            def load_head(h, first=False):
                u = 4 * h
                load_pair(u, 0, w_in[:, :, bass.ds(h * DKA, P)],
                          w_in[:, :, bass.ds(h * DKA + HA * DKA, P)], first)
                load_block(u + 1, 1, w_in[:, :, bass.ds(h * DVA + 2 * HA * DKA, DVA)], first)
                for v in range(2):
                    load_block(u + 2 + v, v, w_in[:, :, bass.ds(h * DVA + 2 * HA * DKA + HA * DVA + v * P, P)])

            def load_ffn(l):
                u0 = U_FFN[l]
                for k0, n in HALVES:
                    with by_two(sp, 0, n) as i:
                        for s in range(2):
                            load_pair(i + (u0 + s), s, w_up[l][:, :, bass.ds((i + (k0 + s)) * P, P)],
                                      w_up[l][:, :, bass.ds((i + (k0 + s)) * P + DFF, P)])
                    u0 += n
                    with by_two(sp, 0, KT) as j:
                        for s in range(2):
                            load_block(j + (u0 + s), s, w_down[l][:, k0:k0 + n, bass.ds((j + s) * P, P)])
                    u0 += KT

            xr = x[0].rearrange("(b p) d -> p b d", p=P)
            for b in range(TB):
                sp.dma_start(x_in[:, b, :], xr[:, b, :]).then_inc(x_loaded, 16)
            load_head(0, first=True)
            with sp.Fori(1, HA) as h:
                load_head(h)
            for m in range(KT // 2):
                load_block(U_OUTA + m, m % 2, w_outA[:, :, m * 2 * P:(m + 1) * 2 * P])
            load_ffn(0)
            for m in range(4):
                load_block(U_V + m, m % 2, w_kvr[:, :, D + m * 2 * P:D + (m + 1) * 2 * P])
            with by_two(sp, 0, HB) as h:
                for s in range(2):
                    load_pair(h + (U_QK + s), s, w_q[:, :, bass.ds((h + s) * P, P)],
                              w_kvr[:, :, bass.ds((h + s) * P, P)])
            for m in range(KT // 2):
                load_block(U_OUTB + m, m % 2, w_outB[:, :, m * 2 * P:(m + 1) * 2 * P])
            load_ffn(1)
            outr = out[0].rearrange("(b p) (a d) -> b a p d", p=P, a=2)
            for b in range(TB):
                for a in range(2):
                    sp.wait_ge(fin_scaled_v if a else fin_scaled_a, b + 1)
                    sp.dma_start(outr[b, a], o_sb[:, b, a * 512:(a + 1) * 512]).then_inc(out_stored, 16)
            sp.wait_ge(out_stored, 16 * 2 * TB)

        @block.gpsimd
        def _(pool):
            pool.memset(ident[:, :], 0.0).then_inc(const_made, 1)
            pool.memset(onesf[:, :], 1.0).then_inc(const_made, 1)
            pool.memset(ident_b[:, :], 0.0).then_inc(const_made, 1)
            pool.memset(mask_b[:, :], 0.0).then_inc(const_made, 1)
            pool.memset(eps[:, :], EPS).then_inc(const_made, 1)
            pool.memset(coef[:, :], 1.0).then_inc(const_made, 1)
            pool.memset(bgate[:, :], 0.0).then_inc(bg_zeroed, 1)
            pool.memset(mixF[:, 4608:5632], 0.0).then_inc(wg_zeroed, 1)
            pool.wait_ge(const_made, 6)
            pool.affine_select(out=ident[:, :], in_=ident[:, :], compare_op=ALU.not_equal, fill=1.0,
                               base=0, pattern=[[-1, P]], channel_multiplier=1).then_inc(const_made, 1)
            pool.affine_select(out=ident_b[:, :], in_=ident_b[:, :], compare_op=ALU.not_equal, fill=1.0,
                               base=0, pattern=[[-1, P]], channel_multiplier=1).then_inc(const_made, 1)
            pool.affine_select(out=mask_b[:, :], in_=mask_b[:, :], compare_op=ALU.is_ge, fill=MASKED,
                               base=0, pattern=[[-1, P]], channel_multiplier=1).then_inc(const_made, 1)
            pool.affine_select(out=tri[:, :], in_=onesf[:, :], compare_op=ALU.is_ge, fill=0.0,
                               base=0, pattern=[[1, P]], channel_multiplier=-1).then_inc(const_made, 1)

            def add_squares(s, j):
                n = 8 * s + j
                pool.wait_ge(sq_made, n + 1)
                if j == 0:
                    if s:
                        pool.wait_ge(norm_summed, s)
                    pool.tensor_copy(sqacc[:, :], sq[:, 0, :]).then_inc(sq_added, 1)
                else:
                    pool.wait_ge(sq_added, n)
                    pool.tensor_tensor(sqacc[:, :], sqacc[:, :], sq[:, j % 2, :], ALU.add)\
                        .then_inc(sq_added, 1)

            def head(h, first=False):
                pool.wait_ge(decay_made, h + 1)
                for j in range(TB):
                    d = decay[:, OFF[j]:OFF[j] + P]
                    pool.tensor_tensor(d, d, tri[:, :], ALU.mult).then_inc(decay_masked, 1)
                pool.wait_ge(num_sq, 2 * h + 2)
                pool.tensor_tensor(num0, num0, num1, ALU.add).then_inc(num_added, 1)
                pool.wait_ge(gate_open, 2 * h + 2)
                pool.wait_ge(head_rstd, h + 1)
                for v in range(2):
                    pool.tensor_tensor(gates[v], gates[v], den, ALU.mult).then_inc(gate_scaled, 1)
                for v in range(2):
                    pool.wait_ge(y_hi_made, 2 * h + v + 1)
                    t = h * 2 + v
                    pool.tensor_tensor(h_lo[:, t, :], numsq[v], f32(h_hi[:, t, :]), ALU.subtract)\
                        .then_inc(y_split, 1)

            def ffn_up(i, f0, s):
                f = i + (f0 + s)
                pool.wait_ge(silu_made, f + 1)
                pool.tensor_tensor(act_o[:, s, :], act_o[:, s, :], rstd[:, :], ALU.mult)\
                    .then_inc(silu_scaled, 1)
                pool.wait_ge(hid_hi_made, f + 1)
                pool.tensor_tensor(h_lo[:, i + s, :], hid[:, s, :], f32(h_hi[:, i + s, :]), ALU.subtract)\
                    .then_inc(hid_split, 1)

            def scale_unit(u, s, gl, gr):
                pool.wait_ge(slot_loaded[s], (u - s) * 16 + 32)
                d = cols(wraw[:, s, :], KT, 2 * P)
                for side, g in enumerate((gl, gr)):
                    half = d[:, :, side * P:(side + 1) * P]
                    pool.tensor_tensor(half, half, gainT[:, g:g + KT].unsqueeze(2).broadcast_to([P, KT, P]),
                                       ALU.mult).then_inc(w_scaled, 1)

            def ffn(l):
                for n_half, (k0, n) in enumerate(HALVES):
                    with by_two(pool, 0, n) as i:
                        for s in range(2):
                            ffn_up(i, l * FT + k0, s)
                for j in range(KT):
                    if l == 0 and j >= KT - 2:
                        scale_unit(U_V + j - (KT - 2), j % 2, G_KV, G_KV)
                    add_squares(S_FFN[l] + 1, j)

            for j in range(KT):
                add_squares(0, j)
            head(0, first=True)
            with pool.Fori(1, HA) as h:
                head(h)
            for j in range(KT):
                add_squares(1, j)
            ffn(0)
            for m in range(2, 4):
                scale_unit(U_V + m, m % 2, G_KV, G_KV)

            def attn_o_lo(h):
                pool.wait_ge(o_hi_made, h + 1)
                pool.tensor_tensor(h_lo[:, h, :], ytmp[:, :], f32(h_hi[:, h, :]), ALU.subtract)\
                    .then_inc(o_split, 1)

            def vh_lo_made(h):
                pool.wait_ge(vh_hi_made, h + 1)
                pool.tensor_tensor(vh_lo, v_all[:, :, bass.ds(h * P, P)], f32(vh_hi), ALU.subtract)\
                    .then_inc(vh_split, 1)

            scale_unit(U_QK, 0, G_Q, G_KV)
            scale_unit(U_QK + 1, 1, G_Q, G_KV)
            vh_lo_made(0)

            def attn(h, s, scale=True, nxt=True, prev=True):
                if scale:
                    scale_unit(h + (U_QK + 2), s, G_Q, G_KV)
                if prev:
                    attn_o_lo(h - 1)
                if nxt:
                    vh_lo_made(h + 1)

            attn(0, 0, prev=False)
            with by_two(pool, 1, HB - 3) as h:
                attn(h, 1)
                attn(h + 1, 0)
            attn(HB - 3, 1)
            attn(HB - 2, 0, scale=False)
            attn(HB - 1, 1, scale=False, nxt=False)
            attn_o_lo(HB - 1)
            for j in range(KT):
                add_squares(3, j)
            ffn(1)

        @block.scalar
        def _(act):
            n = 0
            for src in (attn_norm_g.rearrange("l (t p) -> (l t) p", p=P),
                        ffn_norm_g.rearrange("l (t p) -> (l t) p", p=P),
                        kv_norm_g.rearrange("(t p) -> t p", p=P),
                        final_norm_g.rearrange("(t p) -> t p", p=P),
                        mlstm_head_g[0].rearrange("h (t p) -> (h t) p", p=P),
                        diff_subln_g):
                act.dma_start(gain_rows[n:n + src.shape[0], :], src).then_inc(rows_loaded, 16)
                n += src.shape[0]
            for l in range(2):
                act.dma_start(conv_rows[0:3 * FT, l, :],
                              ffn_conv_w[l].rearrange("w (t p) -> (w t) p", p=P)).then_inc(rows_loaded, 16)
                act.dma_start(conv_rows[3 * FT:4 * FT, l, :],
                              ffn_conv_b[l].rearrange("(t p) -> t p", p=P)).then_inc(rows_loaded, 16)
            for n, src in enumerate((diff_lambda_q1, diff_lambda_k1, diff_lambda_q2, diff_lambda_k2)):
                act.dma_start(lam_in[0:1, n, :], src).then_inc(rows_loaded, 16)
            ROWS = 16 * 14
            act.wait_ge(bg_zeroed, 1)
            act.wait_ge(wg_zeroed, 1)
            wg = w_in[:, :, 2 * HA * (DKA + DVA):]
            bg = mlstm_b_gate.rearrange("a n -> n a")
            for r, c in ((0, 0), (32, HA)):
                act.dma_start(wg_raw[:, :, r:r + HA], wg[:, :, c:c + HA]).then_inc(wg_loaded, 16)
                act.dma_start(bgate[r:r + HA, 0:1], bg[c:c + HA, :]).then_inc(wg_loaded, 16)

            def weights_hi(u, s, scaled=None):
                if scaled is None:
                    act.wait_ge(slot_loaded[s], (u - s) * 16 + 32)
                else:
                    act.wait_ge(w_scaled, scaled)
                if not isinstance(u, int) or u >= 2:
                    act.wait_ge(unit_done, u - 1)
                act.activation(w_hi[:, s, :], wraw[:, s, :], ACT.Copy).then_inc(w_hi_made, 1)

            def split_x(s, j):
                n = 8 * s + j
                if s == 0:
                    act.wait_ge(x_kept, j + 1)
                g = G_STAGE.get(s)
                dst = xg_fin if s == 4 else xs_hi
                act.activation(dst[:, j, :], xT[:, j, :], ACT.Copy,
                               scale=1.0 if g is None else gainT[:, g + j:g + j + 1]).then_inc(xs_hi_made, 1)
                if n >= 2:
                    act.wait_ge(sq_added, n - 1)
                act.activation(sq[:, j % 2, :], xT[:, j, :], ACT.Square).then_inc(sq_made, 1)

            def norm_std(s):
                act.wait_ge(norm_summed, s + 1)
                act.activation(sq[:, 0, :], ps[:, 7, :], ACT.Sqrt, scale=1.0 / D, bias=eps[:, :])\
                    .then_inc(std_made, 1)

            act.wait_ge(rows_loaded, ROWS)
            act.wait_ge(lam_dve, 2)
            act.activation(lam_w[:, 4:6], lam_w[:, 2:4], ACT.Exp).then_inc(lam_exp, 1)
            act.wait_ge(const_made, 10)
            act.activation(ones_r[:, :], onesf[:, :], ACT.Copy).then_inc(ones_r_made, 1)
            act.wait_ge(wg_loaded, 64)
            act.activation(wg_hi, wg_raw, ACT.Copy).then_inc(wg_hi_made, 1)
            act.mul(bgate[:, 1:2], bgate[:, 0:1], 1.0 / SOFTCAP).then_inc(bg_scaled, 1)
            act.wait_ge(rows_kept, 3)
            split_x(0, 0)
            split_x(0, 1)
            weights_hi(0, 0)
            for j in range(2, KT):
                split_x(0, j)
            weights_hi(1, 1)
            norm_std(0)
            act.wait_ge(gate_z, 1)
            act.wait_ge(bg_scaled, 1)
            act.activation(g_t, g_z, ACT.Tanh, scale=1.0 / SOFTCAP, bias=bgate[0:36, 1:2])\
                .then_inc(gate_act, 1)
            act.wait_ge(gate_act, 1)
            act.activation(g_e[32:36, :], g_t[32:36, :], ACT.Exp, scale=-SOFTCAP).then_inc(gate_act, 1)
            act.wait_ge(gate_act, 2)
            act.activation(g_e[32:36, :], g_e[32:36, :], ACT.Ln, bias=1.0).then_inc(gate_act, 1)
            act.wait_ge(gate_scan, 4)
            act.activation(rowsM[:, S:2 * S], g_z[0:HA, :], ACT.Exp).then_inc(rows_made, 1)

            def head(h, first=False):
                u = 4 * h
                for n, t in enumerate((tq, tk)):
                    act.wait_ge(evacuated, 8 * h + 1 + n)
                    act.activation(qk_hi[n], t, ACT.Copy).then_inc(qk_hi_made, 1)
                act.wait_ge(arg_made, 4 * h + 4)
                act.activation(decay, decay, ACT.Exp).then_inc(decay_made, 1)
                act.wait_ge(m_spread, 2 * h + 2)
                act.activation(floor, ps[:, 6, :], ACT.Square, scale=math.sqrt(EPS)).then_inc(floor_kept, 1)
                weights_hi(u + 2, 0)
                act.wait_ge(p_made, 4 * h + 4)
                act.activation(p_hi, pw, ACT.Copy).then_inc(p_hi_made, 1)
                act.wait_ge(unit_done, u + 2)
                act.wait_ge(rcol_made, 1)
                for b in range(TB):
                    act.activation(v_hi[:, b, :], ps[:, 2 + b // 2, (b % 2) * DVA:(b % 2 + 1) * DVA], ACT.Copy,
                                   scale=rcol[:, b:b + 1]).then_inc(v_hi_made, 1)
                weights_hi(u + 3, 1)
                act.wait_ge(evacuated, 8 * h + 7)
                act.activation(gate0, gate0, ACT.Sigmoid).then_inc(gate_open, 1)
                weights_hi(u + 4, 0)
                if not first:
                    act.wait_ge(y_split, 2 * h)
                for v in range(2):
                    act.wait_ge(pv_done, 3 * h + v + 1)
                    act.activation(numsq[v], ps[:, 4 + v, :], ACT.Square).then_inc(num_sq, 1)
                act.wait_ge(pv_done, 3 * h + 3)
                act.activation(den, ps[:, 6, :], ACT.Square, scale=math.sqrt(EPS)).then_inc(den_sq, 1)
                act.wait_ge(evacuated, 8 * h + 8)
                act.activation(gate1, gate1, ACT.Sigmoid).then_inc(gate_open, 1)
                act.wait_ge(var_made, h + 1)
                act.activation(var, var, ACT.Sqrt).then_inc(head_std, 1)
                weights_hi(u + 5, 1)
                for v in range(2):
                    act.wait_ge(y_made, 2 * h + v + 1)
                    act.activation(h_hi[:, h * 2 + v, :], numsq[v], ACT.Copy).then_inc(y_hi_made, 1)

            def out_proj(u0, e0, s):
                for m in range(KT // 2):
                    for t in range(2):
                        act.wait_ge(evacuated, e0 + 2 * m + t + 1)
                        split_x(s, 2 * m + t)
                    weights_hi(u0 + m + 2, m % 2)

            def ffn(l):
                u0, e0, f0 = U_FFN[l], E_FFN[l], l * FT
                for n_half, (k0, n) in enumerate(HALVES):
                    def up(i, s, norm=False):
                        u, f = i + (u0 + s), i + (f0 + s)
                        if norm:
                            norm_std(S_FFN[l])
                        c = i + (k0 + s)
                        act.wait_ge(g_made, f + 1)
                        act.activation(cv[:, s, :], gpad[:, s, 2:S + 2], ACT.Identity,
                                       scale=convT[:, l, bass.ds(c + 2 * FT, 1)],
                                       bias=convT[:, l, bass.ds(c + 3 * FT, 1)]).then_inc(tap2, 1)
                        weights_hi(u + 2, s)
                        act.wait_ge(tap0, f + 1)
                        act.activation(act_o[:, s, :], cv[:, s, :], ACT.Silu).then_inc(silu_made, 1)
                        act.wait_ge(evacuated, i + (e0 + s) + 1)
                        act.activation(h_hi[:, i + s, :], hid[:, s, :], ACT.Copy).then_inc(hid_hi_made, 1)

                    first = 0
                    if n_half == 0:
                        up(0, 0, norm=True)
                        up(0, 1)
                        first = 2
                    with by_two(act, first, n) as i:
                        up(i, 0)
                        up(i, 1)
                    u0, e0, f0 = u0 + n, e0 + n, f0 + n

                    def down(j, s, scaled=None):
                        u = j + (u0 + s)
                        if n_half == 1:
                            act.wait_ge(evacuated, j + (e0 + s) + 1)
                            split_x(S_FFN[l] + 1, j + s)
                        if not (isinstance(u, int) and u + 2 >= U_END):
                            weights_hi(u + 2, s, scaled)

                    if n_half == 0:
                        with by_two(act, 0, KT) as j:
                            down(j, 0)
                            down(j, 1)
                    else:
                        for j in range(0, KT, 2):
                            for s in range(2):
                                down(j, s, 2 * (s + 1) if l == 0 and j == KT - 2 else None)
                    u0, e0 = u0 + KT, e0 + KT

            head(0, first=True)
            with act.Fori(1, HA) as h:
                head(h)
            out_proj(U_OUTA, E_OUTA, 1)
            ffn(0)

            for m in range(4):
                if m == 0:
                    norm_std(2)
                weights_hi(U_V + m + 2, m % 2, 2 * (m + 3))

            def attn_qk_hi(h, n):
                act.wait_ge(evacuated, 2 * h + (E_QK + n + 1))
                act.activation(qk_hi[n], tqk[n], ACT.Copy).then_inc(dqk_hi_made, 1)

            def attn_v_hi(h):
                act.activation(vh_hi, v_all[:, :, bass.ds(h * P, P)], ACT.Copy).then_inc(vh_hi_made, 1)

            def attn_exp(h, k, first):
                w = (TB - k) * P
                for c in range(2):
                    act.wait_ge(maxed, 8 * h + (2 * k + c + 1))
                    if not (first and k < 2):
                        act.wait_ge(pT_turned, 4 * h + (k - 1))
                    act.activation(prob[:, k % 2, c, 0:w], ps[:, 2 + (k % 2) * 2 + c, 0:w],
                                   ACT.Exp, bias=nmax[:, k % 2, c:c + 1],
                                   accum_out=lsum[:, k % 2, c:c + 1]).then_inc(exped, 1)

            def attn_pT_hi(h, k):
                i = TB - 1 - k
                act.wait_ge(pT_turned, 4 * h + (k + 1))
                act.activation(pT_hi[:, 0:i + 1, i * P:(i + 1) * P],
                               ps[:, 6, 0:(i + 1) * P].rearrange("p (j c) -> p j c", c=P), ACT.Copy)\
                    .then_inc(pT_hi_made, 1)

            def attn_norm(h):
                act.wait_ge(o_summed, h + 1)
                act.activation(sq[:, 1, :], ps[:, 6, :], ACT.Ln, scale=1.0 / P, bias=eps[:, :])\
                    .then_inc(o_ln, 1)
                act.wait_ge(o_ln, h + 1)
                act.activation(sqacc[:, :], sq[:, 1, :], ACT.Exp, scale=-0.5).then_inc(o_rstd, 1)

            def attn_o_hi(h):
                act.wait_ge(o_made, h + 1)
                act.activation(h_hi[:, h, :], ytmp[:, :], ACT.Copy).then_inc(o_hi_made, 1)

            def attn(h, s, scaled, prev=True, nxt=True):
                attn_exp(h, 0, not prev)
                attn_exp(h, 1, not prev)
                if prev:
                    attn_norm(h - 1)
                attn_pT_hi(h, 0)
                attn_exp(h, 2, not prev)
                if prev:
                    attn_o_hi(h - 1)
                attn_pT_hi(h, 1)
                attn_exp(h, 3, not prev)
                weights_hi(h + (U_QK + 2), s, scaled)
                attn_pT_hi(h, 2)
                if nxt:
                    attn_qk_hi(h + 1, 0)
                attn_pT_hi(h, 3)
                if nxt:
                    attn_qk_hi(h + 1, 1)
                act.wait_ge(dpv_done, h + 1)
                act.activation(sq[:, 0, :], ps[:, 7, :], ACT.Square).then_inc(o_sq, 1)
                if nxt:
                    attn_v_hi(h + 1)

            SC = 2 * 4
            act.wait_ge(evacuated, E_QK)
            attn_v_hi(0)
            attn_qk_hi(0, 0)
            attn_qk_hi(0, 1)
            attn(0, 0, SC + 2 * 3, prev=False)
            with by_two(act, 1, HB - 3) as h:
                attn(h, 1, 2 * h + (SC + 6))
                attn(h + 1, 0, 2 * h + (SC + 8))
            attn(HB - 3, 1, SC + 2 * HB)
            attn(HB - 2, 0, None)
            attn(HB - 1, 1, None, nxt=False)
            attn_norm(HB - 1)
            attn_o_hi(HB - 1)
            out_proj(U_OUTB, E_OUTB, 3)
            ffn(1)

            act.wait_ge(fin_summed, 1)
            act.activation(rcol[:, :], ps[:, 7, 0:TB], ACT.Sqrt, scale=1.0 / D, bias=eps[:, :])\
                .then_inc(fin_std, 1)
            act.wait_ge(fin_rstd, 1)
            for b in range(TB):
                act.wait_ge(fin_turned, 2 * b + 1)
                act.activation(o_sb[:, b, 0:512], ps[:, 2 * b, :], ACT.Copy, scale=rcol[:, b:b + 1])\
                    .then_inc(fin_scaled_a, 1)

        @block.vector
        def _(dve):
            dve.wait_ge(rows_loaded, 16 * 14)
            dve.tensor_tensor(ytmp[0:1, 0:2 * HDB].rearrange("p (a c) -> p a c", a=2),
                              lam_in[:, 0:4:2, :], lam_in[:, 1:4:2, :], ALU.mult).then_inc(lam_dve, 1)
            dve.wait_ge(lam_dve, 1)
            dve.tensor_reduce(lam_w[:, 2:4], ytmp[0:1, 0:2 * HDB].rearrange("p (a c) -> p a c", a=2),
                              AX.X, ALU.add).then_inc(lam_dve, 1)
            dve.wait_ge(rows_turned, 3)
            dve.tensor_copy(gainT[:, :], ps[:, 4, 0:57]).then_inc(rows_kept, 1)
            for l in range(2):
                dve.tensor_copy(convT[:, l, :], ps[:, 4, 64 + 96 * l:64 + 96 * l + 4 * FT])\
                    .then_inc(rows_kept, 1)
            dve.wait_ge(wg_hi_made, 1)
            dve.tensor_tensor(wg_lo, wg_raw, f32(wg_hi), ALU.subtract).then_inc(wg_split, 1)
            dve.wait_ge(lam_exp, 1)
            dve.tensor_tensor(lam_w[:, 6:7], lam_w[:, 5:6], lam_w[:, 4:5], ALU.subtract).then_inc(lam_dve, 1)
            dve.wait_ge(lam_dve, 3)
            dve.tensor_scalar(lam_w[:, 7:8], lam_w[:, 6:7], -LAM_INIT, None, ALU.add).then_inc(lam_dve, 1)
            dve.wait_ge(rows_kept, 3)
            dve.tensor_scalar(gainT[:, G_SUB:G_SUB + 1], gainT[:, G_SUB:G_SUB + 1], 1.0 - LAM_INIT, None,
                              ALU.mult).then_inc(sub_scaled, 1)

            def weights_lo(u, s):
                dve.wait_ge(w_hi_made, u + 1)
                dve.tensor_tensor(w_lo[:, s, :], wraw[:, s, :], f32(w_hi[:, s, :]), ALU.subtract)\
                    .then_inc(w_split, 1)

            def split_x(s, j):
                n = 8 * s + j
                g = G_STAGE.get(s)
                dve.wait_ge(xs_hi_made, n + 1)
                if g is None:
                    dve.tensor_tensor(xs_lo[:, j, :], xT[:, j, :], f32(xs_hi[:, j, :]), ALU.subtract)\
                        .then_inc(x_split, 1)
                else:
                    dve.scalar_tensor_tensor(out=xs_lo[:, j, :], in0=xT[:, j, :], scalar=gainT[:, g + j:g + j + 1],
                                             in1=f32(xs_hi[:, j, :]), op0=ALU.mult, op1=ALU.subtract)\
                        .then_inc(x_split, 1)

            def norm_rstd(s):
                dve.wait_ge(std_made, s + 1)
                dve.reciprocal(rstd[:, :], sq[:, 0, :]).then_inc(rstd_made, 1)

            for j in range(KT):
                dve.wait_ge(x_turned, j + 1)
                dve.tensor_copy(xT[:, j, :], ps[:, j, :]).then_inc(x_kept, 1)
                if j:
                    split_x(0, j - 1)
            split_x(0, KT - 1)
            weights_lo(0, 0)
            weights_lo(1, 1)
            dve.wait_ge(lam_spread, 1)
            dve.tensor_copy(coef[:, 1:2], ps[:, 4, 32:33]).then_inc(lam_kept, 1)
            norm_rstd(0)
            dve.wait_ge(gate_mm, 1)
            dve.wait_ge(rstd_made, 1)
            dve.tensor_tensor(g_z, ps[0:36, 5, :], rstd[0:36, :], ALU.mult).then_inc(gate_z, 1)
            dve.wait_ge(gate_act, 3)
            dve.tensor_tensor_scan(g_L[0:HA, :], g_e[32:36, :], g_e[32:36, :], 0.0, ALU.add, ALU.max)\
                .then_inc(gate_scan, 1)
            dve.wait_ge(gate_scan, 1)
            dve.scalar_tensor_tensor(out=g_a[0:HA, :], in0=g_t[0:HA, :], scalar=SOFTCAP, in1=g_L[0:HA, :],
                                     op0=ALU.mult, op1=ALU.add).then_inc(gate_scan, 1)
            dve.wait_ge(gate_scan, 2)
            dve.tensor_tensor_scan(g_M[0:HA, :], g_a[0:HA, :], g_a[0:HA, :], 0.0, ALU.max, ALU.max)\
                .then_inc(gate_scan, 1)
            dve.wait_ge(gate_scan, 3)
            dve.tensor_tensor(g_z[0:HA, :], g_L[0:HA, :], g_M[0:HA, :], ALU.subtract).then_inc(gate_scan, 1)
            dve.tensor_scalar(rowsM[:, 0:S], g_M[0:HA, :], -1.0, None, ALU.mult).then_inc(gate_scan, 1)
            dve.wait_ge(a_turned, 1)
            dve.tensor_copy(acol[:, :], ps[:, 5, 0:4 * HA]).then_inc(acol_made, 1)
            dve.wait_ge(rcol_turned, 1)
            dve.tensor_copy(rcol[:, :], ps[:, 4, 0:TB]).then_inc(rcol_made, 1)
            dve.wait_ge(rows_made, 1)
            dve.wait_ge(gate_scan, 5)
            dve.wait_ge(acol_made, 1)
            dve.wait_ge(rcol_made, 1)

            def pick(h):
                dve.tensor_scalar(pw[0:HA, 0:2 * S], rowsM[:, :], ident[0:HA, bass.ds(h, 1)], None, ALU.mult)\
                    .then_inc(m_picked, 1)

            def head(h, last=False):
                u = 4 * h
                dve.wait_ge(unit_done, u + 1)
                dve.scalar_tensor_tensor(out=tq, in0=ps[:, 0, :], scalar=DKA ** -0.5, in1=rstd[:, :],
                                         op0=ALU.mult, op1=ALU.mult).then_inc(evacuated, 1)
                dve.tensor_tensor(tk, ps[:, 1, :], rstd[:, :], ALU.mult).then_inc(evacuated, 1)
                dve.wait_ge(m_spread, 2 * h + 1)
                if not isinstance(h, int) or h:
                    dve.wait_ge(p_made, 4 * h)
                for j in range(TB):
                    dve.tensor_scalar(decay[:, OFF[j]:OFF[j] + S - j * P], ps[:, 7, j * P:S],
                                      acol[:, bass.ds(h + HA * j, 1)], 0.0, ALU.add, ALU.min)\
                        .then_inc(arg_made, 1)
                for n, t in enumerate((tq, tk)):
                    dve.wait_ge(qk_hi_made, 2 * h + n + 1)
                    dve.tensor_tensor(qk_lo[n], t, f32(qk_hi[n]), ALU.subtract).then_inc(qk_split, 1)
                dve.wait_ge(decay_masked, 4 * h + 4)
                dve.wait_ge(m_spread, 2 * h + 2)
                for j in range(TB):
                    dve.wait_ge(scored, 4 * h + (j + 1 if j < 2 else 4))
                    src = ps[:, 4 + j, 0:S - j * P] if j < 3 else ps[:, 6, 2 * P:3 * P]
                    dve.tensor_tensor(pw[:, OFF[j]:OFF[j] + S - j * P], src,
                                      decay[:, OFF[j]:OFF[j] + S - j * P], ALU.mult).then_inc(p_made, 1)
                weights_lo(u + 2, 0)
                dve.wait_ge(p_hi_made, h + 1)
                dve.tensor_tensor(p_lo, pw, f32(p_hi), ALU.subtract).then_inc(p_split, 1)
                for b in range(TB):
                    dve.wait_ge(v_hi_made, 4 * h + (b // 2 * 2 + 2))
                    dve.scalar_tensor_tensor(out=v_lo[:, b, :],
                                             in0=ps[:, 2 + b // 2, (b % 2) * DVA:(b % 2 + 1) * DVA],
                                             scalar=rcol[:, b:b + 1], in1=f32(v_hi[:, b, :]),
                                             op0=ALU.mult, op1=ALU.subtract).then_inc(evacuated, 1)
                weights_lo(u + 3, 1)
                dve.wait_ge(unit_done, u + 3)
                dve.tensor_tensor(gate0, ps[:, 0, :], rstd[:, :], ALU.mult).then_inc(evacuated, 1)
                weights_lo(u + 4, 0)
                dve.wait_ge(den_sq, h + 1)
                dve.tensor_tensor(den, den, floor, ALU.max).then_inc(den_made, 1)
                if not last:
                    dve.wait_ge(p_split, h + 1)
                    pick(h + 1)
                dve.wait_ge(unit_done, u + 4)
                dve.tensor_tensor(gate1, ps[:, 2, :], rstd[:, :], ALU.mult).then_inc(evacuated, 1)
                dve.wait_ge(head_summed, h + 1)
                dve.wait_ge(den_made, h + 1)
                dve.scalar_tensor_tensor(out=var, in0=ps[:, 7, :], scalar=1.0 / DVA, in1=den,
                                         op0=ALU.mult, op1=ALU.add).then_inc(var_made, 1)
                dve.wait_ge(head_std, h + 1)
                dve.reciprocal(den, var).then_inc(head_rstd, 1)
                for v in range(2):
                    dve.wait_ge(gate_scaled, 2 * h + v + 1)
                    dve.scalar_tensor_tensor(out=numsq[v], in0=ps[:, 4 + v, :],
                                             scalar=gainT[:, bass.ds(h * 2 + (G_HEAD + v), 1)], in1=gates[v],
                                             op0=ALU.mult, op1=ALU.mult).then_inc(y_made, 1)
                weights_lo(u + 5, 1)

            def add_x(tile, bank, wait_u):
                dve.wait_ge(unit_done, wait_u)
                dve.tensor_tensor(xT[:, tile, :], xT[:, tile, :], ps[:, bank, :], ALU.add)\
                    .then_inc(evacuated, 1)

            def out_proj(u0, s):
                for m in range(KT // 2):
                    for t in range(2):
                        add_x(2 * m + t, 2 * (m % 2) + t, u0 + m + 1)
                    for t in range(2):
                        split_x(s, 2 * m + t)
                    weights_lo(u0 + m + 2, m % 2)

            def ffn(l):
                u0, f0 = U_FFN[l], l * FT
                dve.memset(gpad[:, :, 0:2], 0.0).then_inc(pads_zeroed, 1)
                for n_half, (k0, n) in enumerate(HALVES):
                    def up(i, s, norm=False):
                        u, f = i + (u0 + s), i + (f0 + s)
                        if norm:
                            norm_rstd(S_FFN[l])
                            dve.wait_ge(rstd_made, S_FFN[l] + 1)
                            dve.wait_ge(pads_zeroed, l + 1)
                        c = i + (k0 + s)
                        dve.wait_ge(unit_done, u + 1)
                        dve.tensor_tensor(gpad[:, s, 2:S + 2], ps[:, 2 * s, :], rstd[:, :], ALU.mult)\
                            .then_inc(g_made, 1)
                        dve.wait_ge(tap2, f + 1)
                        dve.scalar_tensor_tensor(out=cv[:, s, :], in0=gpad[:, s, 1:S + 1],
                                                 scalar=convT[:, l, bass.ds(c + FT, 1)], in1=cv[:, s, :],
                                                 op0=ALU.mult, op1=ALU.add).then_inc(tap1, 1)
                        dve.wait_ge(tap1, f + 1)
                        dve.scalar_tensor_tensor(out=cv[:, s, :], in0=gpad[:, s, 0:S],
                                                 scalar=convT[:, l, bass.ds(c, 1)], in1=cv[:, s, :],
                                                 op0=ALU.mult, op1=ALU.add).then_inc(tap0, 1)
                        weights_lo(u + 2, s)
                        dve.wait_ge(silu_scaled, f + 1)
                        dve.tensor_tensor(hid[:, s, :], ps[:, 2 * s + 1, :], act_o[:, s, :], ALU.mult)\
                            .then_inc(evacuated, 1)

                    first = 0
                    if n_half == 0:
                        up(0, 0, norm=True)
                        up(0, 1)
                        first = 2
                    with by_two(dve, first, n) as i:
                        up(i, 0)
                        up(i, 1)
                    u0, f0 = u0 + n, f0 + n

                    def down(j, s):
                        u = j + (u0 + s)
                        add_x(j + s, 2 * s, u + 1)
                        if n_half == 1 and l == 0:
                            split_x(S_FFN[l] + 1, j + s)
                        if not (isinstance(u, int) and u + 2 >= U_END):
                            weights_lo(u + 2, s)

                    if n_half == 0:
                        with by_two(dve, 0, KT) as j:
                            down(j, 0)
                            down(j, 1)
                    else:
                        for j in range(0, KT, 2):
                            down(j, 0)
                            down(j, 1)
                    u0 += KT

            pick(0)
            head(0)
            with dve.Fori(1, HA - 1) as h:
                head(h)
            head(HA - 1, last=True)
            out_proj(U_OUTA, 1)
            ffn(0)

            for m in range(4):
                if m == 0:
                    norm_rstd(2)
                    dve.wait_ge(rcol_turned, 2)
                    dve.tensor_copy(rcol[:, :], ps[:, 4, 0:TB]).then_inc(rcol_made, 1)
                    dve.wait_ge(rcol_made, 2)
                dve.wait_ge(unit_done, U_V + m + 1)
                for b in range(TB):
                    dve.tensor_scalar(v_all[:, b, m * 2 * P:(m + 1) * 2 * P],
                                      ps[:, 2 * (m % 2) + b // 2, (b % 2) * 2 * P:(b % 2 + 1) * 2 * P],
                                      rcol[:, b:b + 1], None, ALU.mult).then_inc(evacuated, 1)
                weights_lo(U_V + m + 2, m % 2)

            def attn_q(h):
                dve.wait_ge(q_done, h + 1)
                dve.scalar_tensor_tensor(out=tqk[0], in0=ps[:, 0, :], scalar=HDB ** -0.5, in1=rstd[:, :],
                                         op0=ALU.mult, op1=ALU.mult).then_inc(evacuated, 1)

            def attn_k(h):
                dve.wait_ge(unit_done, h + (U_QK + 1))
                dve.tensor_tensor(tqk[1], ps[:, 1, :], rstd[:, :], ALU.mult).then_inc(evacuated, 1)

            def attn_qk_lo(h, n):
                dve.wait_ge(dqk_hi_made, 2 * h + n + 1)
                dve.tensor_tensor(qk_lo[n], tqk[n], f32(qk_hi[n]), ALU.subtract).then_inc(dqk_split, 1)

            def attn_max(h, k):
                w = (TB - k) * P
                for c in range(2):
                    dve.wait_ge(dscored, 8 * h + (2 * k + c + 1))
                    dve.tensor_reduce(nmax[:, k % 2, c:c + 1], ps[:, 2 + (k % 2) * 2 + c, 0:w],
                                      AX.X, ALU.max, negate=True).then_inc(maxed, 1)

            def attn_mix(h, k):
                n = 4 * h + (k + 1)
                r, w = k % 2, (TB - k) * P
                dve.wait_ge(exped, 8 * h + (2 * k + 2))
                dve.reciprocal(rsum[:, r, :], lsum[:, r, :]).then_inc(sum_inv, 1)
                dve.wait_ge(sum_inv, n)
                dve.tensor_tensor(rsum[:, r, :], rsum[:, r, :], coef[:, :], ALU.mult).then_inc(sum_coef, 1)
                dve.wait_ge(sum_coef, n)
                p0, p1 = (prob[:, r, c, 0:w] for c in range(2))
                dve.tensor_scalar(p0, p0, rsum[:, r, 0:1], None, ALU.mult).then_inc(p0_scaled, 1)
                dve.wait_ge(p0_scaled, n)
                dve.scalar_tensor_tensor(out=p0, in0=p1, scalar=rsum[:, r, 1:2], in1=p0,
                                         op0=ALU.mult, op1=ALU.add).then_inc(a_made, 1)

            def attn_pT_lo(h, k):
                i = TB - 1 - k
                dve.wait_ge(pT_hi_made, 4 * h + (k + 1))
                dve.tensor_tensor(pT_lo[:, 0:i + 1, i * P:(i + 1) * P],
                                  ps[:, 6, 0:(i + 1) * P].rearrange("p (j c) -> p j c", c=P),
                                  f32(pT_hi[:, 0:i + 1, i * P:(i + 1) * P]), ALU.subtract).then_inc(pT_split, 1)

            def attn_finish(h, last=False):
                dve.wait_ge(o_rstd, h + 1)
                if last:
                    dve.wait_ge(o_split, h)
                else:
                    dve.wait_ge(vh_split, h + 2)
                dve.scalar_tensor_tensor(out=ytmp[:, :], in0=ps[:, 7, :], scalar=gainT[:, G_SUB:G_SUB + 1],
                                         in1=sqacc[:, :], op0=ALU.mult, op1=ALU.mult).then_inc(o_made, 1)

            def attn(h, s, prev=True, nxt=True):
                attn_max(h, 0)
                attn_max(h, 1)
                attn_mix(h, 0)
                attn_mix(h, 1)
                if prev:
                    attn_finish(h - 1)
                attn_max(h, 2)
                attn_pT_lo(h, 0)
                attn_mix(h, 2)
                attn_max(h, 3)
                attn_pT_lo(h, 1)
                attn_mix(h, 3)
                if nxt:
                    attn_q(h + 1)
                attn_pT_lo(h, 2)
                if nxt:
                    attn_qk_lo(h + 1, 0)
                attn_pT_lo(h, 3)
                weights_lo(h + (U_QK + 2), s)
                if nxt:
                    attn_k(h + 1)
                    attn_qk_lo(h + 1, 1)

            attn_q(0)
            attn_qk_lo(0, 0)
            attn_k(0)
            attn_qk_lo(0, 1)
            attn(0, 0, prev=False)
            with by_two(dve, 1, HB - 3) as h:
                attn(h, 1)
                attn(h + 1, 0)
            attn(HB - 3, 1)
            attn(HB - 2, 0)
            attn(HB - 1, 1, nxt=False)
            attn_finish(HB - 1, last=True)
            out_proj(U_OUTB, 3)
            ffn(1)

            dve.wait_ge(fin_std, 1)
            dve.reciprocal(rcol[:, :], rcol[:, :]).then_inc(fin_rstd, 1)
            dve.wait_ge(fin_rstd, 1)
            for b in range(TB):
                dve.wait_ge(fin_turned, 2 * b + 2)
                dve.tensor_scalar(o_sb[:, b, 512:1024], ps[:, 2 * b + 1, :], rcol[:, b:b + 1], None, ALU.mult)\
                    .then_inc(fin_scaled_v, 1)

        @block.tensor
        def _(pe):
            def mm3(o, w, m, start, stop):
                pe.matmul(o, w[0], m[0], start=start, stop=False)
                pe.matmul(o, w[0], m[1], start=False, stop=False)
                return pe.matmul(o, w[1], m[0], start=False, stop=stop)

            def xs(kt):
                return xs_hi[:, kt, :], xs_lo[:, kt, :]

            def hid_of(kt):
                return h_hi[:, kt, :], h_lo[:, kt, :]

            def wcol(s, t, c, kt, a, b):
                return cols(w_hi[:, s, :], t, c)[:, kt, a:b], cols(w_lo[:, s, :], t, c)[:, kt, a:b]

            def two_tiles(u, s, banks, moving, evac, ready=None, kts=range(KT)):
                if kts[0] == 0:
                    pe.wait_ge(w_split, u + 1)
                    if evac is not None:
                        pe.wait_ge(evacuated, evac)
                for kt in kts:
                    if ready is not None:
                        pe.wait_ge(ready[0], ready[1] + kt + 1)
                    for t, b in enumerate(banks):
                        last = mm3(ps[:, b, :], wcol(s, KT, 2 * P, kt, t * P, (t + 1) * P), moving(kt),
                                   kt == 0, kt == KT - 1)
                if kts[-1] == KT - 1:
                    last.then_inc(unit_done, 1)

            def one_tile(u, s, bank, moving, evac, n, ready=None):
                pe.wait_ge(w_split, u + 1)
                pe.wait_ge(evacuated, evac)
                for kt in range(n):
                    if ready is not None:
                        pe.wait_ge(ready[0], ready[1] + kt + 1)
                    last = mm3(ps[:, bank, :], wcol(s, n, P, kt, 0, P), moving(kt), kt == 0, kt == n - 1)
                last.then_inc(unit_done, 1)

            def token_major(u, s, evac, ready=None, blocks=range(TB)):
                if blocks[0] == 0:
                    pe.wait_ge(w_split, u + 1)
                    if evac is not None:
                        pe.wait_ge(evacuated, evac)
                for b in blocks:
                    for kt in range(KT):
                        if ready is not None and b == 0:
                            pe.wait_ge(ready[0], ready[1] + kt + 1)
                        st = tuple(a[:, b * P:(b + 1) * P] for a in xs(kt))
                        last = mm3(ps[:, 2 * s + b // 2, (b % 2) * 256:(b % 2 + 1) * 256], st,
                                   wcol(s, KT, 2 * P, kt, 0, 2 * P), kt == 0, kt == KT - 1)
                if blocks[-1] == TB - 1:
                    last.then_inc(unit_done, 1)

            def norm_sum(s):
                pe.wait_ge(sq_added, 8 * (s + 1))
                pe.matmul(ps[:, 7, :], onesf[:, :], sqacc[:, :], start=True, stop=True).then_inc(norm_summed, 1)

            def turn_rstd(s):
                pe.wait_ge(rstd_made, s + 1)
                for b in range(TB):
                    last = pe.matmul(ps[:, 4, b:b + 1], rstd[0:1, b * P:(b + 1) * P], onesf[0:1, 0:1],
                                     start=True, stop=True)
                last.then_inc(rcol_turned, 1)

            pe.wait_ge(const_made, 10)
            pe.wait_ge(rows_loaded, 16 * 14)
            pe.transpose(ps[:, 4, 0:57], gain_rows, ident[0:57, 0:57]).then_inc(rows_turned, 1)
            for l in range(2):
                pe.transpose(ps[:, 4, 64 + 96 * l:64 + 96 * l + 4 * FT], conv_rows[:, l, :],
                             ident[0:4 * FT, 0:4 * FT]).then_inc(rows_turned, 1)
            pe.wait_ge(x_loaded, 16 * TB)
            for j in range(KT):
                if j == 4:
                    pe.wait_ge(rows_kept, 3)
                for b in range(TB):
                    last = pe.transpose(ps[:, j, b * P:(b + 1) * P], x_in[:, b, j * P:(j + 1) * P], ident[:, :])
                last.then_inc(x_turned, 1)
            pe.wait_ge(lam_dve, 4)
            pe.wait_ge(x_kept, 8)
            pe.matmul(ps[:, 4, 32:33], onesf[0:1, :], lam_w[0:1, 7:8], start=True, stop=True)\
                .then_inc(lam_spread, 1)
            pe.wait_ge(wg_split, 1)
            for kt in range(KT):
                pe.wait_ge(x_split, kt + 1)
                last = mm3(ps[:, 5, :], (wg_hi[:, kt, :], wg_lo[:, kt, :]), xs(kt), kt == 0, kt == KT - 1)
            last.then_inc(gate_mm, 1)
            norm_sum(0)

            def head(h, first=False):
                u = 4 * h
                two_tiles(u, 0, (0, 1), xs, None if first else 8 * h - 1)
                if first:
                    turn_rstd(0)
                    pe.wait_ge(gate_scan, 2)
                    for b in range(TB):
                        last = pe.transpose(ps[:, 5, HA * b:HA * (b + 1)], g_a[0:HA, b * P:(b + 1) * P],
                                            ident[0:HA, 0:HA])
                    last.then_inc(a_turned, 1)
                pe.wait_ge(m_picked, h + 1)
                if not first:
                    pe.wait_ge(den_sq, h)
                    pe.wait_ge(var_made, h)
                pe.matmul(ps[:, 7, :], onesf[0:HA, :], pw[0:HA, 0:S], start=True, stop=True)\
                    .then_inc(m_spread, 1)
                pe.matmul(ps[:, 6, :], onesf[0:HA, :], pw[0:HA, S:2 * S], start=True, stop=True)\
                    .then_inc(m_spread, 1)
                token_major(u + 1, 1, None if first else 8 * h, blocks=range(0, TB // 2))
                pe.wait_ge(qk_split, 2 * h + 2)
                pe.wait_ge(floor_kept, h + 1)
                if first:
                    pe.wait_ge(rcol_made, 1)
                    pe.wait_ge(acol_made, 1)
                else:
                    pe.wait_ge(y_made, 2 * h)
                for j in range(TB):
                    o = ps[:, 4 + j, 0:S - j * P] if j < 3 else ps[:, 6, 2 * P:3 * P]
                    mm3(o, (k_hi[:, j * P:(j + 1) * P], k_lo[:, j * P:(j + 1) * P]),
                        (q_hi[:, j * P:S], q_lo[:, j * P:S]), True, True).then_inc(scored, 1)
                token_major(u + 1, 1, None, blocks=range(TB // 2, TB))
                one_tile(u + 2, 0, 0, xs, 8 * h + 2, KT)
                pe.wait_ge(evacuated, 8 * h + 6)
                pe.wait_ge(p_split, h + 1)
                for v in range(2):
                    for j in range(TB):
                        pj = tuple(a[:, OFF[j]:OFF[j] + S - j * P] for a in (p_hi, p_lo))
                        last = mm3(ps[:, 4 + v, j * P:S],
                                   (v_hi[:, j, v * P:(v + 1) * P], v_lo[:, j, v * P:(v + 1) * P]), pj,
                                   j == 0, j == TB - 1)
                    last.then_inc(pv_done, 1)
                for j in range(TB):
                    for n, a in enumerate((p_hi, p_lo)):
                        last = pe.matmul(ps[:, 6, j * P:S], ones_r[:, :], a[:, OFF[j]:OFF[j] + S - j * P],
                                         start=(j == 0 and n == 0), stop=(j == TB - 1 and n == 1))
                last.then_inc(pv_done, 1)
                one_tile(u + 3, 1, 2, xs, 8 * h + 6, KT)
                pe.wait_ge(num_added, h + 1)
                pe.wait_ge(arg_made, 4 * h + 4)
                pe.matmul(ps[:, 7, :], onesf[:, :], num0, start=True, stop=True).then_inc(head_summed, 1)

            def out_proj(u0, e0, ready, first=0):
                for m in range(first, KT // 2):
                    s = m % 2
                    evac = e0 if m < 2 else e0 + 2 * (m - 1)
                    two_tiles(u0 + m, s, (2 * s, 2 * s + 1), hid_of, evac, (ready, 0) if m == 0 else None)

            def ffn(l, e_in):
                u0, e0, f0 = U_FFN[l], E_FFN[l], l * FT
                for n_half, (k0, n) in enumerate(HALVES):
                    for s in range(2):
                        two_tiles(u0 + s, s, (2 * s, 2 * s + 1), xs, e_in[s],
                                  (x_split, 8 * S_FFN[l]) if n_half == 0 and s == 0 else None)
                        if n_half == 0 and s == 0:
                            norm_sum(S_FFN[l])
                    with by_two(pe, 2, n) as i:
                        for s in range(2):
                            two_tiles(i + (u0 + s), s, (2 * s, 2 * s + 1), xs, i + (e0 + s - 1))
                    e_in = (e0 + n - 1, e0 + n)
                    u0, e0 = u0 + n, e0 + n
                    for s in range(2):
                        one_tile(u0 + s, s, 2 * s, hid_of, e_in[s], n, (hid_split, f0 + k0) if s == 0 else None)
                    with by_two(pe, 2, KT) as j:
                        for s in range(2):
                            one_tile(j + (u0 + s), s, 2 * s, hid_of, j + (e0 + s - 1), n)
                    e_in = (e0 + KT - 1, e0 + KT)
                    u0, e0 = u0 + KT, e0 + KT

            head(0, first=True)
            with pe.Fori(1, HA) as h:
                head(h)
            out_proj(U_OUTA, E_OUTA, y_split)
            ffn(0, (E_OUTA + 6, E_OUTA + 8))

            for m in range(4):
                token_major(U_V + m, m % 2, E_V - 1 if m == 0 else E_V if m == 1 else E_V + 4 * (m - 1),
                            (x_split, 16) if m == 0 else None)
                if m == 0:
                    norm_sum(2)
                    turn_rstd(2)

            def attn_project(h, s, part):
                if part == 0:
                    pe.wait_ge(w_split, h + (U_QK + 1))
                    pe.wait_ge(evacuated, 2 * h + E_QK)
                t, n = part // 4, KT // 4
                for kt in range(part % 4 * n, (part % 4 + 1) * n):
                    last = mm3(ps[:, t, :], wcol(s, KT, 2 * P, kt, t * P, (t + 1) * P), xs(kt),
                               kt == 0, kt == KT - 1)
                if part % 4 == 3:
                    last.then_inc(unit_done if t else q_done, 1)

            def attn_scores(h, k, first):
                i = TB - 1 - k
                for c in range(2):
                    if not (first and k < 2):
                        pe.wait_ge(exped, 8 * h + (2 * k + c - 3))
                    b = 2 + (k % 2) * 2 + c
                    o = ps[:, b, 0:(i + 1) * P]
                    r = slice(c * HDB, (c + 1) * HDB)
                    qi = tuple(a[r, i * P:(i + 1) * P] for a in (q_hi, q_lo))
                    ks = tuple(a[r, 0:(i + 1) * P] for a in (k_hi, k_lo))
                    pe.matmul(o, qi[0], ks[0], start=True, stop=False)
                    pe.matmul(ps[:, b, i * P:(i + 1) * P], ident_b[:, :], mask_b[:, :],
                              start=False, stop=False)
                    pe.matmul(o, qi[0], ks[1], start=False, stop=False)
                    pe.matmul(o, qi[1], ks[0], start=False, stop=True).then_inc(dscored, 1)

            def attn_turn(h, k, first):
                pe.wait_ge(a_made, 4 * h + (k + 1))
                if not (first and k == 0):
                    pe.wait_ge(pT_split, 4 * h + k)
                for j in range(TB - k):
                    last = pe.transpose(ps[:, 6, j * P:(j + 1) * P], prob[:, k % 2, 0, j * P:(j + 1) * P],
                                        ident[:, :])
                last.then_inc(pT_turned, 1)

            def attn_sum(h):
                pe.wait_ge(o_sq, h + 1)
                pe.wait_ge(pT_split, 4 * h + 4)
                pe.matmul(ps[:, 6, :], onesf[:, :], sq[:, 0, :], start=True, stop=True).then_inc(o_summed, 1)

            def out_first(m, kts):
                two_tiles(U_OUTB + m, m, (2 * m, 2 * m + 1), hid_of, E_OUTB, (o_split, 0), kts=kts)

            def attn(h, s, prev=True, nxt=True):
                def fill(*parts):
                    for part in parts:
                        if nxt:
                            attn_project(h + 1, s, part)
                        elif part < HB - 1:
                            out_first(0, (part,))

                first = not prev
                pe.wait_ge(dqk_split, 2 * h + 2)
                attn_scores(h, 0, first)
                if prev:
                    attn_sum(h - 1)
                attn_scores(h, 1, first)
                fill(0)
                attn_scores(h, 2, first)
                fill(1)
                if prev:
                    pe.wait_ge(o_ln, h)
                attn_turn(h, 0, first)
                attn_scores(h, 3, first)
                fill(2)
                attn_turn(h, 1, first)
                fill(3, 4)
                attn_turn(h, 2, first)
                fill(5)
                attn_turn(h, 3, first)
                fill(6, 7)
                pe.wait_ge(pT_split, 4 * h + 4)
                pe.wait_ge(vh_split, h + 1)
                if prev:
                    pe.wait_ge(o_made, h)
                for j in range(TB):
                    last = mm3(ps[:, 7, j * P:S], (vh_hi[:, j, :], vh_lo[:, j, :]),
                               (pT_hi[:, j, j * P:S], pT_lo[:, j, j * P:S]), j == 0, j == TB - 1)
                last.then_inc(dpv_done, 1)

            for part in range(8):
                attn_project(0, 0, part)
            attn(0, 1, prev=False)
            with by_two(pe, 1, HB - 1) as h:
                attn(h, 0)
                attn(h + 1, 1)
            attn(HB - 1, 0, nxt=False)
            out_first(1, range(0, 2))
            attn_sum(HB - 1)
            out_first(1, range(2, HB - 1))
            out_first(0, (HB - 1,))
            out_first(1, (HB - 1,))
            out_proj(U_OUTB, E_OUTB, None, first=2)
            ffn(1, (E_OUTB + 6, E_OUTB + 8))

            pe.wait_ge(sq_added, 8 * 5)
            for b in range(TB):
                last = pe.matmul(ps[:, 7, b:b + 1], sqacc[:, b * P:(b + 1) * P], onesf[:, 0:1],
                                 start=True, stop=True)
            last.then_inc(fin_summed, 1)
            pe.wait_ge(xs_hi_made, 8 * 5)
            pe.wait_ge(evacuated, E_FFN1 + n_ffn)
            for b in range(TB):
                for a in range(2):
                    if 2 * b + a == 7:
                        pe.wait_ge(fin_std, 1)
                    for t in range(4):
                        last = pe.transpose(ps[:, 2 * b + a, t * P:(t + 1) * P],
                                            xg_fin[:, 4 * a + t, b * P:(b + 1) * P], ident[:, :])
                    last.then_inc(fin_turned, 1)


_INS = ['x', 'attn_norm_g', 'ffn_norm_g', 'mlstm_w_in', 'mlstm_b_gate', 'mlstm_head_g', 'mlstm_w_out',
        'kv_norm_g', 'w_kv', 'diff_w_q', 'diff_lambda_q1', 'diff_lambda_k1', 'diff_lambda_q2',
        'diff_lambda_k2', 'diff_subln_g', 'diff_w_out', 'ffn_w_up', 'ffn_conv_w', 'ffn_conv_b',
        'ffn_w_down', 'final_norm_g']
_OUTS = [((1, 512, 1024), 'float32')]


def kernel(**inputs):
    import numpy as _np
    import concourse.bacc as _bacc
    from concourse import mybir as _mybir
    from concourse.bass_utils import run_bass_kernel_spmd as _run

    nc = _bacc.Bacc("TRN2", target_bir_lowering=False, num_devices=1)
    arrays, args = {}, []
    for name in _INS:
        a = _np.ascontiguousarray(inputs[name])
        arrays[f"in_{name}_dram"] = a
        args.append(nc.dram_tensor(f"in_{name}_dram", a.shape, _mybir.dt.from_np(a.dtype), kind="ExternalInput").ap())
    for i, (shape, dtype) in enumerate(_OUTS):
        dt = _mybir.dt.from_np(_np.dtype(dtype))
        args.append(nc.dram_tensor(f"out_{i}_dram", shape, dt, kind="ExternalOutput").ap())
    build_trunk(nc, *args)
    r = _run(nc, [arrays], core_ids=[0])
    got = tuple(r.results[0][f"out_{i}_dram"] for i in range(len(_OUTS)))
    return got[0]
```

```python
import math
from contextlib import ExitStack, contextmanager

import concourse.bass as bass
from concourse import mybir

F32 = mybir.dt.float32
F32R = mybir.dt.float32r
BF16 = mybir.dt.bfloat16
ALU = mybir.AluOpType
ACT = mybir.ActivationFunctionType
AX = mybir.AxisListType

P = 128
SLOT = 2048
EPS = 1e-6
SOFTCAP = 15.0
MASKED = -1e30
LAM_INIT = 0.8 - 0.6 * math.exp(-0.3 * 1)


@contextmanager
def by_two(engine, start, stop):
    with engine.Fori(0, (stop - start) // 2) as pair:
        yield pair * 2 + start


def build_trunk(nc, x, attn_norm_g, ffn_norm_g, mlstm_w_in, mlstm_b_gate, mlstm_head_g, mlstm_w_out,
                kv_norm_g, w_kv, diff_w_q, diff_lambda_q1, diff_lambda_k1, diff_lambda_q2,
                diff_lambda_k2, diff_subln_g, diff_w_out, ffn_w_up, ffn_conv_w, ffn_conv_b,
                ffn_w_down, final_norm_g, out):
    S, D = x.shape[1], x.shape[2]
    KT = D // P
    TB = S // P
    HA = mlstm_head_g.shape[1]
    DVA = mlstm_head_g.shape[2]
    DKA = P
    HB = D // P
    HDB = P // 2
    DFF = ffn_conv_b.shape[1]
    FT = DFF // P
    assert (S, D, HA, DVA, FT) == (512, 1024, 4, 256, 22)
    HALVES = ((0, 12), (12, 10))
    HT = 12

    U_OUTA, E_OUTA = 4 * HA, 8 * HA
    U_FFN0, E_FFN0 = U_OUTA + KT // 2, E_OUTA + KT
    n_ffn = FT + 2 * KT
    U_V, E_V = U_FFN0 + n_ffn, E_FFN0 + n_ffn
    U_QK, E_QK = U_V + 4, E_V + 4 * TB
    U_OUTB, E_OUTB = U_QK + HB, E_QK + 2 * HB
    U_FFN1, E_FFN1 = U_OUTB + KT // 2, E_OUTB + KT
    U_END = U_FFN1 + n_ffn
    U_FFN, E_FFN = (U_FFN0, U_FFN1), (E_FFN0, E_FFN1)
    S_FFN = (1, 3)
    G_STAGE = {0: 0, 1: 16, 3: 24, 4: 40}
    G_Q, G_KV, G_HEAD, G_SUB = 8, 32, 48, 56
    X_BANK = (5, 0, 1, 2, 3, 6, 7, 4)
    W_AT = 4
    FIN_BLOCKS = (0, 1, 3, 2)

    es = ExitStack()
    with es:
        def sb(name, shape, dt):
            return es.enter_context(nc.sbuf_tensor(name, shape, dt))

        def sem(name):
            return es.enter_context(nc.semaphore(name))

        ps = es.enter_context(nc.psum_tensor("ps", [P, 8, 512], F32))

        xT = sb("xT", [P, KT, S], F32)
        xs_hi = sb("xs_hi", [P, KT, S], F32R)
        xs_lo = sb("xs_lo", [P, KT, S], F32R)
        wraw = sb("wraw", [P, 2, SLOT], F32)
        w_hi = sb("w_hi", [P, 2, SLOT], F32R)
        w_lo = sb("w_lo", [P, 2, SLOT], F32R)
        h_hi = sb("h_hi", [P, HT, S], F32R)
        h_lo = sb("h_lo", [P, HT, S], F32R)
        mixR = sb("mixR", [P, 8 * S], F32R)
        mixF = sb("mixF", [P, 14 * S], F32)
        rowsM = sb("rowsM", [HA, 2 * S], F32)
        rstd = sb("rstd", [P, S], F32)
        sqacc = sb("sqacc", [P, S], F32)
        sq = sb("sq", [P, 2, S], F32)
        ytmp = sb("ytmp", [P, S], F32)
        ident = sb("ident", [P, P], F32)
        onesf = sb("onesf", [P, P], F32)
        ones_r = sb("ones_r", [P, P], F32R)
        tri = sb("tri", [P, P], F32)
        ident_b = sb("ident_b", [P, P], BF16)
        mask_b = sb("mask_b", [P, P], BF16)
        gainT = sb("gainT", [P, 57], F32)
        convT = sb("convT", [P, 2, 4 * FT], F32)
        acol = sb("acol", [P, 4 * HA], F32)
        rcol = sb("rcol", [P, TB], F32)
        eps = sb("eps", [P, 1], F32)
        bgate = sb("bgate", [P, 2], F32)
        lam_in = sb("lam_in", [1, 4, HDB], F32)
        lam_w = sb("lam_w", [1, 8], F32)
        coef = sb("coef", [P, 2], F32)
        nmax = sb("nmax", [P, 2, 2], F32)
        lsum = sb("lsum", [P, 2, 2], F32)
        rsum = sb("rsum", [P, 2, 2], F32)

        def f32(ap):
            return ap.bitcast(F32)

        x_in = mixF[:, 0:4096].rearrange("p (b c) -> p b c", b=TB)
        gain_rows = mixF[0:57, 4096:4224]
        conv_rows = mixF[0:4 * FT, 4224:4480].rearrange("p (l c) -> p l c", l=2)
        wg_raw = mixF[:, 4608:5632].rearrange("p (t c) -> p t c", t=KT)
        wg_hi = h_hi[:, 8:10, :].rearrange("p a b -> p (a b)").rearrange("p (t c) -> p t c", t=KT)
        wg_lo = h_lo[:, 8:10, :].rearrange("p a b -> p (a b)").rearrange("p (t c) -> p t c", t=KT)
        g_z, g_t, g_e, g_L, g_a, g_M = (mixF[0:36, k * S:(k + 1) * S] for k in (0, 1, 2, 3, 13, 4))

        OFF = [j * S - P * (j * (j - 1) // 2) for j in range(TB)]
        PTRI = OFF[-1] + P
        q_hi, q_lo, k_hi, k_lo = (mixR[:, n * S:(n + 1) * S] for n in range(4))
        v_hi = mixR[:, 4 * S:6 * S].rearrange("p (b c) -> p b c", b=TB)
        v_lo = mixR[:, 6 * S:8 * S].rearrange("p (b c) -> p b c", b=TB)
        p_hi = h_hi[:, 8:11, :].rearrange("p a b -> p (a b)")[:, 0:PTRI]
        p_lo = h_lo[:, 8:11, :].rearrange("p a b -> p (a b)")[:, 0:PTRI]
        decay = mixF[:, 0:PTRI]
        pw = mixF[:, PTRI:2 * PTRI]
        tq, tk, floor, den, num0, num1, var, gate0, gate1 = (
            mixF[:, 2 * PTRI + n * S:2 * PTRI + (n + 1) * S] for n in range(9))
        numsq, gates = (num0, num1), (gate0, gate1)

        v_all = mixF[:, 0:4096].rearrange("p (b c) -> p b c", b=TB)
        prob = mixF[:, 4096:6144].rearrange("p (a c s) -> p a c s", a=2, c=2)
        tqk = (mixF[:, 6144:6656], mixF[:, 6656:7168])
        qk_hi = (q_hi, k_hi)
        qk_lo = (q_lo, k_lo)
        vh_hi = mixR[:, 4 * S:5 * S].rearrange("p (b c) -> p b c", b=TB)
        vh_lo = mixR[:, 5 * S:6 * S].rearrange("p (b c) -> p b c", b=TB)
        pT_hi = h_hi[:, 8:12, :]
        pT_lo = h_lo[:, 8:12, :]

        gpad = mixF[:, 0:2 * (S + 2)].rearrange("p (a s) -> p a s", a=2)
        FB = 2 * (S + 2)
        cv, act_o, hid = (mixF[:, FB + n * 2 * S:FB + (n + 1) * 2 * S]
                          .rearrange("p (a s) -> p a s", a=2) for n in range(3))
        xg_fin = mixF[:, 0:KT * S].rearrange("p (t s) -> p t s", t=KT)
        o_sb = wraw[:, :, :].rearrange("p a (b c) -> p (a b) c", b=2)

        x_loaded = [sem(f"x_block{b}_loaded") for b in range(TB)]
        gains_loaded = sem("gains_loaded")
        rows_loaded = sem("rows_loaded")
        wg_loaded = sem("wg_loaded")
        const_made = sem("const_made")
        bg_zeroed = sem("bg_zeroed")
        wg_zeroed = sem("wg_zeroed")
        ones_r_made = sem("ones_r_made")
        rows_turned = sem("rows_turned")
        rows_kept = sem("rows_kept")
        gains_turned = sem("gains_turned")
        gains_kept = sem("gains_kept")
        x_turned = sem("x_turned")
        x_kept = sem("x_kept")
        wg_hi_made = sem("wg_hi_made")
        wg_split = sem("wg_split")
        bg_scaled = sem("bg_scaled")
        lam_dve = sem("lam_dve")
        lam_exp = sem("lam_exp")
        lam_spread = sem("lam_spread")
        lam_kept = sem("lam_kept")
        sub_scaled = sem("sub_scaled")
        gate_mm = sem("gate_mm")
        gate_z = sem("gate_z")
        gate_act = sem("gate_act")
        gate_scan = sem("gate_scan")
        rows_made = sem("rows_made")
        a_turned = sem("a_turned")
        acol_made = sem("acol_made")

        slot_loaded = [sem("slot0_loaded"), sem("slot1_loaded")]
        w_scaled = sem("w_scaled")
        w_hi_made = sem("w_hi_made")
        w_split = sem("w_split")
        unit_done = sem("unit_done")
        evacuated = sem("evacuated")

        xs_hi_made = sem("xs_hi_made")
        x_split = sem("x_split")
        sq_made = sem("sq_made")
        sq_added = sem("sq_added")
        norm_summed = sem("norm_summed")
        std_made = sem("std_made")
        rstd_made = sem("rstd_made")
        rcol_turned = sem("rcol_turned")
        rcol_made = sem("rcol_made")

        m_picked = sem("m_picked")
        m_spread = sem("m_spread")
        floor_kept = sem("floor_kept")
        qk_hi_made = sem("qk_hi_made")
        qk_split = sem("qk_split")
        arg_made = sem("arg_made")
        decay_made = sem("decay_made")
        decay_masked = sem("decay_masked")
        v_hi_made = sem("v_hi_made")
        scored = sem("scored")
        p_made = sem("p_made")
        p_hi_made = sem("p_hi_made")
        p_split = sem("p_split")
        pv_done = sem("pv_done")
        gate_open = sem("gate_open")
        den_made = sem("den_made")
        den_sq = sem("den_sq")
        num_sq = sem("num_sq")
        num_added = sem("num_added")
        head_summed = sem("head_summed")
        var_made = sem("var_made")
        head_std = sem("head_std")
        head_rstd = sem("head_rstd")
        gate_scaled = sem("gate_scaled")
        y_made = sem("y_made")
        y_hi_made = sem("y_hi_made")
        y_split = sem("y_split")

        pads_zeroed = sem("pads_zeroed")
        g_made = sem("g_made")
        tap2 = sem("tap2")
        tap1 = sem("tap1")
        tap0 = sem("tap0")
        silu_made = sem("silu_made")
        silu_scaled = sem("silu_scaled")
        hid_hi_made = sem("hid_hi_made")
        hid_split = sem("hid_split")

        q_done = sem("q_done")
        dscored = sem("dscored")
        maxed = sem("maxed")
        exped = sem("exped")
        sum_inv = sem("sum_inv")
        sum_coef = sem("sum_coef")
        p0_scaled = sem("p0_scaled")
        a_made = sem("a_made")
        pT_turned = sem("pT_turned")
        pT_hi_made = sem("pT_hi_made")
        pT_split = sem("pT_split")
        vh_hi_made = sem("vh_hi_made")
        vh_split = sem("vh_split")
        dqk_hi_made = sem("dqk_hi_made")
        dqk_split = sem("dqk_split")
        dpv_done = sem("dpv_done")
        o_sq = sem("o_sq")
        o_summed = sem("o_summed")
        o_ln = sem("o_ln")
        o_rstd = sem("o_rstd")
        o_made = sem("o_made")
        o_hi_made = sem("o_hi_made")
        o_split = sem("o_split")

        fin_summed = sem("fin_summed")
        fin_std = sem("fin_std")
        fin_rstd = sem("fin_rstd")
        fin_turned = [sem("fin_turned_first"), sem("fin_turned_second")]
        fin_scaled_a = sem("fin_scaled_a")
        fin_scaled_v = sem("fin_scaled_v")
        out_stored = sem("out_stored")

        block = es.enter_context(nc.Block())

        w_in = mlstm_w_in[0].rearrange("(t p) n -> p t n", p=P)
        w_outA = mlstm_w_out[0].rearrange("(t p) n -> p t n", p=P)
        w_kvr = w_kv.rearrange("(t p) n -> p t n", p=P)
        w_q = diff_w_q[0].rearrange("(t p) n -> p t n", p=P)
        w_outB = diff_w_out[0].rearrange("(t p) n -> p t n", p=P)
        w_up = [ffn_w_up[l].rearrange("(t p) n -> p t n", p=P) for l in range(2)]
        w_down = [ffn_w_down[l].rearrange("(t p) n -> p t n", p=P) for l in range(2)]

        def cols(w, t, c):
            return w[:, 0:t * c].rearrange("p (t c) -> p t c", t=t)

        @block.sync
        def _(sp):
            def free_slot(u, peeled=False):
                if not peeled:
                    sp.wait_ge(w_split, u - 1)

            def load_pair(u, s, left, right, peeled=False):
                free_slot(u, peeled)
                d = cols(wraw[:, s, :], KT, 2 * P)
                sp.dma_start(d[:, :, 0:P], left).then_inc(slot_loaded[s], 16)
                sp.dma_start(d[:, :, P:2 * P], right).then_inc(slot_loaded[s], 16)

            def load_block(u, s, src, peeled=False):
                free_slot(u, peeled)
                t, c = src.shape[1], src.shape[2]
                d = cols(wraw[:, s, :], t, c)
                sp.dma_start(d[:, 0:t // 2, :], src[:, 0:t // 2, :]).then_inc(slot_loaded[s], 16)
                sp.dma_start(d[:, t // 2:t, :], src[:, t // 2:t, :]).then_inc(slot_loaded[s], 16)

            def load_rows():
                for n, src in enumerate((diff_lambda_q1, diff_lambda_k1, diff_lambda_q2, diff_lambda_k2)):
                    sp.dma_start(lam_in[0:1, n, :], src).then_inc(rows_loaded, 16)
                for l in range(2):
                    sp.dma_start(conv_rows[0:3 * FT, l, :],
                                 ffn_conv_w[l].rearrange("w (t p) -> (w t) p", p=P)).then_inc(rows_loaded, 16)
                    sp.dma_start(conv_rows[3 * FT:4 * FT, l, :],
                                 ffn_conv_b[l].rearrange("(t p) -> t p", p=P)).then_inc(rows_loaded, 16)

            def load_head(h, first=False):
                u = 4 * h
                load_pair(u, 0, w_in[:, :, bass.ds(h * DKA, P)],
                          w_in[:, :, bass.ds(h * DKA + HA * DKA, P)], first)
                load_block(u + 1, 1, w_in[:, :, bass.ds(h * DVA + 2 * HA * DKA, DVA)], first)
                if first:
                    load_rows()
                for v in range(2):
                    load_block(u + 2 + v, v, w_in[:, :, bass.ds(h * DVA + 2 * HA * DKA + HA * DVA + v * P, P)])

            def load_ffn(l):
                u0 = U_FFN[l]
                for k0, n in HALVES:
                    with by_two(sp, 0, n) as i:
                        for s in range(2):
                            load_pair(i + (u0 + s), s, w_up[l][:, :, bass.ds((i + (k0 + s)) * P, P)],
                                      w_up[l][:, :, bass.ds((i + (k0 + s)) * P + DFF, P)])
                    u0 += n
                    with by_two(sp, 0, KT) as j:
                        for s in range(2):
                            load_block(j + (u0 + s), s, w_down[l][:, k0:k0 + n, bass.ds((j + s) * P, P)])
                    u0 += KT

            xr = x[0].rearrange("(b p) d -> p b d", p=P)
            gains = (attn_norm_g.rearrange("l (t p) -> (l t) p", p=P),
                     ffn_norm_g.rearrange("l (t p) -> (l t) p", p=P),
                     kv_norm_g.rearrange("(t p) -> t p", p=P),
                     final_norm_g.rearrange("(t p) -> t p", p=P),
                     mlstm_head_g[0].rearrange("h (t p) -> (h t) p", p=P),
                     diff_subln_g)
            row = 0
            for b in range(TB):
                sp.dma_start(x_in[:, b, :], xr[:, b, :]).then_inc(x_loaded[b], 16)
                for g in gains[2 * b:2 * b + 2]:
                    sp.dma_start(gain_rows[row:row + g.shape[0], :], g).then_inc(gains_loaded, 16)
                    row += g.shape[0]
            load_head(0, first=True)
            with sp.Fori(1, HA) as h:
                load_head(h)
            for m in range(KT // 2):
                load_block(U_OUTA + m, m % 2, w_outA[:, :, m * 2 * P:(m + 1) * 2 * P])
            load_ffn(0)
            for m in range(4):
                load_block(U_V + m, m % 2, w_kvr[:, :, D + m * 2 * P:D + (m + 1) * 2 * P])
            with by_two(sp, 0, HB) as h:
                for s in range(2):
                    load_pair(h + (U_QK + s), s, w_q[:, :, bass.ds((h + s) * P, P)],
                              w_kvr[:, :, bass.ds((h + s) * P, P)])
            for m in range(KT // 2):
                load_block(U_OUTB + m, m % 2, w_outB[:, :, m * 2 * P:(m + 1) * 2 * P])
            load_ffn(1)
            outr = out[0].rearrange("(b p) (a d) -> b a p d", p=P, a=2)
            for n in range(TB):
                for a in range(2):
                    b = FIN_BLOCKS[n] if a else n
                    sp.wait_ge(fin_scaled_v if a else fin_scaled_a, n + 1)
                    sp.dma_start(outr[b, a], o_sb[:, b, a * 512:(a + 1) * 512]).then_inc(out_stored, 16)
            sp.wait_ge(out_stored, 16 * 2 * TB)

        @block.gpsimd
        def _(pool):
            pool.memset(ident[:, :], 0.0).then_inc(const_made, 1)
            pool.memset(onesf[:, :], 1.0).then_inc(const_made, 1)
            pool.memset(ident_b[:, :], 0.0).then_inc(const_made, 1)
            pool.memset(mask_b[:, :], 0.0).then_inc(const_made, 1)
            pool.memset(eps[:, :], EPS).then_inc(const_made, 1)
            pool.memset(coef[:, :], 1.0).then_inc(const_made, 1)
            pool.memset(bgate[:, :], 0.0).then_inc(bg_zeroed, 1)
            pool.memset(mixF[:, 4608:5632], 0.0).then_inc(wg_zeroed, 1)
            pool.wait_ge(const_made, 6)
            pool.affine_select(out=ident[:, :], in_=ident[:, :], compare_op=ALU.not_equal, fill=1.0,
                               base=0, pattern=[[-1, P]], channel_multiplier=1).then_inc(const_made, 1)
            pool.affine_select(out=ident_b[:, :], in_=ident_b[:, :], compare_op=ALU.not_equal, fill=1.0,
                               base=0, pattern=[[-1, P]], channel_multiplier=1).then_inc(const_made, 1)
            pool.affine_select(out=mask_b[:, :], in_=mask_b[:, :], compare_op=ALU.is_ge, fill=MASKED,
                               base=0, pattern=[[-1, P]], channel_multiplier=1).then_inc(const_made, 1)
            pool.affine_select(out=tri[:, :], in_=onesf[:, :], compare_op=ALU.is_ge, fill=0.0,
                               base=0, pattern=[[1, P]], channel_multiplier=-1).then_inc(const_made, 1)

            def add_squares(s, j):
                n = 8 * s + j
                pool.wait_ge(sq_made, n + 1)
                if j == 0:
                    if s:
                        pool.wait_ge(norm_summed, s)
                    pool.tensor_copy(sqacc[:, :], sq[:, 0, :]).then_inc(sq_added, 1)
                else:
                    pool.wait_ge(sq_added, n)
                    pool.tensor_tensor(sqacc[:, :], sqacc[:, :], sq[:, j % 2, :], ALU.add)\
                        .then_inc(sq_added, 1)

            def head(h, first=False):
                pool.wait_ge(decay_made, h + 1)
                for j in range(TB):
                    d = decay[:, OFF[j]:OFF[j] + P]
                    pool.tensor_tensor(d, d, tri[:, :], ALU.mult).then_inc(decay_masked, 1)
                pool.wait_ge(num_sq, 2 * h + 2)
                pool.tensor_tensor(num0, num0, num1, ALU.add).then_inc(num_added, 1)
                pool.wait_ge(gate_open, 2 * h + 2)
                pool.wait_ge(head_rstd, h + 1)
                for v in range(2):
                    pool.tensor_tensor(gates[v], gates[v], den, ALU.mult).then_inc(gate_scaled, 1)
                for v in range(2):
                    pool.wait_ge(y_hi_made, 2 * h + v + 1)
                    t = h * 2 + v
                    pool.tensor_tensor(h_lo[:, t, :], numsq[v], f32(h_hi[:, t, :]), ALU.subtract)\
                        .then_inc(y_split, 1)

            def ffn_up(i, f0, s):
                f = i + (f0 + s)
                pool.wait_ge(silu_made, f + 1)
                pool.tensor_tensor(act_o[:, s, :], act_o[:, s, :], rstd[:, :], ALU.mult)\
                    .then_inc(silu_scaled, 1)
                pool.wait_ge(hid_hi_made, f + 1)
                pool.tensor_tensor(h_lo[:, i + s, :], hid[:, s, :], f32(h_hi[:, i + s, :]), ALU.subtract)\
                    .then_inc(hid_split, 1)

            def scale_unit(u, s, gl, gr):
                pool.wait_ge(slot_loaded[s], (u - s) * 16 + 32)
                d = cols(wraw[:, s, :], KT, 2 * P)
                for side, g in enumerate((gl, gr)):
                    half = d[:, :, side * P:(side + 1) * P]
                    pool.tensor_tensor(half, half, gainT[:, g:g + KT].unsqueeze(2).broadcast_to([P, KT, P]),
                                       ALU.mult).then_inc(w_scaled, 1)

            def ffn(l):
                for n_half, (k0, n) in enumerate(HALVES):
                    with by_two(pool, 0, n) as i:
                        for s in range(2):
                            ffn_up(i, l * FT + k0, s)
                for j in range(KT):
                    if l == 0 and j >= KT - 2:
                        scale_unit(U_V + j - (KT - 2), j % 2, G_KV, G_KV)
                    if (l, j) != (1, KT - 1):
                        add_squares(S_FFN[l] + 1, j)

            for j in range(KT):
                add_squares(0, j)
            head(0, first=True)
            with pool.Fori(1, HA) as h:
                head(h)
            for j in range(KT):
                add_squares(1, j)
            ffn(0)
            for m in range(2, 4):
                scale_unit(U_V + m, m % 2, G_KV, G_KV)

            def attn_o_lo(h):
                pool.wait_ge(o_hi_made, h + 1)
                pool.tensor_tensor(h_lo[:, h, :], ytmp[:, :], f32(h_hi[:, h, :]), ALU.subtract)\
                    .then_inc(o_split, 1)

            def vh_lo_made(h):
                pool.wait_ge(vh_hi_made, h + 1)
                pool.tensor_tensor(vh_lo, v_all[:, :, bass.ds(h * P, P)], f32(vh_hi), ALU.subtract)\
                    .then_inc(vh_split, 1)

            scale_unit(U_QK, 0, G_Q, G_KV)
            scale_unit(U_QK + 1, 1, G_Q, G_KV)
            vh_lo_made(0)

            scale_unit(U_QK + 2, 0, G_Q, G_KV)

            def weights_lo(u, s):
                pool.wait_ge(w_hi_made, u + 1)
                pool.tensor_tensor(w_lo[:, s, :], wraw[:, s, :], f32(w_hi[:, s, :]), ALU.subtract)\
                    .then_inc(w_split, 1)

            def attn(h, s, scale=True, nxt=True, prev=True):
                weights_lo(h + (U_QK + 2), 1 - s)
                if prev:
                    attn_o_lo(h - 1)
                if scale:
                    scale_unit(h + (U_QK + 3), s, G_Q, G_KV)
                if nxt:
                    vh_lo_made(h + 1)

            attn(0, 1, prev=False)
            with by_two(pool, 1, HB - 3) as h:
                attn(h, 0)
                attn(h + 1, 1)
            attn(HB - 3, 0, scale=False)
            attn(HB - 2, 1, scale=False)
            attn(HB - 1, 0, scale=False, nxt=False)
            attn_o_lo(HB - 1)
            for j in range(KT):
                add_squares(3, j)
            ffn(1)

        @block.scalar
        def _(act):
            act.wait_ge(bg_zeroed, 1)
            act.wait_ge(wg_zeroed, 1)
            wg = w_in[:, :, 2 * HA * (DKA + DVA):]
            bg = mlstm_b_gate.rearrange("a n -> n a")
            for r, c in ((0, 0), (32, HA)):
                act.dma_start(wg_raw[:, :, r:r + HA], wg[:, :, c:c + HA]).then_inc(wg_loaded, 16)
                act.dma_start(bgate[r:r + HA, 0:1], bg[c:c + HA, :]).then_inc(wg_loaded, 16)

            def weights_hi(u, s, scaled=None):
                if scaled is None:
                    act.wait_ge(slot_loaded[s], (u - s) * 16 + 32)
                else:
                    act.wait_ge(w_scaled, scaled)
                if not isinstance(u, int) or u >= 2:
                    act.wait_ge(unit_done, u - 1)
                act.activation(w_hi[:, s, :], wraw[:, s, :], ACT.Copy).then_inc(w_hi_made, 1)

            def split_x(s, j):
                n = 8 * s + j
                if s == 0:
                    act.wait_ge(x_kept, j + 1)
                g = G_STAGE.get(s)
                if n == 8 * 5 - 1:
                    act.wait_ge(sq_added, n - 1)
                    act.activation(sq[:, j % 2, :], xT[:, j, :], ACT.Square).then_inc(sq_made, 1)
                dst = xg_fin if s == 4 else xs_hi
                act.activation(dst[:, j, :], xT[:, j, :], ACT.Copy,
                               scale=1.0 if g is None else gainT[:, g + j:g + j + 1]).then_inc(xs_hi_made, 1)
                if n == 8 * 5 - 1:
                    return
                if n >= 2:
                    act.wait_ge(sq_added, n - 1)
                act.activation(sq[:, j % 2, :], xT[:, j, :], ACT.Square).then_inc(sq_made, 1)

            def norm_std(s):
                act.wait_ge(norm_summed, s + 1)
                act.activation(sq[:, 0, :], ps[:, 7, :], ACT.Sqrt, scale=1.0 / D, bias=eps[:, :])\
                    .then_inc(std_made, 1)

            act.wait_ge(const_made, 10)
            act.activation(ones_r[:, :], onesf[:, :], ACT.Copy).then_inc(ones_r_made, 1)
            act.wait_ge(gains_kept, 1)
            for j in range(W_AT):
                split_x(0, j)
                if j == 0:
                    act.wait_ge(wg_loaded, 64)
                    act.activation(wg_hi, wg_raw, ACT.Copy).then_inc(wg_hi_made, 1)
                    act.mul(bgate[:, 1:2], bgate[:, 0:1], 1.0 / SOFTCAP).then_inc(bg_scaled, 1)
            weights_hi(0, 0)
            for j in range(W_AT, KT):
                split_x(0, j)
            weights_hi(1, 1)
            norm_std(0)
            act.wait_ge(lam_dve, 2)
            act.activation(lam_w[:, 4:6], lam_w[:, 2:4], ACT.Exp).then_inc(lam_exp, 1)
            act.wait_ge(gate_z, 1)
            act.wait_ge(bg_scaled, 1)
            act.activation(g_t, g_z, ACT.Tanh, scale=1.0 / SOFTCAP, bias=bgate[0:36, 1:2])\
                .then_inc(gate_act, 1)
            act.wait_ge(gate_act, 1)
            act.activation(g_e[32:36, :], g_t[32:36, :], ACT.Exp, scale=-SOFTCAP).then_inc(gate_act, 1)
            act.wait_ge(gate_act, 2)
            act.activation(g_e[32:36, :], g_e[32:36, :], ACT.Ln, bias=1.0).then_inc(gate_act, 1)
            act.wait_ge(gate_scan, 4)
            act.activation(rowsM[:, S:2 * S], g_z[0:HA, :], ACT.Exp).then_inc(rows_made, 1)

            def head(h, first=False):
                u = 4 * h
                for n, t in enumerate((tq, tk)):
                    act.wait_ge(evacuated, 8 * h + 1 + n)
                    act.activation(qk_hi[n], t, ACT.Copy).then_inc(qk_hi_made, 1)
                if first:
                    weights_hi(u + 2, 0)
                act.wait_ge(arg_made, 4 * h + 4)
                act.activation(decay, decay, ACT.Exp).then_inc(decay_made, 1)
                act.wait_ge(m_spread, 2 * h + 2)
                act.activation(floor, ps[:, 6, :], ACT.Square, scale=math.sqrt(EPS)).then_inc(floor_kept, 1)
                if not first:
                    weights_hi(u + 2, 0)
                act.wait_ge(p_made, 4 * h + 4)
                act.activation(p_hi, pw, ACT.Copy).then_inc(p_hi_made, 1)
                act.wait_ge(unit_done, u + 2)
                act.wait_ge(rcol_made, 1)
                for b in range(TB):
                    act.activation(v_hi[:, b, :], ps[:, 2 + b // 2, (b % 2) * DVA:(b % 2 + 1) * DVA], ACT.Copy,
                                   scale=rcol[:, b:b + 1]).then_inc(v_hi_made, 1)
                weights_hi(u + 3, 1)
                act.wait_ge(evacuated, 8 * h + 7)
                act.activation(gate0, gate0, ACT.Sigmoid).then_inc(gate_open, 1)
                weights_hi(u + 4, 0)
                if not first:
                    act.wait_ge(y_split, 2 * h)
                for v in range(2):
                    act.wait_ge(pv_done, 3 * h + v + 1)
                    act.activation(numsq[v], ps[:, 4 + v, :], ACT.Square).then_inc(num_sq, 1)
                act.wait_ge(pv_done, 3 * h + 3)
                act.activation(den, ps[:, 6, :], ACT.Square, scale=math.sqrt(EPS)).then_inc(den_sq, 1)
                act.wait_ge(evacuated, 8 * h + 8)
                act.activation(gate1, gate1, ACT.Sigmoid).then_inc(gate_open, 1)
                act.wait_ge(var_made, h + 1)
                act.activation(var, var, ACT.Sqrt).then_inc(head_std, 1)
                weights_hi(u + 5, 1)
                for v in range(2):
                    act.wait_ge(y_made, 2 * h + v + 1)
                    act.activation(h_hi[:, h * 2 + v, :], numsq[v], ACT.Copy).then_inc(y_hi_made, 1)

            def out_proj(u0, e0, s):
                for m in range(KT // 2):
                    if m < KT // 2 - 1:
                        weights_hi(u0 + m + 2, m % 2)
                    for t in range(2):
                        act.wait_ge(evacuated, e0 + 2 * m + t + 1)
                        split_x(s, 2 * m + t)
                    if m == KT // 2 - 1:
                        weights_hi(u0 + m + 2, m % 2)

            def ffn(l):
                u0, e0, f0 = U_FFN[l], E_FFN[l], l * FT
                for n_half, (k0, n) in enumerate(HALVES):
                    def up(i, s, norm=False):
                        u, f = i + (u0 + s), i + (f0 + s)
                        if norm:
                            norm_std(S_FFN[l])
                        c = i + (k0 + s)
                        if norm:
                            weights_hi(u + 2, s)
                        act.wait_ge(g_made, f + 1)
                        act.activation(cv[:, s, :], gpad[:, s, 2:S + 2], ACT.Identity,
                                       scale=convT[:, l, bass.ds(c + 2 * FT, 1)],
                                       bias=convT[:, l, bass.ds(c + 3 * FT, 1)]).then_inc(tap2, 1)
                        if not norm:
                            weights_hi(u + 2, s)
                        act.wait_ge(tap0, f + 1)
                        act.activation(act_o[:, s, :], cv[:, s, :], ACT.Silu).then_inc(silu_made, 1)
                        act.wait_ge(evacuated, i + (e0 + s) + 1)
                        act.activation(h_hi[:, i + s, :], hid[:, s, :], ACT.Copy).then_inc(hid_hi_made, 1)

                    first = 0
                    if n_half == 0:
                        up(0, 0, norm=True)
                        up(0, 1)
                        first = 2
                    with by_two(act, first, n) as i:
                        up(i, 0)
                        up(i, 1)
                    u0, e0, f0 = u0 + n, e0 + n, f0 + n

                    def down(j, s, scaled=None):
                        u = j + (u0 + s)
                        last = n_half == 1 and j + s == KT - 1
                        prepare = not (isinstance(u, int) and u + 2 >= U_END)
                        if prepare and not last:
                            weights_hi(u + 2, s, scaled)
                        if n_half == 1:
                            act.wait_ge(evacuated, j + (e0 + s) + 1)
                            split_x(S_FFN[l] + 1, j + s)
                        if prepare and last:
                            weights_hi(u + 2, s, scaled)

                    if n_half == 0:
                        with by_two(act, 0, KT) as j:
                            down(j, 0)
                            down(j, 1)
                    else:
                        for j in range(0, KT, 2):
                            for s in range(2):
                                down(j, s, 2 * (s + 1) if l == 0 and j == KT - 2 else None)
                    u0, e0 = u0 + KT, e0 + KT

            head(0, first=True)
            with act.Fori(1, HA) as h:
                head(h)
            out_proj(U_OUTA, E_OUTA, 1)
            ffn(0)

            for m in range(4):
                if m == 0:
                    norm_std(2)
                weights_hi(U_V + m + 2, m % 2, 2 * (m + 3))

            def attn_qk_hi(h, n):
                act.wait_ge(evacuated, 2 * h + (E_QK + n + 1))
                act.activation(qk_hi[n], tqk[n], ACT.Copy).then_inc(dqk_hi_made, 1)

            def attn_v_hi(h):
                act.activation(vh_hi, v_all[:, :, bass.ds(h * P, P)], ACT.Copy).then_inc(vh_hi_made, 1)

            def attn_exp(h, k, first):
                w = (TB - k) * P
                for c in range(2):
                    act.wait_ge(maxed, 8 * h + (2 * k + c + 1))
                    if not (first and k < 2):
                        act.wait_ge(pT_turned, 4 * h + (k - 1))
                    act.activation(prob[:, k % 2, c, 0:w], ps[:, 2 + (k % 2) * 2 + c, 0:w],
                                   ACT.Exp, bias=nmax[:, k % 2, c:c + 1],
                                   accum_out=lsum[:, k % 2, c:c + 1]).then_inc(exped, 1)

            def attn_pT_hi(h, k):
                i = TB - 1 - k
                act.wait_ge(pT_turned, 4 * h + (k + 1))
                act.activation(pT_hi[:, 0:i + 1, i * P:(i + 1) * P],
                               ps[:, 6, 0:(i + 1) * P].rearrange("p (j c) -> p j c", c=P), ACT.Copy)\
                    .then_inc(pT_hi_made, 1)

            def attn_ln(h):
                act.wait_ge(o_summed, h + 1)
                act.activation(sq[:, 1, :], ps[:, 6, :], ACT.Ln, scale=1.0 / P, bias=eps[:, :])\
                    .then_inc(o_ln, 1)

            def attn_rstd(h):
                act.wait_ge(o_ln, h + 1)
                act.activation(sqacc[:, :], sq[:, 1, :], ACT.Exp, scale=-0.5).then_inc(o_rstd, 1)

            def attn_o_hi(h):
                act.wait_ge(o_made, h + 1)
                act.activation(h_hi[:, h, :], ytmp[:, :], ACT.Copy).then_inc(o_hi_made, 1)

            def attn(h, s, scaled, prev=True, nxt=True):
                weights_hi(h + (U_QK + 2), s, scaled)
                attn_exp(h, 0, not prev)
                attn_exp(h, 1, not prev)
                if prev:
                    attn_ln(h - 1)
                attn_pT_hi(h, 0)
                if prev:
                    attn_rstd(h - 1)
                attn_pT_hi(h, 1)
                attn_exp(h, 2, not prev)
                if prev:
                    attn_o_hi(h - 1)
                attn_exp(h, 3, not prev)
                attn_pT_hi(h, 2)
                if nxt:
                    attn_qk_hi(h + 1, 0)
                attn_pT_hi(h, 3)
                if nxt:
                    attn_qk_hi(h + 1, 1)
                act.wait_ge(dpv_done, h + 1)
                act.activation(sq[:, 0, :], ps[:, 7, :], ACT.Square).then_inc(o_sq, 1)
                if nxt:
                    attn_v_hi(h + 1)

            SC = 2 * 4
            act.wait_ge(evacuated, E_QK)
            attn_v_hi(0)
            attn_qk_hi(0, 0)
            attn_qk_hi(0, 1)
            attn(0, 0, SC + 2 * 3, prev=False)
            with by_two(act, 1, HB - 3) as h:
                attn(h, 1, 2 * h + (SC + 6))
                attn(h + 1, 0, 2 * h + (SC + 8))
            attn(HB - 3, 1, SC + 2 * HB)
            attn(HB - 2, 0, None)
            attn(HB - 1, 1, None, nxt=False)
            attn_ln(HB - 1)
            attn_rstd(HB - 1)
            attn_o_hi(HB - 1)
            out_proj(U_OUTB, E_OUTB, 3)
            ffn(1)

            act.wait_ge(fin_summed, 1)
            act.activation(rcol[:, :], ps[:, 5, 0:TB], ACT.Sqrt, scale=1.0 / D, bias=eps[:, :])\
                .then_inc(fin_std, 1)
            act.wait_ge(fin_rstd, 1)
            for b in range(TB):
                act.wait_ge(fin_turned[0], b + 1)
                act.activation(o_sb[:, b, 0:512], ps[:, 2 * b, :], ACT.Copy, scale=rcol[:, b:b + 1])\
                    .then_inc(fin_scaled_a, 1)

        @block.vector
        def _(dve):
            dve.wait_ge(gains_turned, 1)
            dve.tensor_copy(gainT[:, :], ps[:, 4, 0:57]).then_inc(gains_kept, 1)
            dve.wait_ge(gains_kept, 1)

            def weights_lo(u, s):
                dve.wait_ge(w_hi_made, u + 1)
                dve.tensor_tensor(w_lo[:, s, :], wraw[:, s, :], f32(w_hi[:, s, :]), ALU.subtract)\
                    .then_inc(w_split, 1)

            def split_x(s, j):
                n = 8 * s + j
                g = G_STAGE.get(s)
                dve.wait_ge(xs_hi_made, n + 1)
                if g is None:
                    dve.tensor_tensor(xs_lo[:, j, :], xT[:, j, :], f32(xs_hi[:, j, :]), ALU.subtract)\
                        .then_inc(x_split, 1)
                else:
                    dve.scalar_tensor_tensor(out=xs_lo[:, j, :], in0=xT[:, j, :], scalar=gainT[:, g + j:g + j + 1],
                                             in1=f32(xs_hi[:, j, :]), op0=ALU.mult, op1=ALU.subtract)\
                        .then_inc(x_split, 1)

            def norm_rstd(s):
                dve.wait_ge(std_made, s + 1)
                dve.reciprocal(rstd[:, :], sq[:, 0, :]).then_inc(rstd_made, 1)

            for j in range(KT):
                dve.wait_ge(x_turned, j + 1)
                dve.tensor_copy(xT[:, j, :], ps[:, X_BANK[j], :]).then_inc(x_kept, 1)
                if j:
                    split_x(0, j - 1)
                if j == 1:
                    dve.wait_ge(wg_hi_made, 1)
                    dve.tensor_tensor(wg_lo, wg_raw, f32(wg_hi), ALU.subtract).then_inc(wg_split, 1)
                if j == W_AT:
                    weights_lo(0, 0)
            split_x(0, KT - 1)
            weights_lo(1, 1)
            def queries_keys(h):
                dve.wait_ge(unit_done, 4 * h + 1)
                dve.scalar_tensor_tensor(out=tq, in0=ps[:, 0, :], scalar=DKA ** -0.5, in1=rstd[:, :],
                                         op0=ALU.mult, op1=ALU.mult).then_inc(evacuated, 1)
                dve.tensor_tensor(tk, ps[:, 1, :], rstd[:, :], ALU.mult).then_inc(evacuated, 1)

            dve.wait_ge(rows_loaded, 16 * 8)
            dve.tensor_tensor(ytmp[0:1, 0:2 * HDB].rearrange("p (a c) -> p a c", a=2),
                              lam_in[:, 0:4:2, :], lam_in[:, 1:4:2, :], ALU.mult).then_inc(lam_dve, 1)
            dve.wait_ge(lam_dve, 1)
            dve.tensor_reduce(lam_w[:, 2:4], ytmp[0:1, 0:2 * HDB].rearrange("p (a c) -> p a c", a=2),
                              AX.X, ALU.add).then_inc(lam_dve, 1)
            norm_rstd(0)
            dve.wait_ge(gate_mm, 1)
            dve.wait_ge(rstd_made, 1)
            dve.tensor_tensor(g_z, ps[0:36, 5, :], rstd[0:36, :], ALU.mult).then_inc(gate_z, 1)
            dve.wait_ge(lam_exp, 1)
            dve.tensor_tensor(lam_w[:, 6:7], lam_w[:, 5:6], lam_w[:, 4:5], ALU.subtract).then_inc(lam_dve, 1)
            dve.wait_ge(lam_dve, 3)
            dve.tensor_scalar(lam_w[:, 7:8], lam_w[:, 6:7], -LAM_INIT, None, ALU.add).then_inc(lam_dve, 1)
            dve.tensor_scalar(gainT[:, G_SUB:G_SUB + 1], gainT[:, G_SUB:G_SUB + 1], 1.0 - LAM_INIT, None,
                              ALU.mult).then_inc(sub_scaled, 1)
            dve.wait_ge(rows_turned, 2)
            for l in range(2):
                dve.tensor_copy(convT[:, l, :], ps[:, 4, 64 + 96 * l:64 + 96 * l + 4 * FT])\
                    .then_inc(rows_kept, 1)
            queries_keys(0)
            dve.wait_ge(gate_act, 3)
            dve.tensor_tensor_scan(g_L[0:HA, :], g_e[32:36, :], g_e[32:36, :], 0.0, ALU.add, ALU.max)\
                .then_inc(gate_scan, 1)
            dve.wait_ge(gate_scan, 1)
            dve.scalar_tensor_tensor(out=g_a[0:HA, :], in0=g_t[0:HA, :], scalar=SOFTCAP, in1=g_L[0:HA, :],
                                     op0=ALU.mult, op1=ALU.add).then_inc(gate_scan, 1)
            dve.wait_ge(gate_scan, 2)
            dve.tensor_tensor_scan(g_M[0:HA, :], g_a[0:HA, :], g_a[0:HA, :], 0.0, ALU.max, ALU.max)\
                .then_inc(gate_scan, 1)
            dve.wait_ge(gate_scan, 3)
            dve.tensor_tensor(g_z[0:HA, :], g_L[0:HA, :], g_M[0:HA, :], ALU.subtract).then_inc(gate_scan, 1)
            dve.tensor_scalar(rowsM[:, 0:S], g_M[0:HA, :], -1.0, None, ALU.mult).then_inc(gate_scan, 1)
            dve.wait_ge(rows_made, 1)
            dve.wait_ge(gate_scan, 5)

            def pick(h):
                one = ident[0:HA, bass.ds(h, 1)]
                dve.tensor_scalar(p_hi[0:HA, 0:2 * S], rowsM[:, :], one, None, ALU.mult).then_inc(m_picked, 1)
                dve.wait_ge(m_picked, 2 * h + 1)
                dve.scalar_tensor_tensor(out=p_lo[0:HA, 0:2 * S], in0=rowsM[:, :], scalar=one,
                                         in1=f32(p_hi[0:HA, 0:2 * S]), op0=ALU.mult, op1=ALU.subtract)\
                    .then_inc(m_picked, 1)

            def head(h, first=False, last=False):
                u = 4 * h
                if not first:
                    queries_keys(h)
                if first:
                    dve.wait_ge(rcol_turned, 1)
                    dve.tensor_copy(rcol[:, :], ps[:, 4, 0:TB]).then_inc(rcol_made, 1)
                    dve.wait_ge(lam_spread, 1)
                    dve.tensor_copy(coef[:, 1:2], ps[:, 4, 32:33]).then_inc(lam_kept, 1)
                    dve.wait_ge(a_turned, 1)
                    dve.tensor_copy(acol[:, :], ps[:, 5, 0:4 * HA]).then_inc(acol_made, 1)
                    dve.wait_ge(acol_made, 1)
                    dve.wait_ge(rcol_made, 1)
                else:
                    dve.wait_ge(p_made, 4 * h)
                dve.wait_ge(m_spread, 2 * h + 1)
                for j in range(TB):
                    dve.tensor_scalar(decay[:, OFF[j]:OFF[j] + S - j * P], ps[:, 7, j * P:S],
                                      acol[:, bass.ds(h + HA * j, 1)], 0.0, ALU.add, ALU.min)\
                        .then_inc(arg_made, 1)
                for n, t in enumerate((tq, tk)):
                    dve.wait_ge(qk_hi_made, 2 * h + n + 1)
                    dve.tensor_tensor(qk_lo[n], t, f32(qk_hi[n]), ALU.subtract).then_inc(qk_split, 1)
                if first:
                    weights_lo(u + 2, 0)
                dve.wait_ge(decay_masked, 4 * h + 4)
                dve.wait_ge(m_spread, 2 * h + 2)
                for j in range(TB):
                    dve.wait_ge(scored, 4 * h + (j + 1 if j < 2 else 4))
                    src = ps[:, 4 + j, 0:S - j * P] if j < 3 else ps[:, 6, 2 * P:3 * P]
                    dve.tensor_tensor(pw[:, OFF[j]:OFF[j] + S - j * P], src,
                                      decay[:, OFF[j]:OFF[j] + S - j * P], ALU.mult).then_inc(p_made, 1)
                if not first:
                    weights_lo(u + 2, 0)
                dve.wait_ge(p_hi_made, h + 1)
                dve.tensor_tensor(p_lo, pw, f32(p_hi), ALU.subtract).then_inc(p_split, 1)
                for b in range(TB):
                    dve.wait_ge(v_hi_made, 4 * h + (b // 2 * 2 + 2))
                    dve.scalar_tensor_tensor(out=v_lo[:, b, :],
                                             in0=ps[:, 2 + b // 2, (b % 2) * DVA:(b % 2 + 1) * DVA],
                                             scalar=rcol[:, b:b + 1], in1=f32(v_hi[:, b, :]),
                                             op0=ALU.mult, op1=ALU.subtract).then_inc(evacuated, 1)
                weights_lo(u + 3, 1)
                dve.wait_ge(unit_done, u + 3)
                dve.tensor_tensor(gate0, ps[:, 0, :], rstd[:, :], ALU.mult).then_inc(evacuated, 1)
                weights_lo(u + 4, 0)
                dve.wait_ge(den_sq, h + 1)
                dve.tensor_tensor(den, den, floor, ALU.max).then_inc(den_made, 1)
                if not last:
                    dve.wait_ge(pv_done, 3 * h + 3)
                    pick(h + 1)
                dve.wait_ge(unit_done, u + 4)
                dve.tensor_tensor(gate1, ps[:, 2, :], rstd[:, :], ALU.mult).then_inc(evacuated, 1)
                dve.wait_ge(head_summed, h + 1)
                dve.wait_ge(den_made, h + 1)
                dve.scalar_tensor_tensor(out=var, in0=ps[:, 7, :], scalar=1.0 / DVA, in1=den,
                                         op0=ALU.mult, op1=ALU.add).then_inc(var_made, 1)
                dve.wait_ge(head_std, h + 1)
                dve.reciprocal(den, var).then_inc(head_rstd, 1)
                weights_lo(u + 5, 1)
                for v in range(2):
                    dve.wait_ge(gate_scaled, 2 * h + v + 1)
                    dve.scalar_tensor_tensor(out=numsq[v], in0=ps[:, 4 + v, :],
                                             scalar=gainT[:, bass.ds(h * 2 + (G_HEAD + v), 1)], in1=gates[v],
                                             op0=ALU.mult, op1=ALU.mult).then_inc(y_made, 1)

            def add_x(tile, bank, wait_u):
                dve.wait_ge(unit_done, wait_u)
                dve.tensor_tensor(xT[:, tile, :], xT[:, tile, :], ps[:, bank, :], ALU.add)\
                    .then_inc(evacuated, 1)

            def out_proj(u0, s):
                for m in range(KT // 2):
                    for t in range(2):
                        add_x(2 * m + t, 2 * (m % 2) + t, u0 + m + 1)
                    if m < KT // 2 - 1:
                        weights_lo(u0 + m + 2, m % 2)
                    for t in range(2):
                        split_x(s, 2 * m + t)
                    if m == KT // 2 - 1:
                        weights_lo(u0 + m + 2, m % 2)

            def ffn(l):
                u0, f0 = U_FFN[l], l * FT
                dve.memset(gpad[:, :, 0:2], 0.0).then_inc(pads_zeroed, 1)
                for n_half, (k0, n) in enumerate(HALVES):
                    def up(i, s, norm=False):
                        u, f = i + (u0 + s), i + (f0 + s)
                        if norm:
                            norm_rstd(S_FFN[l])
                            dve.wait_ge(rstd_made, S_FFN[l] + 1)
                            dve.wait_ge(pads_zeroed, l + 1)
                        c = i + (k0 + s)
                        dve.wait_ge(unit_done, u + 1)
                        dve.tensor_tensor(gpad[:, s, 2:S + 2], ps[:, 2 * s, :], rstd[:, :], ALU.mult)\
                            .then_inc(g_made, 1)
                        dve.wait_ge(tap2, f + 1)
                        dve.scalar_tensor_tensor(out=cv[:, s, :], in0=gpad[:, s, 1:S + 1],
                                                 scalar=convT[:, l, bass.ds(c + FT, 1)], in1=cv[:, s, :],
                                                 op0=ALU.mult, op1=ALU.add).then_inc(tap1, 1)
                        dve.wait_ge(tap1, f + 1)
                        dve.scalar_tensor_tensor(out=cv[:, s, :], in0=gpad[:, s, 0:S],
                                                 scalar=convT[:, l, bass.ds(c, 1)], in1=cv[:, s, :],
                                                 op0=ALU.mult, op1=ALU.add).then_inc(tap0, 1)
                        weights_lo(u + 2, s)
                        dve.wait_ge(silu_scaled, f + 1)
                        dve.tensor_tensor(hid[:, s, :], ps[:, 2 * s + 1, :], act_o[:, s, :], ALU.mult)\
                            .then_inc(evacuated, 1)

                    first = 0
                    if n_half == 0:
                        up(0, 0, norm=True)
                        up(0, 1)
                        first = 2
                    with by_two(dve, first, n) as i:
                        up(i, 0)
                        up(i, 1)
                    u0, f0 = u0 + n, f0 + n

                    def down(j, s):
                        u = j + (u0 + s)
                        add_x(j + s, 4 + s, u + 1)
                        last = n_half == 1 and j + s == KT - 1
                        prepare = not (isinstance(u, int) and u + 2 >= U_END)
                        if prepare and not last:
                            weights_lo(u + 2, s)
                        if n_half == 1 and l == 0:
                            split_x(S_FFN[l] + 1, j + s)
                        if prepare and last:
                            weights_lo(u + 2, s)

                    if n_half == 0:
                        with by_two(dve, 0, KT) as j:
                            down(j, 0)
                            down(j, 1)
                    else:
                        for j in range(0, KT, 2):
                            down(j, 0)
                            down(j, 1)
                    u0 += KT

            pick(0)
            head(0, first=True)
            with dve.Fori(1, HA - 1) as h:
                head(h)
            head(HA - 1, last=True)
            out_proj(U_OUTA, 1)
            ffn(0)

            for m in range(4):
                if m == 0:
                    norm_rstd(2)
                    dve.wait_ge(rcol_turned, 2)
                    dve.tensor_copy(rcol[:, :], ps[:, 4, 0:TB]).then_inc(rcol_made, 1)
                    dve.wait_ge(rcol_made, 2)
                dve.wait_ge(unit_done, U_V + m + 1)
                for b in range(TB):
                    dve.tensor_scalar(v_all[:, b, m * 2 * P:(m + 1) * 2 * P],
                                      ps[:, 2 * (m % 2) + b // 2, (b % 2) * 2 * P:(b % 2 + 1) * 2 * P],
                                      rcol[:, b:b + 1], None, ALU.mult).then_inc(evacuated, 1)
                weights_lo(U_V + m + 2, m % 2)

            def attn_q(h):
                dve.wait_ge(q_done, h + 1)
                dve.scalar_tensor_tensor(out=tqk[0], in0=ps[:, 0, :], scalar=HDB ** -0.5, in1=rstd[:, :],
                                         op0=ALU.mult, op1=ALU.mult).then_inc(evacuated, 1)

            def attn_k(h):
                dve.wait_ge(unit_done, h + (U_QK + 1))
                dve.tensor_tensor(tqk[1], ps[:, 1, :], rstd[:, :], ALU.mult).then_inc(evacuated, 1)

            def attn_qk_lo(h, n):
                dve.wait_ge(dqk_hi_made, 2 * h + n + 1)
                dve.tensor_tensor(qk_lo[n], tqk[n], f32(qk_hi[n]), ALU.subtract).then_inc(dqk_split, 1)

            def attn_max(h, k):
                w = (TB - k) * P
                for c in range(2):
                    dve.wait_ge(dscored, 8 * h + (2 * k + c + 1))
                    dve.tensor_reduce(nmax[:, k % 2, c:c + 1], ps[:, 2 + (k % 2) * 2 + c, 0:w],
                                      AX.X, ALU.max, negate=True).then_inc(maxed, 1)

            def attn_mix(h, k):
                n = 4 * h + (k + 1)
                r, w = k % 2, (TB - k) * P
                dve.wait_ge(exped, 8 * h + (2 * k + 2))
                dve.reciprocal(rsum[:, r, :], lsum[:, r, :]).then_inc(sum_inv, 1)
                dve.wait_ge(sum_inv, n)
                dve.tensor_tensor(rsum[:, r, :], rsum[:, r, :], coef[:, :], ALU.mult).then_inc(sum_coef, 1)
                dve.wait_ge(sum_coef, n)
                p0, p1 = (prob[:, r, c, 0:w] for c in range(2))
                dve.tensor_scalar(p0, p0, rsum[:, r, 0:1], None, ALU.mult).then_inc(p0_scaled, 1)
                dve.wait_ge(p0_scaled, n)
                dve.scalar_tensor_tensor(out=p0, in0=p1, scalar=rsum[:, r, 1:2], in1=p0,
                                         op0=ALU.mult, op1=ALU.add).then_inc(a_made, 1)

            def attn_pT_lo(h, k):
                i = TB - 1 - k
                dve.wait_ge(pT_hi_made, 4 * h + (k + 1))
                dve.tensor_tensor(pT_lo[:, 0:i + 1, i * P:(i + 1) * P],
                                  ps[:, 6, 0:(i + 1) * P].rearrange("p (j c) -> p j c", c=P),
                                  f32(pT_hi[:, 0:i + 1, i * P:(i + 1) * P]), ALU.subtract).then_inc(pT_split, 1)

            def attn_finish(h, last=False):
                dve.wait_ge(o_rstd, h + 1)
                if last:
                    dve.wait_ge(o_split, h)
                else:
                    dve.wait_ge(vh_split, h + 2)
                dve.scalar_tensor_tensor(out=ytmp[:, :], in0=ps[:, 7, :], scalar=gainT[:, G_SUB:G_SUB + 1],
                                         in1=sqacc[:, :], op0=ALU.mult, op1=ALU.mult).then_inc(o_made, 1)

            def attn(h, prev=True, nxt=True):
                attn_max(h, 0)
                attn_max(h, 1)
                attn_mix(h, 0)
                attn_mix(h, 1)
                attn_max(h, 2)
                attn_pT_lo(h, 0)
                attn_max(h, 3)
                if prev:
                    attn_finish(h - 1)
                attn_pT_lo(h, 1)
                attn_mix(h, 2)
                attn_mix(h, 3)
                if nxt:
                    attn_q(h + 1)
                attn_pT_lo(h, 2)
                if nxt:
                    attn_qk_lo(h + 1, 0)
                attn_pT_lo(h, 3)
                if nxt:
                    attn_k(h + 1)
                    attn_qk_lo(h + 1, 1)

            dve.wait_ge(lam_kept, 1)
            dve.wait_ge(sub_scaled, 1)
            attn_q(0)
            attn_qk_lo(0, 0)
            attn_k(0)
            attn_qk_lo(0, 1)
            attn(0, prev=False)
            with dve.Fori(1, HB - 1) as h:
                attn(h)
            attn(HB - 1, nxt=False)
            attn_finish(HB - 1, last=True)
            out_proj(U_OUTB, 3)
            ffn(1)

            dve.wait_ge(fin_std, 1)
            dve.reciprocal(rcol[:, :], rcol[:, :]).then_inc(fin_rstd, 1)
            dve.wait_ge(fin_rstd, 1)
            for n, b in enumerate(FIN_BLOCKS):
                dve.wait_ge(fin_turned[1], n + 1)
                dve.tensor_scalar(o_sb[:, b, 512:1024], ps[:, 2 * b + 1, :], rcol[:, b:b + 1], None, ALU.mult)\
                    .then_inc(fin_scaled_v, 1)

        @block.tensor
        def _(pe):
            def mm3(o, w, m, start, stop):
                pe.matmul(o, w[0], m[0], start=start, stop=False)
                pe.matmul(o, w[0], m[1], start=False, stop=False)
                return pe.matmul(o, w[1], m[0], start=False, stop=stop)

            def xs(kt):
                return xs_hi[:, kt, :], xs_lo[:, kt, :]

            def hid_of(kt):
                return h_hi[:, kt, :], h_lo[:, kt, :]

            def wcol(s, t, c, kt, a, b):
                return cols(w_hi[:, s, :], t, c)[:, kt, a:b], cols(w_lo[:, s, :], t, c)[:, kt, a:b]

            def two_tiles(u, s, banks, moving, evac, ready=None, kts=range(KT)):
                if kts[0] == 0:
                    pe.wait_ge(w_split, u + 1)
                    if evac is not None:
                        pe.wait_ge(evacuated, evac)
                for kt in kts:
                    if ready is not None:
                        pe.wait_ge(ready[0], ready[1] + kt + 1)
                    for t, b in enumerate(banks):
                        last = mm3(ps[:, b, :], wcol(s, KT, 2 * P, kt, t * P, (t + 1) * P), moving(kt),
                                   kt == 0, kt == KT - 1)
                if kts[-1] == KT - 1:
                    last.then_inc(unit_done, 1)

            def in_turn(n, late, ahead):
                return (0, range(0, late)), (1, range(0, ahead)), (0, range(late, n)), (1, range(ahead, n))

            def one_tile(u, s, bank, moving, evac, n, ready=None, kts=None):
                kts = kts or range(n)
                if kts[0] == 0:
                    pe.wait_ge(w_split, u + 1)
                    if evac is not None:
                        pe.wait_ge(evacuated, evac)
                for kt in kts:
                    if ready is not None:
                        pe.wait_ge(ready[0], ready[1] + kt + 1)
                    last = mm3(ps[:, bank, :], wcol(s, n, P, kt, 0, P), moving(kt), kt == 0, kt == n - 1)
                if kts[-1] == n - 1:
                    last.then_inc(unit_done, 1)

            def token_major(u, s, evac, ready=None, blocks=range(TB)):
                if blocks[0] == 0:
                    pe.wait_ge(w_split, u + 1)
                    if evac is not None:
                        pe.wait_ge(evacuated, evac)
                for b in blocks:
                    for kt in range(KT):
                        if ready is not None and b == 0:
                            pe.wait_ge(ready[0], ready[1] + kt + 1)
                        st = tuple(a[:, b * P:(b + 1) * P] for a in xs(kt))
                        last = mm3(ps[:, 2 * s + b // 2, (b % 2) * 256:(b % 2 + 1) * 256], st,
                                   wcol(s, KT, 2 * P, kt, 0, 2 * P), kt == 0, kt == KT - 1)
                if blocks[-1] == TB - 1:
                    last.then_inc(unit_done, 1)

            def norm_sum(s):
                pe.wait_ge(sq_added, 8 * (s + 1))
                pe.matmul(ps[:, 7, :], onesf[:, :], sqacc[:, :], start=True, stop=True).then_inc(norm_summed, 1)

            def turn_rstd(s):
                pe.wait_ge(rstd_made, s + 1)
                for b in range(TB):
                    last = pe.matmul(ps[:, 4, b:b + 1], rstd[0:1, b * P:(b + 1) * P], onesf[0:1, 0:1],
                                     start=True, stop=True)
                last.then_inc(rcol_turned, 1)

            pe.wait_ge(const_made, 10)
            for b in range(TB):
                if b == TB - 1:
                    pe.wait_ge(gains_loaded, 16 * 6)
                    pe.transpose(ps[:, 4, 0:57], gain_rows, ident[0:57, 0:57]).then_inc(gains_turned, 1)
                pe.wait_ge(x_loaded[b], 16)
                for j in range(KT if b == TB - 1 else KT - 1):
                    if j == KT - 1:
                        pe.wait_ge(gains_kept, 1)
                    for bb in (range(TB) if j == KT - 1 else (b,)):
                        last = pe.transpose(ps[:, X_BANK[j], bb * P:(bb + 1) * P],
                                            x_in[:, bb, j * P:(j + 1) * P], ident[:, :])
                    if b == TB - 1:
                        last.then_inc(x_turned, 1)
            pe.wait_ge(wg_split, 1)
            for half in (range(0, KT // 2), range(KT // 2, KT)):
                for kt in half:
                    pe.wait_ge(x_split, kt + 1)
                    last = mm3(ps[:, 5, :], (wg_hi[:, kt, :], wg_lo[:, kt, :]), xs(kt), kt == 0, kt == KT - 1)
                if half[0]:
                    last.then_inc(gate_mm, 1)
                    norm_sum(0)
                two_tiles(0, 0, (0, 1), xs, None, kts=half)

            def head(h, first=False):
                u = 4 * h
                if not first:
                    two_tiles(u, 0, (0, 1), xs, 8 * h - 1)
                else:
                    pe.wait_ge(rows_loaded, 16 * 8)
                    for l in range(2):
                        pe.transpose(ps[:, 4, 64 + 96 * l:64 + 96 * l + 4 * FT], conv_rows[:, l, :],
                                     ident[0:4 * FT, 0:4 * FT]).then_inc(rows_turned, 1)
                    pe.wait_ge(x_kept, KT)
                    token_major(u + 1, 1, None, blocks=range(0, TB - 1))
                    pe.wait_ge(rows_kept, 2)
                    pe.wait_ge(lam_dve, 4)
                    pe.matmul(ps[:, 4, 32:33], onesf[0:1, :], lam_w[0:1, 7:8], start=True, stop=True)\
                        .then_inc(lam_spread, 1)
                    turn_rstd(0)
                    pe.wait_ge(gate_scan, 2)
                    for b in range(TB):
                        last = pe.transpose(ps[:, 5, HA * b:HA * (b + 1)], g_a[0:HA, b * P:(b + 1) * P],
                                            ident[0:HA, 0:HA])
                    last.then_inc(a_turned, 1)
                pe.wait_ge(m_picked, 2 * h + 2)
                if not first:
                    pe.wait_ge(den_sq, h)
                    pe.wait_ge(var_made, h)
                if first:
                    pe.wait_ge(ones_r_made, 1)
                for n, bank in enumerate((7, 6)):
                    r = slice(n * S, (n + 1) * S)
                    pe.matmul(ps[:, bank, :], ones_r[0:HA, :], p_hi[0:HA, r], start=True, stop=False)
                    pe.matmul(ps[:, bank, :], ones_r[0:HA, :], p_lo[0:HA, r], start=False, stop=True)\
                        .then_inc(m_spread, 1)
                if first:
                    token_major(u + 1, 1, None, blocks=(TB - 1,))
                else:
                    token_major(u + 1, 1, 8 * h, blocks=range(0, TB // 2))
                pe.wait_ge(qk_split, 2 * h + 2)
                pe.wait_ge(floor_kept, h + 1)
                if first:
                    pe.wait_ge(rcol_made, 1)
                    pe.wait_ge(acol_made, 1)
                else:
                    pe.wait_ge(y_made, 2 * h)
                for j in range(TB):
                    o = ps[:, 4 + j, 0:S - j * P] if j < 3 else ps[:, 6, 2 * P:3 * P]
                    mm3(o, (k_hi[:, j * P:(j + 1) * P], k_lo[:, j * P:(j + 1) * P]),
                        (q_hi[:, j * P:S], q_lo[:, j * P:S]), True, True).then_inc(scored, 1)
                if not first:
                    token_major(u + 1, 1, None, blocks=range(TB // 2, TB))
                one_tile(u + 2, 0, 0, xs, 8 * h + 2, KT)
                pe.wait_ge(evacuated, 8 * h + 6)
                pe.wait_ge(p_split, h + 1)
                for v in range(2):
                    for j in range(TB):
                        pj = tuple(a[:, OFF[j]:OFF[j] + S - j * P] for a in (p_hi, p_lo))
                        last = mm3(ps[:, 4 + v, j * P:S],
                                   (v_hi[:, j, v * P:(v + 1) * P], v_lo[:, j, v * P:(v + 1) * P]), pj,
                                   j == 0, j == TB - 1)
                    last.then_inc(pv_done, 1)
                for j in range(TB):
                    for n, a in enumerate((p_hi, p_lo)):
                        last = pe.matmul(ps[:, 6, j * P:S], ones_r[:, :], a[:, OFF[j]:OFF[j] + S - j * P],
                                         start=(j == 0 and n == 0), stop=(j == TB - 1 and n == 1))
                last.then_inc(pv_done, 1)
                one_tile(u + 3, 1, 2, xs, 8 * h + 6, KT)
                pe.wait_ge(num_added, h + 1)
                pe.wait_ge(arg_made, 4 * h + 4)
                pe.matmul(ps[:, 7, :], onesf[:, :], num0, start=True, stop=True).then_inc(head_summed, 1)

            def out_proj(u0, e0, ready, first=0):
                for m in range(first, KT // 2):
                    s = m % 2
                    evac = e0 if m < 2 else e0 + 2 * (m - 1)
                    two_tiles(u0 + m, s, (2 * s, 2 * s + 1), hid_of, evac, (ready, 0) if m == 0 else None)

            def ffn(l, e_in):
                u0, e0, f0 = U_FFN[l], E_FFN[l], l * FT
                for n_half, (k0, n) in enumerate(HALVES):
                    for s, kts in in_turn(KT, KT - 2, 1):
                        two_tiles(u0 + s, s, (2 * s, 2 * s + 1), xs, e_in[s] if n_half == 0 else None,
                                  (x_split, 8 * S_FFN[l]) if n_half == 0 else None, kts=kts)
                        if n_half == 0 and s == 0 and kts[-1] == KT - 1:
                            norm_sum(S_FFN[l])
                    with by_two(pe, 2, n) as i:
                        for s in range(2):
                            two_tiles(i + (u0 + s), s, (2 * s, 2 * s + 1), xs, i + (e0 + s - 1))
                    u0, e0 = u0 + n, e0 + n
                    for s, kts in in_turn(n, n - 1, 3 if n < HT else 2):
                        one_tile(u0 + s, s, 4 + s, hid_of, None, n, (hid_split, f0 + k0), kts=kts)
                    with by_two(pe, 2, KT) as j:
                        for s in range(2):
                            one_tile(j + (u0 + s), s, 4 + s, hid_of, j + (e0 + s - 1), n)
                    u0, e0 = u0 + KT, e0 + KT

            head(0, first=True)
            with pe.Fori(1, HA) as h:
                head(h)
            for m, kts in in_turn(KT, KT - 2, 2):
                two_tiles(U_OUTA + m, m, (2 * m, 2 * m + 1), hid_of, E_OUTA, (y_split, 0), kts=kts)
            out_proj(U_OUTA, E_OUTA, None, first=2)
            ffn(0, (E_OUTA + 6, E_OUTA + 8))

            for m in range(4):
                evac = None if m < 2 else E_V + 4 * (m - 1)
                if m != 1:
                    token_major(U_V + m, m % 2, evac, (x_split, 16) if m == 0 else None)
                    if m == 0:
                        norm_sum(2)
                else:
                    token_major(U_V + m, m % 2, evac, blocks=range(0, TB // 2))
                    turn_rstd(2)
                    token_major(U_V + m, m % 2, evac, blocks=range(TB // 2, TB))

            def attn_project(h, s, part):
                first = isinstance(h, int) and h == 0
                if part == 0:
                    pe.wait_ge(w_split, h + (U_QK + 1))
                if part % 4 == 0:
                    pe.wait_ge(evacuated, E_QK - TB if first else 2 * h + (E_QK - 1 + part // 4))
                t, n = part // 4, KT // 4
                for kt in range(part % 4 * n, (part % 4 + 1) * n):
                    last = mm3(ps[:, t, :], wcol(s, KT, 2 * P, kt, t * P, (t + 1) * P), xs(kt),
                               kt == 0, kt == KT - 1)
                if part % 4 == 3:
                    last.then_inc(unit_done if t else q_done, 1)

            def attn_scores(h, k, first):
                i = TB - 1 - k
                if not (first and k < 2):
                    pe.wait_ge(exped, 8 * h + (2 * k - 2))
                for step in range(4):
                    for c in range(2):
                        b = 2 + (k % 2) * 2 + c
                        o = ps[:, b, 0:(i + 1) * P]
                        r = slice(c * HDB, (c + 1) * HDB)
                        qi = tuple(a[r, i * P:(i + 1) * P] for a in (q_hi, q_lo))
                        ks = tuple(a[r, 0:(i + 1) * P] for a in (k_hi, k_lo))
                        if step == 0:
                            pe.matmul(o, qi[0], ks[0], start=True, stop=False)
                        elif step == 1:
                            pe.matmul(ps[:, b, i * P:(i + 1) * P], ident_b[:, :], mask_b[:, :],
                                      start=False, stop=False)
                        elif step == 2:
                            pe.matmul(o, qi[0], ks[1], start=False, stop=False)
                        else:
                            pe.matmul(o, qi[1], ks[0], start=False, stop=True).then_inc(dscored, 1)

            def attn_turn(h, k, first):
                pe.wait_ge(a_made, 4 * h + (k + 1))
                if not (first and k == 0):
                    pe.wait_ge(pT_split, 4 * h + k)
                for j in range(TB - k):
                    last = pe.transpose(ps[:, 6, j * P:(j + 1) * P], prob[:, k % 2, 0, j * P:(j + 1) * P],
                                        ident[:, :])
                last.then_inc(pT_turned, 1)

            def attn_sum(h):
                pe.wait_ge(o_sq, h + 1)
                pe.wait_ge(pT_split, 4 * h + 4)
                pe.matmul(ps[:, 6, :], onesf[:, :], sq[:, 0, :], start=True, stop=True).then_inc(o_summed, 1)

            def out_first(m, kts):
                two_tiles(U_OUTB + m, m, (2 * m, 2 * m + 1), hid_of, E_OUTB, (o_split, 0), kts=kts)

            def attn(h, s, prev=True, nxt=True, nxt2=True):
                def fill(*parts):
                    for part in (part + EARLY for part in parts if part + EARLY < 8):
                        if nxt:
                            attn_project(h + 1, s, part)
                        elif part < HB - 1:
                            out_first(0, (part,))

                first = not prev
                pe.wait_ge(dqk_split, 2 * h + 2)
                attn_scores(h, 0, first)
                attn_scores(h, 1, first)
                if prev:
                    attn_sum(h - 1)
                fill(0)
                attn_scores(h, 2, first)
                fill(1)
                if prev:
                    pe.wait_ge(o_ln, h)
                attn_turn(h, 0, first)
                attn_scores(h, 3, first)
                fill(2)
                attn_turn(h, 1, first)
                fill(3, 4)
                attn_turn(h, 2, first)
                fill(5)
                attn_turn(h, 3, first)
                fill(6, 7)
                pe.wait_ge(pT_split, 4 * h + 4)
                pe.wait_ge(vh_split, h + 1)
                if prev:
                    pe.wait_ge(o_made, h)
                for j in range(TB):
                    last = mm3(ps[:, 7, j * P:S], (vh_hi[:, j, :], vh_lo[:, j, :]),
                               (pT_hi[:, j, j * P:S], pT_lo[:, j, j * P:S]), j == 0, j == TB - 1)
                last.then_inc(dpv_done, 1)
                if nxt:
                    for part in range(EARLY):
                        if nxt2:
                            attn_project(h + 2, 1 - s, part)
                        else:
                            out_first(0, (part,))

            EARLY = 1
            for part in range(8):
                attn_project(0, 0, part)
            for part in range(EARLY):
                attn_project(1, 1, part)
            attn(0, 1, prev=False)
            with by_two(pe, 1, HB - 3) as h:
                attn(h, 0)
                attn(h + 1, 1)
            attn(HB - 3, 0)
            attn(HB - 2, 1, nxt2=False)
            attn(HB - 1, 0, nxt=False)
            out_first(1, (0,))
            attn_sum(HB - 1)
            out_first(1, range(1, HB - 3))
            out_first(0, (HB - 1,))
            out_first(1, range(HB - 3, HB))
            out_proj(U_OUTB, E_OUTB, None, first=2)
            ffn(1, (E_OUTB + 6, E_OUTB + 8))

            def turn_back(b, a, tiles):
                for t in tiles:
                    last = pe.transpose(ps[:, 2 * b + a, t * P:(t + 1) * P],
                                        xg_fin[:, 4 * a + t, b * P:(b + 1) * P], ident[:, :])
                if tiles[-1] == 3:
                    last.then_inc(fin_turned[a], 1)

            pe.wait_ge(xs_hi_made, 8 * 4 + 7)
            pe.wait_ge(evacuated, E_FFN1 + n_ffn - 1)
            for b in range(TB):
                turn_back(b, 0, range(4))
            for b in (0, 1, 3):
                turn_back(b, 1, range(3))
            pe.wait_ge(evacuated, E_FFN1 + n_ffn)
            pe.wait_ge(sq_added, 8 * 5 - 1)
            pe.wait_ge(sq_made, 8 * 5)
            for b in range(TB):
                pe.matmul(ps[:, 5, b:b + 1], sqacc[:, b * P:(b + 1) * P], onesf[:, 0:1], start=True, stop=False)
                last = pe.matmul(ps[:, 5, b:b + 1], sq[:, 1, b * P:(b + 1) * P], onesf[:, 0:1],
                                 start=False, stop=True)
            last.then_inc(fin_summed, 1)
            pe.wait_ge(xs_hi_made, 8 * 5)
            for b in (0, 1, 3):
                turn_back(b, 1, (3,))
            pe.wait_ge(fin_std, 1)
            turn_back(2, 1, range(4))


_INS = ['x', 'attn_norm_g', 'ffn_norm_g', 'mlstm_w_in', 'mlstm_b_gate', 'mlstm_head_g', 'mlstm_w_out',
        'kv_norm_g', 'w_kv', 'diff_w_q', 'diff_lambda_q1', 'diff_lambda_k1', 'diff_lambda_q2',
        'diff_lambda_k2', 'diff_subln_g', 'diff_w_out', 'ffn_w_up', 'ffn_conv_w', 'ffn_conv_b',
        'ffn_w_down', 'final_norm_g']
_OUTS = [((1, 512, 1024), 'float32')]


def kernel(**inputs):
    import numpy as _np
    import concourse.bacc as _bacc
    from concourse import mybir as _mybir
    from concourse.bass_utils import run_bass_kernel_spmd as _run

    nc = _bacc.Bacc("TRN2", target_bir_lowering=False, num_devices=1)
    arrays, args = {}, []
    for name in _INS:
        a = _np.ascontiguousarray(inputs[name])
        arrays[f"in_{name}_dram"] = a
        args.append(nc.dram_tensor(f"in_{name}_dram", a.shape, _mybir.dt.from_np(a.dtype), kind="ExternalInput").ap())
    for i, (shape, dtype) in enumerate(_OUTS):
        dt = _mybir.dt.from_np(_np.dtype(dtype))
        args.append(nc.dram_tensor(f"out_{i}_dram", shape, dt, kind="ExternalOutput").ap())
    build_trunk(nc, *args)
    r = _run(nc, [arrays], core_ids=[0])
    got = tuple(r.results[0][f"out_{i}_dram"] for i in range(len(_OUTS)))
    return got[0]
```
